# Optimizing a Trainium2 kernel written in Bass

```python
import jax, jax.numpy as jnp
from jax import lax
import numpy as np
import jax
import jax.numpy as jnp

D_MODEL = 1024
BATCH = 1
SEQ = 512
DEPTH = 1

CHUNK = 64
Q_BLOCK = 128
ROPE_THETA = 10000.0
EPS = 1e-6
GN_EPS = 1e-5
NEG_BIG = -1e30
A_HEADS = 8
A_HEAD_DIM = 64
IDX_HEADS = 8
IDX_DIM = 64
TOPK_MAX = 256
A_WIDTH = A_HEADS * A_HEAD_DIM
R_HEADS = 4
R_QK_DIM = 128
R_V_DIM = 256
R_WIDTH = R_HEADS * R_V_DIM
D_FF = 2816
PLE_DIM = 256
IN_SPLITS = (
    A_HEADS * A_HEAD_DIM,
    A_HEAD_DIM,
    A_HEAD_DIM,
    IDX_HEADS * IDX_DIM,
    IDX_DIM,
    IDX_HEADS,
    R_HEADS * R_QK_DIM,
    R_HEADS * R_QK_DIM,
    R_HEADS * R_V_DIM,
    R_HEADS * R_V_DIM,
    D_MODEL,
    D_MODEL,
)
IN_WIDTH = sum(IN_SPLITS)


def rms_norm(x, g):
    xf = x.astype(jnp.float32)
    y = xf * lax.rsqrt(jnp.mean(xf * xf, axis=-1, keepdims=True) + EPS)
    return (y * g.astype(jnp.float32)).astype(x.dtype)

def swiglu(x, w_gate, w_up, w_down):
    return (jax.nn.silu(x @ w_gate) * (x @ w_up)) @ w_down

def rope(t, pos):
    half = t.shape[-1] // 2
    inv = ROPE_THETA ** (-jnp.arange(half, dtype=jnp.float32) / half)
    ang = pos.astype(jnp.float32)[..., None] * inv
    cos = jnp.cos(ang)[:, :, None, :]
    sin = jnp.sin(ang)[:, :, None, :]
    t1 = t[..., :half].astype(jnp.float32)
    t2 = t[..., half:].astype(jnp.float32)
    return jnp.concatenate([t1 * cos - t2 * sin, t2 * cos + t1 * sin], axis=-1).astype(t.dtype)

def dsa_attention(q, k, v, q_idx, k_idx, w_idx, n_sel):
    b, s = q.shape[0], q.shape[1]
    nb = s // Q_BLOCK
    key_pos = jnp.arange(s)
    k_idx32 = k_idx.astype(jnp.float32)

    def to_blocks(t):
        return jnp.moveaxis(t.reshape((b, nb, Q_BLOCK) + t.shape[2:]), 1, 0)

    def one_block(args):
        qb, qib, wb, blk = args
        qpos = blk * Q_BLOCK + jnp.arange(Q_BLOCK)
        visible_end = (qpos // CHUNK + 1) * CHUNK
        admissible = key_pos[None, :] < visible_end[:, None]
        rel = jax.nn.relu(jnp.einsum('bqhd,bsd->bqhs', qib.astype(jnp.float32), k_idx32))
        score = jnp.einsum('bqhs,bqh->bqs', rel, wb.astype(jnp.float32))
        score = jnp.where(admissible[None], score, NEG_BIG)
        top_val, top_pos = lax.top_k(score, n_sel)
        valid = top_val > 0.5 * NEG_BIG
        k_sel = jax.vmap(lambda kb, ib: kb[ib])(k, top_pos)
        v_sel = jax.vmap(lambda vb, ib: vb[ib])(v, top_pos)
        logits = jnp.einsum('bqhd,bqkd->bqhk', qb, k_sel).astype(jnp.float32) * (A_HEAD_DIM ** -0.5)
        logits = jnp.where(valid[:, :, None, :], logits, NEG_BIG)
        probs = jax.nn.softmax(logits, axis=-1).astype(v.dtype)
        return jnp.einsum('bqhk,bqkd->bqhd', probs, v_sel)

    out = lax.map(one_block, (to_blocks(q), to_blocks(q_idx), to_blocks(w_idx), jnp.arange(nb)))
    return jnp.moveaxis(out, 0, 1).reshape(b, s, -1)

def retention(q, k, v):
    b, s, h, dk = q.shape
    dv = v.shape[-1]
    n = s // CHUNK
    log_gamma = jnp.log1p(-jnp.exp2(-5.0 - jnp.arange(h, dtype=jnp.float32)))
    idx = jnp.arange(CHUNK, dtype=jnp.float32)
    decay_intra = jnp.exp(log_gamma[:, None, None] * jnp.abs(idx[:, None] - idx[None, :]))
    decay_q = jnp.exp(log_gamma[None, :] * (idx[:, None] + 1.0))
    decay_k = jnp.exp(log_gamma[None, :] * (CHUNK - 1.0 - idx[:, None]))
    decay_chunk = jnp.exp(log_gamma * CHUNK)
    qc = q.reshape(b, n, CHUNK, h, dk)
    kc = (k * (dk ** -0.5)).reshape(b, n, CHUNK, h, dk)
    vc = v.reshape(b, n, CHUNK, h, dv)
    scores = jnp.einsum('bnihd,bnjhd->bnhij', qc, kc) * decay_intra
    y_intra = jnp.einsum('bnhij,bnjhe->bnihe', scores, vc)
    kv = jnp.einsum('bnjhd,bnjhe,jh->nbhde', kc, vc, decay_k)

    def step(state, kv_n):
        return decay_chunk[None, :, None, None] * state + kv_n, state

    _, prev = lax.scan(step, jnp.zeros((b, h, dk, dv), jnp.float32), kv)
    y_cross = jnp.einsum('bnihd,nbhde->bnihe', qc, prev) * decay_q[None, None, :, :, None]
    return (y_intra + y_cross).reshape(b, s, h, dv)

def group_norm_heads(y, g):
    mean = jnp.mean(y, axis=-1, keepdims=True)
    var = jnp.mean(jnp.square(y - mean), axis=-1, keepdims=True)
    yn = (y - mean) * lax.rsqrt(var + GN_EPS)
    return yn.reshape(y.shape[0], y.shape[1], -1) * g.astype(jnp.float32)

def first_inputs(seed: int = 0) -> dict:
    key = jax.random.key(seed)
    ks = jax.random.split(key, 24)
    f32 = jnp.float32

    def w(k, shape, fan_in, scale=1.0):
        return jax.random.normal(k, shape, f32) * (scale * fan_in ** -0.5)

    def gain(k, shape):
        return 1.0 + 0.05 * jax.random.normal(k, shape, f32)

    offsets = jax.random.randint(ks[2], (BATCH, 1), 0, 4096)
    positions = (offsets + jnp.arange(SEQ)[None, :]).astype(jnp.int32)
    return {
        'x': jax.random.normal(ks[0], (BATCH, SEQ, D_MODEL), f32),
        'p': jax.random.normal(ks[1], (DEPTH, BATCH, SEQ, PLE_DIM), f32),
        'positions': positions,
        'ffn1_norm': gain(ks[3], (DEPTH, D_MODEL)),
        'ffn1_w_gate': w(ks[4], (DEPTH, D_MODEL, D_FF), D_MODEL),
        'ffn1_w_up': w(ks[5], (DEPTH, D_MODEL, D_FF), D_MODEL),
        'ffn1_w_down': w(ks[6], (DEPTH, D_FF, D_MODEL), D_FF, 0.5),
        'mix_norm': gain(ks[7], (DEPTH, D_MODEL)),
        'w_in': w(ks[8], (DEPTH, D_MODEL, IN_WIDTH), D_MODEL),
        'ret_gn': gain(ks[9], (DEPTH, R_WIDTH)),
        'w_branch_a': w(ks[10], (DEPTH, A_WIDTH, D_MODEL), A_WIDTH),
        'w_branch_b': w(ks[11], (DEPTH, R_WIDTH, D_MODEL), R_WIDTH),
        'w_out': w(ks[12], (DEPTH, D_MODEL, D_MODEL), D_MODEL, 0.5),
        'ffn2_norm': gain(ks[13], (DEPTH, D_MODEL)),
        'ffn2_w_gate': w(ks[14], (DEPTH, D_MODEL, D_FF), D_MODEL),
        'ffn2_w_up': w(ks[15], (DEPTH, D_MODEL, D_FF), D_MODEL),
        'ffn2_w_down': w(ks[16], (DEPTH, D_FF, D_MODEL), D_FF, 0.5),
        'ple_norm': gain(ks[17], (DEPTH, D_MODEL)),
        'w_ple_gate': w(ks[18], (DEPTH, D_MODEL, D_MODEL), D_MODEL),
        'w_ple_proj': w(ks[19], (DEPTH, PLE_DIM, D_MODEL), PLE_DIM, 0.5),
        'final_norm': gain(ks[20], (D_MODEL,)),
    }

def first_block(x, p, positions, ffn1_norm, ffn1_w_gate, ffn1_w_up, ffn1_w_down,
              mix_norm, w_in, ret_gn, w_branch_a, w_branch_b, w_out,
              ffn2_norm, ffn2_w_gate, ffn2_w_up, ffn2_w_down,
              ple_norm, w_ple_gate, w_ple_proj, final_norm):
    b, s, _ = x.shape
    n_sel = min(TOPK_MAX, s // 4)
    split_points = []
    acc = 0
    for sz in IN_SPLITS[:-1]:
        acc += sz
        split_points.append(acc)

    h = x
    for i in range(DEPTH):
        h = h + 0.5 * swiglu(rms_norm(h, ffn1_norm[i]), ffn1_w_gate[i], ffn1_w_up[i], ffn1_w_down[i])

        u = rms_norm(h, mix_norm[i])
        z = u @ w_in[i]
        (aq, ak, av, iq, ik, iw, rq, rk, rv, rg, ga, gb) = jnp.split(z, split_points, axis=-1)

        aq = rope(aq.reshape(b, s, A_HEADS, A_HEAD_DIM), positions)
        ak = rope(ak[:, :, None, :], positions)[:, :, 0, :]
        iq = rope(iq.reshape(b, s, IDX_HEADS, IDX_DIM), positions) * (IDX_DIM ** -0.5)
        ik = rope(ik[:, :, None, :], positions)[:, :, 0, :]
        iw = iw * (IDX_HEADS ** -0.5)
        y_a = dsa_attention(aq, ak, av, iq, ik, iw, n_sel)

        rq = rope(rq.reshape(b, s, R_HEADS, R_QK_DIM), positions).astype(jnp.float32)
        rk = rope(rk.reshape(b, s, R_HEADS, R_QK_DIM), positions).astype(jnp.float32)
        rv = rv.reshape(b, s, R_HEADS, R_V_DIM).astype(jnp.float32)
        y_r = group_norm_heads(retention(rq, rk, rv), ret_gn[i]).astype(x.dtype) * jax.nn.silu(rg)

        merged = jax.nn.sigmoid(ga) * (y_a @ w_branch_a[i]) + jax.nn.sigmoid(gb) * (y_r @ w_branch_b[i])
        h = h + merged @ w_out[i]

        h = h + 0.5 * swiglu(rms_norm(h, ffn2_norm[i]), ffn2_w_gate[i], ffn2_w_up[i], ffn2_w_down[i])

        gate = jax.nn.sigmoid(rms_norm(h, ple_norm[i]) @ w_ple_gate[i])
        h = h + gate * (p[i] @ w_ple_proj[i])

    return rms_norm(h, final_norm)


N_MIXERS = 4
NORM_EPS = 1e-6
GLA_HEADS = 4
GLA_DK = D_MODEL // 2
GLA_DV = D_MODEL
GLA_RANK = 16
GLA_TAU = 16.0
GLA_CHUNK = 64
GLA_IN = 2 * GLA_DK + 2 * GLA_DV + GLA_RANK
RWKV_HEAD = 64
RWKV_HEADS = D_MODEL // RWKV_HEAD
RWKV_DECAY_RANK = 64
RWKV_A_RANK = 64
RWKV_GATE_RANK = 128
RWKV_GN_EPS = 64e-5
RWKV_SHIFT_MIXES = 6
SB_HEADS = 16
SB_HEAD_DIM = D_MODEL // SB_HEADS
SB_BLOCK = 128
ML_HEADS = 4
ML_DK = D_MODEL // 2
ML_DV = D_MODEL
ML_CHUNK = 64
ML_IN = 2 * ML_DK + 2 * ML_DV + 2 * ML_HEADS
FFN_DIM = 2816
CONV_WIDTH = 3


def rms_norm_2(x, g, eps=NORM_EPS):
    xf = x.astype(jnp.float32)
    y = xf * lax.rsqrt(jnp.mean(xf * xf, axis=-1, keepdims=True) + eps)
    return (y * g.astype(jnp.float32)).astype(x.dtype)

def _to_chunks(t, chunk):
    b, s, h, d = t.shape
    return t.reshape(b, s // chunk, chunk, h, d).transpose(1, 0, 3, 2, 4)

def _from_chunks(t):
    n, b, h, c, d = t.shape
    return t.transpose(1, 0, 3, 2, 4).reshape(b, n * c, h, d)

def _gates_to_chunks(t, chunk):
    b, s, h = t.shape
    return t.reshape(b, s // chunk, chunk, h).transpose(1, 0, 3, 2)

def gla_mixer(x, w_in, w_alpha_up, b_alpha, out_norm, w_out):
    f32 = jnp.float32
    b, s, _ = x.shape
    h, dk, dv, c = GLA_HEADS, GLA_DK // GLA_HEADS, GLA_DV // GLA_HEADS, GLA_CHUNK
    proj = x @ w_in
    q, k, v, r, a_low = jnp.split(
        proj, [GLA_DK, 2 * GLA_DK, 2 * GLA_DK + GLA_DV, 2 * GLA_DK + 2 * GLA_DV], axis=-1)
    log_alpha = jax.nn.log_sigmoid((a_low @ w_alpha_up + b_alpha).astype(f32)) / GLA_TAU
    q = q.astype(f32).reshape(b, s, h, dk) * dk ** -0.5
    k = k.astype(f32).reshape(b, s, h, dk)
    v = v.astype(f32).reshape(b, s, h, dv)
    qc, kc, vc = _to_chunks(q, c), _to_chunks(k, c), _to_chunks(v, c)
    cum = jnp.cumsum(_to_chunks(log_alpha.reshape(b, s, h, dk), c), axis=3)
    causal = jnp.tril(jnp.ones((c, c), dtype=bool))

    def step(state, inp):
        qi, ki, vi, bi = inp
        q_dec = qi * jnp.exp(bi)
        k_inv = ki * jnp.exp(-bi)
        scores = jnp.where(causal, jnp.einsum('bhtd,bhsd->bhts', q_dec, k_inv), 0.0)
        o = (jnp.einsum('bhts,bhsv->bhtv', scores, vi)
             + jnp.einsum('bhtd,bhdv->bhtv', q_dec, state))
        b_last = bi[:, :, -1:, :]
        k_end = ki * jnp.exp(b_last - bi)
        state = (state * jnp.exp(b_last)[:, :, 0, :, None]
                 + jnp.einsum('bhsd,bhsv->bhdv', k_end, vi))
        return state, o

    state0 = jnp.zeros((b, h, dk, dv), f32)
    _, o = lax.scan(step, state0, (qc, kc, vc, cum))
    o = _from_chunks(o)
    o = rms_norm_2(o, out_norm.reshape(h, dv)).reshape(b, s, GLA_DV)
    return (o.astype(x.dtype) * jax.nn.silu(r)) @ w_out

def rwkv7_mixer(x, mu, w_rkv, w0, w1, w2, a0, a1, a2, g1, g2, k_k, k_a, r_k, gn_g, gn_b, w_out):
    f32 = jnp.float32
    b, s, d = x.shape
    h, n = RWKV_HEADS, RWKV_HEAD
    x_prev = jnp.pad(x, ((0, 0), (1, 0), (0, 0)))[:, :-1]
    xx = x_prev - x
    xr, xw, xk, xv, xa, xg = (x + xx * mu[j] for j in range(RWKV_SHIFT_MIXES))
    r = xr @ w_rkv[0]
    k = xk @ w_rkv[1]
    v = xv @ w_rkv[2]
    w_log = -jax.nn.softplus(-(w0 + jnp.tanh(xw @ w1) @ w2).astype(f32)) - 0.5
    decay = jnp.exp(-jnp.exp(w_log))
    a = jax.nn.sigmoid((a0 + (xa @ a1) @ a2).astype(f32))
    g = jax.nn.sigmoid(xg @ g1) @ g2
    kk = (k * k_k).astype(f32).reshape(b, s, h, n)
    kk = kk / jnp.maximum(jnp.sqrt(jnp.sum(kk * kk, axis=-1, keepdims=True)), 1e-12)
    k = k.astype(f32) * (1.0 + (a - 1.0) * k_a.astype(f32))
    r = r.astype(f32).reshape(b, s, h, n)
    k = k.reshape(b, s, h, n)
    v = v.astype(f32).reshape(b, s, h, n)
    a = a.reshape(b, s, h, n)
    decay = decay.reshape(b, s, h, n)

    def step(state, inp):
        r_t, w_t, k_t, v_t, kk_t, a_t = inp
        sa = jnp.einsum('bhvk,bhk->bhv', state, -kk_t)
        state = (state * w_t[:, :, None, :]
                 + sa[..., None] * (kk_t * a_t)[:, :, None, :]
                 + v_t[..., None] * k_t[:, :, None, :])
        return state, jnp.einsum('bhvk,bhk->bhv', state, r_t)

    tm = lambda t: jnp.moveaxis(t, 1, 0)
    state0 = jnp.zeros((b, h, n, n), f32)
    _, y = lax.scan(step, state0, (tm(r), tm(decay), tm(k), tm(v), tm(kk), tm(a)))
    y = jnp.moveaxis(y, 0, 1)
    mean = jnp.mean(y, axis=-1, keepdims=True)
    var = jnp.mean(jnp.square(y - mean), axis=-1, keepdims=True)
    yn = ((y - mean) * lax.rsqrt(var + RWKV_GN_EPS)).reshape(b, s, d) * gn_g.astype(f32) + gn_b.astype(f32)
    bonus = jnp.sum(r * k * r_k.astype(f32).reshape(h, n), axis=-1, keepdims=True) * v
    out = (yn + bonus.reshape(b, s, d)).astype(x.dtype) * g
    return out @ w_out

def stick_breaking_mixer(x, w_qkv, w_out):
    f32 = jnp.float32
    b, s, d = x.shape
    h, dh, qb_len = SB_HEADS, SB_HEAD_DIM, SB_BLOCK
    q, k, v = jnp.split(x @ w_qkv, 3, axis=-1)
    q = q.reshape(b, s, h, dh) * dh ** -0.5
    k = k.reshape(b, s, h, dh)
    v = v.reshape(b, s, h, dh)
    n_blocks = s // qb_len
    q_blocks = q.reshape(b, n_blocks, qb_len, h, dh).transpose(1, 0, 3, 2, 4)
    starts = jnp.arange(n_blocks, dtype=jnp.int32) * qb_len
    key_pos = jnp.arange(s, dtype=jnp.int32)

    def block(args):
        q_blk, start = args
        z = jnp.einsum('bhqd,bkhd->bhqk', q_blk, k).astype(f32)
        q_pos = start + jnp.arange(qb_len, dtype=jnp.int32)
        before = key_pos[None, :] < q_pos[:, None]
        log_keep = jnp.where(before, jax.nn.log_sigmoid(-z), 0.0)
        suffix = lax.cumsum(log_keep, axis=3, reverse=True)
        log_w = jax.nn.log_sigmoid(z) + suffix - log_keep
        w = jnp.where(before, jnp.exp(log_w), 0.0)
        return jnp.einsum('bhqk,bkhd->bhqd', w.astype(v.dtype), v)

    o = lax.map(block, (q_blocks, starts))
    o = o.transpose(1, 0, 3, 2, 4).reshape(b, s, d)
    return o @ w_out

def mlstm_mixer(x, w_in, b_if, out_norm, w_out):
    f32 = jnp.float32
    b, s, _ = x.shape
    h, dk, dv, c = ML_HEADS, ML_DK // ML_HEADS, ML_DV // ML_HEADS, ML_CHUNK
    proj = x @ w_in
    q, k, v, o_pre, if_pre = jnp.split(
        proj, [ML_DK, 2 * ML_DK, 2 * ML_DK + ML_DV, 2 * ML_DK + 2 * ML_DV], axis=-1)
    if_pre = (if_pre + b_if).astype(f32)
    i_pre = if_pre[..., :h]
    log_f = jax.nn.log_sigmoid(if_pre[..., h:])
    qc = _to_chunks(q.astype(f32).reshape(b, s, h, dk), c)
    kc = _to_chunks(k.astype(f32).reshape(b, s, h, dk) * dk ** -0.5, c)
    vc = _to_chunks(v.astype(f32).reshape(b, s, h, dv), c)
    ic = _gates_to_chunks(i_pre, c)
    cum_f = jnp.cumsum(_gates_to_chunks(log_f, c), axis=-1)
    causal = jnp.tril(jnp.ones((c, c), dtype=bool))

    def step(carry, inp):
        c_st, n_st, m_prev = carry
        qi, ki, vi, ii, bi = inp
        d_log = jnp.where(causal, bi[..., :, None] - bi[..., None, :] + ii[..., None, :], -jnp.inf)
        inter = bi + m_prev[..., None]
        m_t = jnp.maximum(inter, jnp.max(d_log, axis=-1))
        w_intra = jnp.exp(d_log - m_t[..., None])
        scale = jnp.exp(inter - m_t)
        qk = jnp.einsum('bhtd,bhsd->bhts', qi, ki) * w_intra
        num = (jnp.einsum('bhts,bhsv->bhtv', qk, vi)
               + scale[..., None] * jnp.einsum('bhtd,bhdv->bhtv', qi, c_st))
        den = jnp.sum(qk, axis=-1) + scale * jnp.einsum('bhtd,bhd->bht', qi, n_st)
        h_out = num / jnp.maximum(jnp.abs(den), jnp.exp(-m_t))[..., None]
        b_last = bi[..., -1]
        g_end = b_last[..., None] - bi + ii
        m_new = jnp.maximum(b_last + m_prev, jnp.max(g_end, axis=-1))
        w_end = jnp.exp(g_end - m_new[..., None])
        carry_scale = jnp.exp(b_last + m_prev - m_new)
        c_st = carry_scale[..., None, None] * c_st + jnp.einsum('bhs,bhsd,bhsv->bhdv', w_end, ki, vi)
        n_st = carry_scale[..., None] * n_st + jnp.einsum('bhs,bhsd->bhd', w_end, ki)
        return (c_st, n_st, m_new), h_out

    carry0 = (jnp.zeros((b, h, dk, dv), f32), jnp.zeros((b, h, dk), f32), jnp.zeros((b, h), f32))
    _, hs = lax.scan(step, carry0, (qc, kc, vc, ic, cum_f))
    hs = _from_chunks(hs)
    hs = rms_norm_2(hs, out_norm.reshape(h, dv)).reshape(b, s, ML_DV)
    return (hs.astype(x.dtype) * jax.nn.sigmoid(o_pre)) @ w_out

def conv_ffn(x, w_up, conv_w, conv_b, w_down):
    s = x.shape[1]
    u = x @ w_up
    u_pad = jnp.pad(u, ((0, 0), (CONV_WIDTH - 1, 0), (0, 0)))
    u = sum(u_pad[:, j:j + s] * conv_w[j] for j in range(CONV_WIDTH)) + conv_b
    gate, up = jnp.split(u, 2, axis=-1)
    return (jax.nn.silu(gate) * up) @ w_down

def second_inputs(seed: int = 0) -> dict:
    key = jax.random.key(seed)
    ks = iter(jax.random.split(key, 96))
    f32 = jnp.float32
    D, F2 = D_MODEL, 2 * FFN_DIM

    def nrm(shape, scale):
        return scale * jax.random.normal(next(ks), shape, f32)

    def dense(fan_in, shape):
        return nrm(shape, fan_in ** -0.5)

    def gain(n):
        return 1.0 + nrm((n,), 0.02)

    def unif(shape, lo, hi):
        return jax.random.uniform(next(ks), shape, f32, lo, hi)

    p = {}

    def ffn_params(i):
        p[f"l{i}_norm2"] = gain(D)
        p[f"l{i}_ffn_w_up"] = dense(D, (D, F2))
        p[f"l{i}_ffn_conv_w"] = dense(CONV_WIDTH, (CONV_WIDTH, F2))
        p[f"l{i}_ffn_conv_b"] = nrm((F2,), 0.02)
        p[f"l{i}_ffn_w_down"] = dense(FFN_DIM, (FFN_DIM, D))

    p["x"] = nrm((BATCH, SEQ, D), 1.0)
    p["l0_norm1"] = gain(D)
    p["l0_gla_w_in"] = dense(D, (D, GLA_IN))
    p["l0_gla_w_alpha_up"] = dense(GLA_RANK, (GLA_RANK, GLA_DK))
    p["l0_gla_b_alpha"] = nrm((GLA_DK,), 0.1)
    p["l0_gla_out_norm"] = gain(GLA_DV)
    p["l0_gla_w_out"] = dense(GLA_DV, (GLA_DV, D))
    ffn_params(0)
    p["l1_norm1"] = gain(D)
    p["l1_rwkv_mu"] = unif((RWKV_SHIFT_MIXES, D), 0.0, 1.0)
    p["l1_rwkv_w_rkv"] = dense(D, (3, D, D))
    p["l1_rwkv_w0"] = unif((D,), -6.0, -1.0)
    p["l1_rwkv_w1"] = dense(D, (D, RWKV_DECAY_RANK))
    p["l1_rwkv_w2"] = nrm((RWKV_DECAY_RANK, D), 0.1 * RWKV_DECAY_RANK ** -0.5)
    p["l1_rwkv_a0"] = nrm((D,), 0.1)
    p["l1_rwkv_a1"] = dense(D, (D, RWKV_A_RANK))
    p["l1_rwkv_a2"] = dense(RWKV_A_RANK, (RWKV_A_RANK, D))
    p["l1_rwkv_g1"] = dense(D, (D, RWKV_GATE_RANK))
    p["l1_rwkv_g2"] = dense(RWKV_GATE_RANK, (RWKV_GATE_RANK, D))
    p["l1_rwkv_k_k"] = 0.85 + nrm((D,), 0.05)
    p["l1_rwkv_k_a"] = 1.0 + nrm((D,), 0.05)
    p["l1_rwkv_r_k"] = nrm((D,), 0.1)
    p["l1_rwkv_gn_g"] = gain(D)
    p["l1_rwkv_gn_b"] = nrm((D,), 0.02)
    p["l1_rwkv_w_out"] = dense(D, (D, D))
    ffn_params(1)
    p["l2_norm1"] = gain(D)
    p["l2_sb_w_qkv"] = dense(D, (D, 3 * D))
    p["l2_sb_w_out"] = dense(D, (D, D))
    ffn_params(2)
    p["l3_norm1"] = gain(D)
    p["l3_ml_w_in"] = dense(D, (D, ML_IN))
    p["l3_ml_b_if"] = jnp.concatenate([nrm((ML_HEADS,), 0.1), unif((ML_HEADS,), 3.0, 6.0)])
    p["l3_ml_out_norm"] = gain(ML_DV)
    p["l3_ml_w_out"] = dense(ML_DV, (ML_DV, D))
    ffn_params(3)
    p["final_norm"] = gain(D)
    return p

def second_block(x,
              l0_norm1, l0_gla_w_in, l0_gla_w_alpha_up, l0_gla_b_alpha, l0_gla_out_norm, l0_gla_w_out,
              l0_norm2, l0_ffn_w_up, l0_ffn_conv_w, l0_ffn_conv_b, l0_ffn_w_down,
              l1_norm1, l1_rwkv_mu, l1_rwkv_w_rkv, l1_rwkv_w0, l1_rwkv_w1, l1_rwkv_w2,
              l1_rwkv_a0, l1_rwkv_a1, l1_rwkv_a2, l1_rwkv_g1, l1_rwkv_g2,
              l1_rwkv_k_k, l1_rwkv_k_a, l1_rwkv_r_k, l1_rwkv_gn_g, l1_rwkv_gn_b, l1_rwkv_w_out,
              l1_norm2, l1_ffn_w_up, l1_ffn_conv_w, l1_ffn_conv_b, l1_ffn_w_down,
              l2_norm1, l2_sb_w_qkv, l2_sb_w_out,
              l2_norm2, l2_ffn_w_up, l2_ffn_conv_w, l2_ffn_conv_b, l2_ffn_w_down,
              l3_norm1, l3_ml_w_in, l3_ml_b_if, l3_ml_out_norm, l3_ml_w_out,
              l3_norm2, l3_ffn_w_up, l3_ffn_conv_w, l3_ffn_conv_b, l3_ffn_w_down,
              final_norm):
    mixers = (
        lambda h: gla_mixer(h, l0_gla_w_in, l0_gla_w_alpha_up, l0_gla_b_alpha, l0_gla_out_norm, l0_gla_w_out),
        lambda h: rwkv7_mixer(h, l1_rwkv_mu, l1_rwkv_w_rkv, l1_rwkv_w0, l1_rwkv_w1, l1_rwkv_w2,
                              l1_rwkv_a0, l1_rwkv_a1, l1_rwkv_a2, l1_rwkv_g1, l1_rwkv_g2,
                              l1_rwkv_k_k, l1_rwkv_k_a, l1_rwkv_r_k, l1_rwkv_gn_g, l1_rwkv_gn_b,
                              l1_rwkv_w_out),
        lambda h: stick_breaking_mixer(h, l2_sb_w_qkv, l2_sb_w_out),
        lambda h: mlstm_mixer(h, l3_ml_w_in, l3_ml_b_if, l3_ml_out_norm, l3_ml_w_out),
    )
    norm1 = (l0_norm1, l1_norm1, l2_norm1, l3_norm1)
    norm2 = (l0_norm2, l1_norm2, l2_norm2, l3_norm2)
    ffns = (
        (l0_ffn_w_up, l0_ffn_conv_w, l0_ffn_conv_b, l0_ffn_w_down),
        (l1_ffn_w_up, l1_ffn_conv_w, l1_ffn_conv_b, l1_ffn_w_down),
        (l2_ffn_w_up, l2_ffn_conv_w, l2_ffn_conv_b, l2_ffn_w_down),
        (l3_ffn_w_up, l3_ffn_conv_w, l3_ffn_conv_b, l3_ffn_w_down),
    )
    for layer in range(DEPTH):
        x = x + mixers[layer % N_MIXERS](rms_norm_2(x, norm1[layer]))
        x = x + conv_ffn(rms_norm_2(x, norm2[layer]), *ffns[layer])
    return rms_norm_2(x, final_norm)


def setup_inputs(seed=0):
    out = dict(first_inputs(seed))
    for name, value in second_inputs(seed + 1).items():
        if name != "x":
            out[name + "_2"] = value
    return out


def reference(
    x, p, positions, ffn1_norm, ffn1_w_gate, ffn1_w_up, ffn1_w_down, mix_norm, w_in, ret_gn,
    w_branch_a, w_branch_b, w_out, ffn2_norm, ffn2_w_gate, ffn2_w_up, ffn2_w_down, ple_norm,
    w_ple_gate, w_ple_proj, final_norm, l0_norm1_2, l0_gla_w_in_2, l0_gla_w_alpha_up_2,
    l0_gla_b_alpha_2, l0_gla_out_norm_2, l0_gla_w_out_2, l0_norm2_2, l0_ffn_w_up_2,
    l0_ffn_conv_w_2, l0_ffn_conv_b_2, l0_ffn_w_down_2, l1_norm1_2, l1_rwkv_mu_2,
    l1_rwkv_w_rkv_2, l1_rwkv_w0_2, l1_rwkv_w1_2, l1_rwkv_w2_2, l1_rwkv_a0_2, l1_rwkv_a1_2,
    l1_rwkv_a2_2, l1_rwkv_g1_2, l1_rwkv_g2_2, l1_rwkv_k_k_2, l1_rwkv_k_a_2, l1_rwkv_r_k_2,
    l1_rwkv_gn_g_2, l1_rwkv_gn_b_2, l1_rwkv_w_out_2, l1_norm2_2, l1_ffn_w_up_2, l1_ffn_conv_w_2,
    l1_ffn_conv_b_2, l1_ffn_w_down_2, l2_norm1_2, l2_sb_w_qkv_2, l2_sb_w_out_2, l2_norm2_2,
    l2_ffn_w_up_2, l2_ffn_conv_w_2, l2_ffn_conv_b_2, l2_ffn_w_down_2, l3_norm1_2, l3_ml_w_in_2,
    l3_ml_b_if_2, l3_ml_out_norm_2, l3_ml_w_out_2, l3_norm2_2, l3_ffn_w_up_2, l3_ffn_conv_w_2,
    l3_ffn_conv_b_2, l3_ffn_w_down_2, final_norm_2,
):
    x = first_block(
        x, p, positions, ffn1_norm, ffn1_w_gate, ffn1_w_up, ffn1_w_down, mix_norm, w_in, ret_gn,
        w_branch_a, w_branch_b, w_out, ffn2_norm, ffn2_w_gate, ffn2_w_up, ffn2_w_down, ple_norm,
        w_ple_gate, w_ple_proj, final_norm,
    )
    return second_block(
        x, l0_norm1_2, l0_gla_w_in_2, l0_gla_w_alpha_up_2, l0_gla_b_alpha_2, l0_gla_out_norm_2,
        l0_gla_w_out_2, l0_norm2_2, l0_ffn_w_up_2, l0_ffn_conv_w_2, l0_ffn_conv_b_2,
        l0_ffn_w_down_2, l1_norm1_2, l1_rwkv_mu_2, l1_rwkv_w_rkv_2, l1_rwkv_w0_2, l1_rwkv_w1_2,
        l1_rwkv_w2_2, l1_rwkv_a0_2, l1_rwkv_a1_2, l1_rwkv_a2_2, l1_rwkv_g1_2, l1_rwkv_g2_2,
        l1_rwkv_k_k_2, l1_rwkv_k_a_2, l1_rwkv_r_k_2, l1_rwkv_gn_g_2, l1_rwkv_gn_b_2,
        l1_rwkv_w_out_2, l1_norm2_2, l1_ffn_w_up_2, l1_ffn_conv_w_2, l1_ffn_conv_b_2,
        l1_ffn_w_down_2, l2_norm1_2, l2_sb_w_qkv_2, l2_sb_w_out_2, l2_norm2_2, l2_ffn_w_up_2,
        l2_ffn_conv_w_2, l2_ffn_conv_b_2, l2_ffn_w_down_2, l3_norm1_2, l3_ml_w_in_2,
        l3_ml_b_if_2, l3_ml_out_norm_2, l3_ml_w_out_2, l3_norm2_2, l3_ffn_w_up_2,
        l3_ffn_conv_w_2, l3_ffn_conv_b_2, l3_ffn_w_down_2, final_norm_2,
    )


_drawn_inputs = setup_inputs


def setup_inputs(seed=0):
    import zlib

    import numpy as np

    out = dict(_drawn_inputs(seed))
    spreads = {}
    factors = {'ffn1_norm': 3.48,
     'ret_gn': 4.979,
     'ffn2_norm': 3.613,
     'ple_norm': 31.231,
     'l0_gla_out_norm_2': 5.097,
     'l0_norm2_2': 4.155,
     'l0_ffn_conv_b_2': 4.284,
     'final_norm_2': 8.376}
    for name, (base, spread) in spreads.items():
        noise = np.random.default_rng([zlib.crc32(name.encode()), seed]).standard_normal(out[name].shape)
        drawn = base * np.exp(spread * noise) if base else spread * noise
        out[name] = jnp.asarray(drawn.astype(out[name].dtype))
    for name, factor in factors.items():
        out[name] = (out[name] * factor).astype(out[name].dtype)
    return out
```

```python
from contextlib import ExitStack

import numpy as np
import concourse.bass as bass
from concourse import mybir

F32 = mybir.dt.float32
F32R = mybir.dt.float32r
I32 = mybir.dt.int32
ALU = mybir.AluOpType
ACT = mybir.ActivationFunctionType
AX_X = mybir.AxisListType.X

P = 128
S = 512
NT = S // P
D = 1024
KD = D // P
FF = 2816
KF = FF // P
CHUNK = 64
TOPK = min(256, S // 4)
A_HEADS, A_DIM = 8, 64
R_HEADS, R_QK, R_V = 4, 128, 256
G_HEADS, G_DK, G_DV, G_RANK, G_TAU = 4, 128, 256, 16, 16.0
PLE = 256
NORM_EPS, GN_EPS = 1e-6, 1e-5
NEG_BIG = -1e30
TAKEN = -3.0e38

RING = 4
BANKS = 4
SLAB = 8 * P
DOWN_SLABS = 3
DOWN_LAST = (KF - 2 * 8) * P

TWO_PI = 2.0 * np.pi
PI_A = 6.28125
PI_B = float(np.float32(np.floor((TWO_PI - PI_A) * 2 ** 21) / 2 ** 21))
PI_C = float(np.float32(TWO_PI - PI_A - PI_B))
PI_MAX = 3.1415925

VECTORS = [("ffn1_norm", KD), ("mix_norm", KD), ("ret_gn", KD), ("ffn2_norm", KD), ("ple_norm", KD),
           ("final_norm", KD), ("l0_norm1", KD), ("gla_out_norm", KD), ("l0_norm2", KD), ("final_norm_2", KD),
           ("b_alpha", 4), ("conv_w0", 2 * KF), ("conv_w1", 2 * KF), ("conv_w2", 2 * KF), ("conv_b", 2 * KF)]
COL = {name: sum(n for _, n in VECTORS[:i]) for i, (name, _) in enumerate(VECTORS)}
NCOLS = sum(n for _, n in VECTORS)
C_ID, C_MASK, C_INV_A, C_INV_R, C_SGN_A, C_SGN_R, NCONST = 0, P, P + CHUNK, P + CHUNK + 1, P + CHUNK + 2, P + CHUNK + 3, P + CHUNK + 4

MIX = [("avw",), ("rv", 0), ("rg", 0, 0), ("rg", 0, 1), ("rv", 1), ("kk",), ("iq", 0), ("iq", 1), ("iq", 2), ("iq", 3),
       ("rq", 0), ("rk", 0), ("index", 3), ("rscore", 0), ("rg", 1, 0), ("ry", 0), ("rg", 1, 1), ("rnorm", 0),
       ("rq", 1), ("rk", 1), ("index", 2), ("rscore", 1), ("rv", 2), ("ry", 1), ("rg", 2, 0), ("rnorm", 1),
       ("rg", 2, 1), ("rq", 2), ("rk", 2), ("index", 1), ("rscore", 2), ("rv", 3), ("ry", 2), ("rg", 3, 0),
       ("rnorm", 2), ("rg", 3, 1), ("rq", 3), ("rk", 3), ("aq", 0), ("rscore", 3), ("aq", 1), ("ry", 3), ("aq", 2),
       ("rnorm", 3), ("aq", 3), ("logits", 3), ("logits", 0), ("attend", 3), ("logits", 2), ("attend", 0),
       ("logits", 1), ("attend", 2), ("attend", 1)]
for _m in range(0, KD, 2):
    MIX += [("wa", _m)]
    for _q in (_m, _m + 1):
        MIX += [("ga", _q), ("gb", _q), ("wb", _q)]
MIX += [("wout", m) for m in range(KD)]

PLE_STEPS = [("pgate", 0), ("pgate", 1), ("pproj", 0), ("pproj", 1)] + [("pgate", m) for m in range(2, KD)]

GLA = [("alow",), ("gv", 0), ("alpha",), ("gk", 0), ("gq", 0), ("gstate", 0), ("gv", 1), ("gk", 1), ("gq", 1),
       ("gout", 0), ("gstate", 1), ("gv", 2), ("gk", 2), ("gq", 2), ("gout", 1), ("gstate", 2), ("gv", 3), ("gk", 3),
       ("gq", 3), ("gout", 2), ("gstate", 3), ("gr", 0), ("gr", 1), ("gout", 3)]
GLA += [("gt", 0), ("gt", 1)]
for _c in range(2, KD):
    GLA += [("gr", _c), ("gt", _c)]
GLA += [("gwout", m) for m in range(KD)]

PROJECTS = {"avw": (1, 1), "rv": (2, 2), "rg": (1, 1), "kk": (1, 1), "iq": (1, 1), "rq": (1, 1), "rk": (1, 1),
            "aq": (1, 1), "attend": (0, 1), "wa": (1, 2), "ga": (1, 1), "gb": (1, 1), "wb": (1, 1), "wout": (1, 1),
            "pgate": (1, 1), "pproj": (1, 4), "alow": (1, 1), "alpha": (0, 4), "gk": (1, 1), "gq": (1, 1),
            "gv": (2, 2), "gr": (1, 1), "gout": (0, 2), "gwout": (1, 1)}
ROPE = ("kk", "iq", "aq", "rq", "rk")


class Plan:

    def __init__(self):
        self.slabs = self.tiles = self.mids = 0
        self.release = []
        self.width = []
        self.first = {}

    def up(self, name):
        self.first[name] = (self.slabs, self.tiles)
        for _ in range(2 * KF):
            self.tiles += 1
            self.release.append(("tile", self.tiles))
            self.width.append(SLAB)
        self.slabs += 2 * KF

    def down(self, name):
        self.first[name] = (self.slabs, self.tiles)
        for _ in range(KD):
            self.tiles += 1
            for s in range(DOWN_SLABS - 1):
                self.mids += 1
                self.release.append(("mid", self.mids))
                self.width.append(SLAB)
            self.release.append(("tile", self.tiles))
            self.width.append(DOWN_LAST)
        self.slabs += KD * DOWN_SLABS

    def steps(self, name, steps):
        self.first[name] = (self.slabs, self.tiles)
        for step in steps:
            slabs, tiles = PROJECTS.get(step[0], (0, 0))
            self.first[step] = (self.slabs, self.tiles)
            self.tiles += tiles
            for _ in range(slabs):
                self.release.append(("tile", self.tiles))
                self.width.append({"avw": KD * 72, "alow": KD * G_RANK}.get(step[0], SLAB))
            self.slabs += slabs


def layer_program(nc, A, out):
    plan = Plan()
    plan.up("up1")
    plan.down("down1")
    plan.steps("mix", MIX)
    plan.up("up2")
    plan.down("down2")
    plan.steps("ple", PLE_STEPS)
    plan.steps("gla", GLA)
    plan.up("up3")
    plan.down("down3")
    N = plan.slabs

    with ExitStack() as ctx:
        def sb(name, shape, dt=F32, on=ctx):
            return on.enter_context(nc.sbuf_tensor(name, shape, dt))

        def sem(name):
            return ctx.enter_context(nc.semaphore(name))

        w_raw = sb("w_raw", [P, RING, SLAB])
        w_hi = sb("w_hi", [P, RING, SLAB], F32R)
        w_lo = sb("w_lo", [P, RING, SLAB], F32R)
        h = sb("h", [P, KD, S])
        u_hi = sb("u_hi", [P, KD, S], F32R)
        u_lo = sb("u_lo", [P, KD, S], F32R)
        tmp = sb("tmp", [P, 6, S])
        ssum = sb("ssum", [P, S])
        rstd = sb("rstd", [P, S])
        ones = sb("ones", [P, P])
        cols = sb("cols", [P, NCOLS])
        consts = sb("consts", [P, NCONST])
        eps = sb("eps", [P, 2])
        rstd_tok = sb("rstd_tok", [P, NT])
        small = sb("small", [P, 176])
        gate_t, up_t, sq = tmp[:, 0:2, :], tmp[:, 2:4, :], tmp[:, 4:6, :]
        neg_max, row_sum, row_max, row_inv = (small[:, c:c + 16] for c in (16, 32, 64, 80))
        top8 = small[:, 168:176]
        head_sq, head_root, head_x, head_rstd = (small[:, c:c + 16] for c in (96, 112, 128, 144))
        ident = consts[:, C_ID:C_ID + P]

        with ExitStack() as region:
            hid_hi = sb("hid_hi", [P, KF, S], F32R, region)
            hid_lo = sb("hid_lo", [P, KF, S], F32R, region)
        with ExitStack() as region:
            yr_hi = sb("yr_hi", [P, KD, S], F32R, region)
            yr_lo = sb("yr_lo", [P, KD, S], F32R, region)
            with ExitStack() as inner:
                q8 = sb("q8", [P, 4, S], F32, inner)
                ikd = sb("ikd", [P, S], F32, inner)
                akd = sb("akd", [P, S], F32, inner)
                bias = sb("bias", [P, NT * (NT + 1) // 2 * P], F32, inner)
                avt = sb("avt", [P, NT, 72], F32, inner)
                with ExitStack() as sub:
                    cos_a = sb("cos_a", [P, S], F32, sub)
                    sin_a = sb("sin_a", [P, S], F32, sub)
                    cos_r = sb("cos_r", [P, S], F32, sub)
                    sin_r = sb("sin_r", [P, S], F32, sub)
                    rv = sb("rv", [P, 2, NT, R_V], F32, sub)
                    srg = sb("srg", [P, 2, 2, S], F32, sub)
                    rqk = sb("rqk", [P, 2, S], F32, sub)
                    wts = sb("wts", [P, NT * (NT + 1) // 2 * P], F32, sub)
                    dec = sb("dec", [P, S], F32, sub)
                    work = sb("work", [P, S], F32, sub)
                with ExitStack() as sub:
                    pt = sb("pt", [P, 2, S], F32, sub)
                    probs = sb("probs", [P, 5 * 2 * S], F32, sub)
                    ya_hi = sb("ya_hi", [P, 4, S], F32R, sub)
                    ya_lo = sb("ya_lo", [P, 4, S], F32R, sub)
            with ExitStack() as inner:
                mg_hi = sb("mg_hi", [P, KD, S], F32R, inner)
                mg_lo = sb("mg_lo", [P, KD, S], F32R, inner)
        with ExitStack() as region:
            gy_hi = sb("gy_hi", [P, KD, S], F32R, region)
            gy_lo = sb("gy_lo", [P, KD, S], F32R, region)
            gcum = sb("gcum", [P, G_HEADS, S], F32, region)
            gres = sb("gres", [P, S], F32, region)
            ssum2 = sb("ssum2", [P, S], F32, region)
            with ExitStack() as inner:
                proj = sb("proj", [P, KD, S], F32, inner)
                p_raw = sb("p_raw", [P, 2, S], F32, inner)
                p_hi = sb("p_hi", [P, 2, S], F32R, inner)
                p_lo = sb("p_lo", [P, 2, S], F32R, inner)
            with ExitStack() as inner:
                gvt = sb("gvt", [P, 2, NT, G_DV], F32, inner)
                gkq = sb("gkq", [P, 2, S], F32, inner)
                gki = sb("gki", [P, S], F32, inner)
                gqd = sb("gqd", [P, S], F32, inner)
                gket = sb("gket", [P, NT, P], F32, inner)
                gsc = sb("gsc", [P, NT, P], F32, inner)
                gst = sb("gst", [P, 7, G_DV], F32, inner)
                go = sb("go", [P, G_HEADS, NT, G_DV], F32, inner)
                walpha = sb("walpha", [P, 4 * P], F32, inner)
                alow_t = sb("alow_t", [P, S], F32, inner)

        acc = ctx.enter_context(nc.psum_tensor("acc", [P, BANKS, S], F32))
        aux = ctx.enter_context(nc.psum_tensor("aux", [P, 4, S], F32))

        raw_loaded = [sem(f"raw_loaded{i}") for i in range(RING)]
        hi_ready = sem("hi_ready")
        lo_ready = sem("lo_ready")
        slab_used = sem("slab_used")
        tile_done = sem("tile_done")
        tile_freed = sem("tile_freed")
        x_loaded = [sem(f"x_loaded{i}") for i in range(KD)]
        vec_loaded = sem("vec_loaded")
        pos_loaded = sem("pos_loaded")
        consts_set = sem("consts_set")
        gate_act = sem("gate_act")
        prod_ready = sem("prod_ready")
        prod_hi = sem("prod_hi")
        hid_ready = sem("hid_ready")
        conv_set = sem("conv_set")
        conv_done = sem("conv_done")
        conv_step = sem("conv_step")
        u_hi_ready = sem("u_hi_ready")
        u_ready = sem("u_ready")
        sq_ready = sem("sq_ready")
        sq_added = sem("sq_added")
        stat_done = sem("stat_done")
        root_ready = sem("root_ready")
        rstd_ready = sem("rstd_ready")
        ms2_ready = sem("ms2_ready")
        dve_step = sem("dve_step")
        angle_ready = sem("angle_ready")
        table_ready = sem("table_ready")
        swapped = [sem("swapped0"), sem("swapped1")]
        rope_ready = sem("rope_ready")
        keys_copied = sem("keys_copied")
        dec_loaded = sem("dec_loaded")
        idx_scored = sem("idx_scored")
        idx_relu = sem("idx_relu")
        idx_added = sem("idx_added")
        sel_ready = sem("sel_ready")
        rs_done = sem("rs_done")
        rw_ready = sem("rw_ready")
        rv_ready = sem("rv_ready")
        ry_done = sem("ry_done")
        ry_sq = sem("ry_sq")
        ry_sum = sem("ry_sum")
        ry_freed = sem("ry_freed")
        lg_done = sem("lg_done")
        lg_read = sem("lg_read")
        neg_ready = sem("neg_ready")
        exp_done = sem("exp_done")
        p_ready = sem("p_ready")
        pt_done = sem("pt_done")
        pt_ready = sem("pt_ready")
        split_in = sem("split_in")
        split_hi = sem("split_hi")
        split_ready = sem("split_ready")
        pt_loaded = sem("ple_loaded")
        h_updated = sem("h_updated")
        p_split = sem("p_split")
        gsc_ready = sem("gsc_ready")
        out_ready = sem("out_ready")
        al_ln = sem("al_ln")
        al_ready = sem("al_ready")
        ge_ready = sem("ge_ready")
        gd_ready = sem("gd_ready")
        gqk_ready = sem("gqk_ready")
        gke_done = sem("gke_done")
        gke_ready = sem("gke_ready")
        gs_done = sem("gs_done")
        gkv_done = sem("gkv_done")
        gst_ready = sem("gst_ready")
        gv_ready = sem("gv_ready")
        go_sq = sem("go_sq")
        gon_ready = sem("gon_ready")
        gt_done = sem("gt_done")
        out_stored = sem("out_stored")

        SQ = [0, 8, 16, 24, 32, 48, 56, 64]
        rope_steps = [s for s in MIX if s[0] in ROPE]
        gate_steps = [s for s in MIX + PLE_STEPS + GLA if s[0] in ("rg", "ga", "gb", "pgate", "gr")]
        split_steps = []
        for s in MIX:
            if s[0] == "rnorm":
                split_steps += [(s, 0), (s, 1)]
            elif s[0] in ("attend", "wb"):
                split_steps += [(s, 0)]
        split_steps += [(("gt", c), 0) for c in range(KD)]
        made_steps = [s for s in split_steps if s[0][0] != "attend"]
        index_units = {b: A_HEADS * i for i, b in enumerate((3, 2, 1))}
        logit_steps = [s for s in MIX if s[0] == "logits"]
        attend_steps = [s for s in MIX if s[0] == "attend"]
        pt_base = {}
        for s in attend_steps:
            pt_base[s] = sum(2 * (t[1] + 1) for t in attend_steps[:attend_steps.index(s)])
        FFNS = 3

        def nth(steps, step):
            return steps.index(step)

        def splits_before(step):
            return sum(MIX.index(s) < MIX.index(step) for s, _ in split_steps if s in MIX)

        def gates_before(step):
            before = {"rg": 1, "ga": 1, "gb": 1, "pgate": 2, "gr": 2}[step[0]]
            return before * KF + nth(gate_steps, step)

        z_gate = tmp.rearrange("p a b -> p (a b)")[:, 2 * S:3 * S + 2]
        z_up = tmp.rearrange("p a b -> p (a b)")[:, 3 * S + 2:4 * S + 4]
        GATES_FFN = [0, KF + nth(gate_steps, ("pgate", 0)), 2 * KF + len(gate_steps)]
        bias_at = {0: 0, 1: P, 2: 3 * P, 3: 6 * P}
        wts_at = {0: 0, 1: 4 * P, 2: 7 * P, 3: 9 * P}
        probs_at = {3: 0, 0: 8 * S, 2: 0, 1: 6 * S}

        def probs_of(b, hd):
            n = (b + 1) * P
            return probs[:, probs_at[b] + hd * n:probs_at[b] + (hd + 1) * n]

        def state_bank(c):
            at = (c // 2) % 2 * G_DV
            return aux[:, c % 2, at:at + G_DV]

        def blk(b):
            return slice(b * P, (b + 1) * P)

        def load_count(n):
            return 16 * (n // RING + 1)

        block = ctx.enter_context(nc.Block())

        @block.sync
        def _(sp):
            def load(n, src):
                if n >= RING:
                    sp.wait_ge(lo_ready, n - RING + 1)
                sp.dma_start(w_raw[:, n % RING, 0:plan.width[n]], src).then_inc(raw_loaded[n % RING], 16)

            def load_up(name, w, first=0):
                n0 = plan.first[name][0]
                with sp.Fori(first // RING, 2 * KF // RING) as i:
                    for j in range(RING):
                        sp.wait_ge(lo_ready, i * RING + (n0 + j - RING + 1))
                        sp.dma_start(w_raw[:, (n0 + j) % RING, :], w[i * RING + j]).then_inc(raw_loaded[(n0 + j) % RING], 16)

            def load_down(name, w):
                n0 = plan.first[name][0]
                with sp.Fori(0, 2) as i:
                    for j in range(4 * DOWN_SLABS):
                        width, at = plan.width[n0 + j], (j % DOWN_SLABS) * SLAB
                        sp.wait_ge(lo_ready, i * (4 * DOWN_SLABS) + (n0 + j - RING + 1))
                        sp.dma_start(w_raw[:, (n0 + j) % RING, 0:width],
                                     w[i * 4 + j // DOWN_SLABS][:, at:at + width]).then_inc(raw_loaded[(n0 + j) % RING], 16)

            sp.dma_start(cols[:, :], A["vectors"]).then_inc(vec_loaded, 16)
            sp.dma_start(consts[:, :], A["consts"]).then_inc(vec_loaded, 16)
            for n in range(2):
                load(n, A["w_up1"][n])
            for c in range(KD):
                sp.dma_start(h[:, c, :], A["xT"][c]).then_inc(x_loaded[c], 16)
            for n in range(2, RING):
                load(n, A["w_up1"][n])
            load_up("up1", A["w_up1"], RING)
            load_down("down1", A["w_down1"])

            mix0 = plan.first["mix"][0]
            mix_end = plan.first["up2"][0]
            loaded = [mix0]

            def load_mix(upto):
                while loaded[0] < min(upto, mix_end):
                    n = loaded[0]
                    load(n, A["w_avw"] if n == mix0 else A["w_mix"][n - mix0 - 1])
                    loaded[0] += 1
            load_mix(mix0 + 3)
            sp.wait_ge(tile_done, plan.first["mix"][1])
            sp.dma_start(tmp[:, 0, :].bitcast(I32), A["positions"]).then_inc(pos_loaded, 16)
            sp.dma_start(dec[:, :], A["decay"][0]).then_inc(dec_loaded, 16)
            for step in MIX:
                n, t = plan.first[step]
                load_mix(n + 6)
                if step[0] in ROPE:
                    z = nth(rope_steps, step)
                    half = 64 if step[0] in ("rq", "rk") else 32
                    sp.wait_ge(tile_freed, t + 1)
                    for g in range(P // half):
                        to, of = g * half, (g ^ 1) * half
                        sp.dma_start(up_t[to:to + half, z % 2, :], gate_t[of:of + half, z % 2, :]).then_inc(swapped[z % 2], 16)
                if step[0] == "iq" and step[1] == 0:
                    sp.wait_ge(rope_ready, 1)
                    sp.dma_start(ikd[64:128, :], ikd[0:64, :]).then_inc(keys_copied, 16)
                    sp.dma_start(akd[0:64, :], akd[64:128, :]).then_inc(keys_copied, 16)
                if step[0] == "ry" and step[1] + 1 < R_HEADS:
                    sp.wait_ge(rw_ready, NT * (step[1] + 1))
                    sp.dma_start(dec[:, :], A["decay"][step[1] + 1]).then_inc(dec_loaded, 16)
            load_up("up2", A["w_up2"])
            load_down("down2", A["w_down2"])
            ple0 = plan.first["ple"][0]
            for n in range(ple0, ple0 + 4):
                load(n, A["w_ple"][n - ple0])
            sp.wait_ge(tile_done, plan.first["ple"][1])
            sp.dma_start(p_raw[:, :, :], A["pT"]).then_inc(pt_loaded, 16)
            for n in range(ple0 + 4, plan.first["gla"][0]):
                load(n, A["w_ple"][n - ple0])
            gla0 = plan.first["gla"][0]
            load(gla0, A["w_alow"])
            for n in range(gla0 + 1, gla0 + 3):
                load(n, A["w_gla"][n - gla0 - 1])
            sp.wait_ge(h_updated, KD)
            sp.dma_start(walpha[0:G_RANK, :], A["w_alpha"]).then_inc(pt_loaded, 16)
            for n in range(gla0 + 3, plan.first["up3"][0]):
                load(n, A["w_gla"][n - gla0 - 1])
            load_up("up3", A["w_up3"])
            load_down("down3", A["w_down3"])
            for c in range(KD):
                sp.wait_ge(out_ready, c + 1)
                sp.dma_start(out[c], h[:, c, :]).then_inc(out_stored, 16)
            sp.wait_ge(out_stored, 16 * KD)

        @block.gpsimd
        def _(pool):
            pool.memset(ones[:, :], 1.0).then_inc(consts_set, 1)
            pool.memset(eps[:, 0:1], NORM_EPS).then_inc(consts_set, 1)
            pool.memset(eps[:, 1:2], GN_EPS).then_inc(consts_set, 1)

            def lo_part(slot, width, count):
                pool.wait_ge(hi_ready, count)
                pool.tensor_tensor(w_lo[:, slot, 0:width], w_raw[:, slot, 0:width], w_hi[:, slot, 0:width].bitcast(F32),
                                   ALU.subtract).then_inc(lo_ready, 1)

            def lo_run(n0, n1):
                rounds = (n1 - n0) // RING
                if rounds:
                    with pool.Fori(0, rounds) as i:
                        for j in range(RING):
                            lo_part((n0 + j) % RING, SLAB, i * RING + (n0 + j + 1))
                for n in range(n0 + rounds * RING, n1):
                    lo_part(n % RING, SLAB, n + 1)

            def lo_down(n0):
                with pool.Fori(0, 2) as i:
                    for j in range(4 * DOWN_SLABS):
                        lo_part((n0 + j) % RING, plan.width[n0 + j], i * (4 * DOWN_SLABS) + (n0 + j + 1))

            def at(name):
                return plan.first[name][0]
            lo_run(0, at("down1"))
            lo_down(at("down1"))
            lo_part(at("mix") % RING, plan.width[at("mix")], at("mix") + 1)
            lo_run(at("mix") + 1, at("down2"))
            lo_down(at("down2"))
            lo_run(at("ple"), at("gla"))
            lo_part(at("gla") % RING, plan.width[at("gla")], at("gla") + 1)
            lo_run(at("gla") + 1, at("down3"))
            lo_down(at("down3"))

        @block.scalar
        def _(act):
            done = [0]

            def hi_part(slot, width, count, used):
                act.wait_ge(raw_loaded[slot], count)
                if used is not None:
                    act.wait_ge(used[0], used[1])
                act.activation(w_hi[:, slot, 0:width], w_raw[:, slot, 0:width], ACT.Copy).then_inc(hi_ready, 1)

            def split_slabs(upto):
                while done[0] < min(upto, N):
                    n = done[0]
                    used = None
                    if n >= RING:
                        kind, count = plan.release[n - RING]
                        used = (tile_done if kind == "tile" else slab_used, count)
                    hi_part(n % RING, plan.width[n], load_count(n), used)
                    done[0] += 1

            def norm_chunk(k, c, gain, tile=None):
                if tile is not None:
                    act.wait_ge(tile_freed, tile + 1)
                if gain is not None:
                    act.activation(u_hi[:, c, :], h[:, c, :], ACT.Copy, scale=gain).then_inc(u_hi_ready, 1)
                e = SQ[k] + c
                if e >= 2:
                    act.wait_ge(sq_added, e - 1)
                act.activation(sq[:, e % 2, :], h[:, c, :], ACT.Square).then_inc(sq_ready, 1)

            def root(k):
                act.wait_ge(stat_done, k + 1)
                act.activation(sq[:, 1, :], aux[:, 0, :], ACT.Sqrt, bias=eps[:, 0:1], scale=1.0 / D).then_inc(root_ready, 1)

            def ffn_up(f, name, conv=False):
                n0, t0 = plan.first[name]

                def pair(b, i2, i4, split_a, split_b):
                    if conv:
                        act.wait_ge(tile_freed, i4 + (t0 + 2 * b + 1))
                        act.activation(tmp[:, 0, :], z_gate[:, 2:2 + S], ACT.Identity, scale=conv_col("conv_w2", i2, b, 0),
                                       bias=conv_col("conv_b", i2, b, 0)).then_inc(conv_set, 1)
                        act.wait_ge(conv_done, i4 + (2 * b + 1))
                        act.activation(tmp[:, 0, :], tmp[:, 0, :], ACT.Silu).then_inc(gate_act, 1)
                        split_a()
                        act.wait_ge(tile_freed, i4 + (t0 + 2 * b + 2))
                        act.activation(tmp[:, 1, :], z_up[:, 2:2 + S], ACT.Identity, scale=conv_col("conv_w2", i2, b, KF),
                                       bias=conv_col("conv_b", i2, b, KF)).then_inc(conv_set, 1)
                    else:
                        act.wait_ge(tile_freed, i4 + (t0 + 2 * b + 1))
                        act.activation(gate_t[:, b, :], gate_t[:, b, :], ACT.Silu).then_inc(gate_act, 1)
                        split_a()
                    act.wait_ge(prod_ready, i2 + (f * KF + b + 1))
                    src = tmp[:, 1, :] if conv else up_t[:, b, :]
                    act.activation(hid_hi[:, i2 + b, :], src, ACT.Copy).then_inc(prod_hi, 1)
                    split_b()

                rounds = KF // 2
                with act.Fori(0, rounds - 1) as i:
                    for b in range(2):
                        def ahead(j):
                            n = n0 + RING + j
                            hi_part(n % RING, SLAB, i * 16 + load_count(n), (tile_done, i * 4 + (t0 + j + 1)))
                        pair(b, i * 2, i * 4, lambda: ahead(2 * b), lambda: ahead(2 * b + 1))
                done[0] = n0 + 4 * rounds
                for b in range(2):
                    p = 2 * (rounds - 1) + b
                    pair(b, 2 * (rounds - 1), 4 * (rounds - 1), lambda: split_slabs(n0 + 2 * p + 5), lambda: split_slabs(n0 + 2 * p + 6))

            def ffn_down(name, k, gain):
                n0, t0 = plan.first[name]
                for m in range(KD):
                    split_slabs(n0 + DOWN_SLABS * (m + 1) + RING)
                    norm_chunk(k, m, gain(m), t0 + m)

            def tables():
                for i, (dst, scale) in enumerate(((cos_a, None), (sin_a, C_SGN_A), (cos_r, None), (sin_r, C_SGN_R))):
                    act.wait_ge(angle_ready, i + 1)
                    sc = 1.0 if scale is None else consts[:, scale:scale + 1]
                    act.activation(dst[:, :], tmp[:, 2 + i % 2, :], ACT.Sin, scale=sc).then_inc(table_ready, 1)

            def split_to_hi(step, half, dst, src):
                act.wait_ge(split_in, nth(made_steps, (step, half)) + 1)
                act.activation(dst, src, ACT.Copy).then_inc(split_hi, 1)

            def col(name, c):
                return cols[:, COL[name] + c:COL[name] + c + 1]

            def conv_col(name, i2, b, off):
                at = i2 + (COL[name] + off + b)
                return cols[:, at:at + 1] if isinstance(at, int) else cols[:, bass.ds(at, 1)]

            act.wait_ge(vec_loaded, 32)
            for c in range(KD):
                act.wait_ge(x_loaded[c], 16)
                norm_chunk(0, c, col("ffn1_norm", c))
                split_slabs(min(c + 1, RING))
            act.wait_ge(consts_set, 3)
            root(0)
            ffn_up(0, "up1")
            ffn_down("down1", 1, lambda m: col("mix_norm", m))
            act.wait_ge(stat_done, 2)
            act.activation(small[:, 0:NT], aux[:, 1, 0:NT], ACT.Sqrt, bias=eps[:, 0:1], scale=1.0 / D)
            act.activation(sq[:, 1, :], aux[:, 0, :], ACT.Sqrt, bias=eps[:, 0:1], scale=1.0 / D).then_inc(root_ready, 1)
            tables()

            for step in MIX:
                kind = step[0]
                n, t = plan.first[step]
                if kind in ("rg", "ga", "gb"):
                    act.wait_ge(tile_freed, t + 1)
                    buf = {"rg": lambda: srg[:, step[1] % 2, step[2], :], "ga": lambda: up_t[:, 0, :], "gb": lambda: up_t[:, 1, :]}[kind]()
                    act.activation(buf, buf, ACT.Silu if kind == "rg" else ACT.Sigmoid).then_inc(gate_act, 1)
                elif kind == "index":
                    nk = (step[1] + 1) * P
                    act.wait_ge(split_ready, splits_before(step))
                    for hd in range(A_HEADS):
                        j = index_units[step[1]] + hd
                        act.wait_ge(idx_scored, j + 1)
                        if j >= 2:
                            act.wait_ge(idx_added, j - 1)
                        act.activation(sq[:, j % 2, 0:nk], aux[:, 2 + j % 2, 0:nk], ACT.Relu, scale=A_DIM ** -0.5).then_inc(idx_relu, 1)
                elif kind == "rnorm":
                    r = step[1]
                    act.wait_ge(ry_done, r + 1)
                    for half in range(2):
                        act.activation(sq[:, half, :], aux[:, half, :], ACT.Square).then_inc(ry_sq, 1)
                    act.wait_ge(stat_done, 3 + r)
                    act.activation(sq[:, 1, :], aux[:, 2, :], ACT.Sqrt, bias=eps[:, 1:2], scale=1.0 / R_V).then_inc(root_ready, 1)
                    for half in range(2):
                        split_to_hi(step, half, yr_hi[:, 2 * r + half, :], sq[:, half, :])
                elif kind == "logits":
                    b, i = step[1], nth(logit_steps, step)
                    act.wait_ge(neg_ready, i + 1)
                    for hd in range(A_HEADS):
                        act.activation(probs_of(b, hd), probs_of(b, hd), ACT.Exp, bias=neg_max[:, 8 * (i % 2) + hd:8 * (i % 2) + hd + 1],
                                       accum_out=row_sum[:, 8 * (i % 2) + hd:8 * (i % 2) + hd + 1]).then_inc(exp_done, 1)
                elif kind == "attend":
                    b = step[1]
                    for g in range(2 * (b + 1)):
                        gg = pt_base[step] + g
                        act.wait_ge(pt_done, gg + 1)
                        act.activation(pt[:, gg % 2, :], aux[:, 2 + gg % 2, :], ACT.Copy).then_inc(pt_ready, 1)
                    act.wait_ge(tile_freed, t + 1)
                    act.activation(ya_hi[:, :, blk(b)], tmp[:, 0, :].rearrange("p (c q) -> p c q", c=4), ACT.Copy).then_inc(split_hi, 1)
                elif kind == "wb":
                    split_to_hi(step, 0, mg_hi[:, step[1], :], gate_t[:, step[1] % 2, :])
                elif kind == "wout":
                    norm_chunk(2, step[1], col("ffn2_norm", step[1]), t)
                split_slabs(n + PROJECTS.get(kind, (0, 0))[0] + RING)
            root(6)
            ffn_up(1, "up2")
            ffn_down("down2", 3, lambda m: col("ple_norm", m))
            root(7)

            act.wait_ge(pt_loaded, 16)
            for c in range(2):
                act.activation(p_hi[:, c, :], p_raw[:, c, :], ACT.Copy).then_inc(p_split, 1)

            def gla_squares(m):
                act.wait_ge(h_updated, m + 1)
                for e, scale in ((0, 1.0), (1, col("final_norm", m))):
                    act.wait_ge(sq_added, SQ[4] + 2 * m + e - 1)
                    act.activation(sq[:, e, :], h[:, m, :], ACT.Square, scale=scale).then_inc(sq_ready, 1)

            for step in PLE_STEPS:
                n, t = plan.first[step]
                if step[0] == "pgate":
                    m = step[1]
                    act.wait_ge(tile_freed, t + 1)
                    act.activation(gate_t[:, m % 2, :], gate_t[:, m % 2, :], ACT.Sigmoid).then_inc(gate_act, 1)
                    if m >= 2:
                        gla_squares(m)
                elif step[1] == 1:
                    gla_squares(0)
                    gla_squares(1)
                split_slabs(n + PROJECTS[step[0]][0] + RING)
            act.wait_ge(tile_done, plan.first["gla"][1])
            for m in range(KD):
                act.activation(u_hi[:, m, :], h[:, m, :], ACT.Copy, scale=small[:, 48 + m:49 + m]).then_inc(u_hi_ready, 1)
            act.wait_ge(stat_done, 9)
            act.activation(sq[:, 1, :], aux[:, 0, :], ACT.Sqrt, bias=eps[:, 0:1], scale=1.0 / D)
            act.activation(small[:, 0:NT], aux[:, 2, 0:NT], ACT.Sqrt, bias=eps[:, 0:1], scale=1.0 / D).then_inc(root_ready, 1)
            act.wait_ge(ms2_ready, 1)
            act.activation(up_t[:, 1, :], up_t[:, 0, :], ACT.Sqrt, bias=eps[:, 0:1], scale=1.0 / D)
            act.activation(small[:, 4:4 + NT], small[:, 12:12 + NT], ACT.Sqrt, bias=eps[:, 0:1], scale=1.0 / D).then_inc(root_ready, 1)

            for step in GLA:
                kind = step[0]
                n, t = plan.first[step]
                if kind == "alpha":
                    for c in range(G_HEADS):
                        x = gate_t[:, c % 2, :]
                        act.wait_ge(tile_freed, t + c + 1)
                        if c >= 2:
                            act.wait_ge(al_ready, c - 1)
                        act.activation(x, gcum[:, c, :], ACT.Abs).then_inc(al_ln, 1)
                        act.wait_ge(al_ln, 3 * c + 1)
                        act.activation(x, x, ACT.Exp, scale=-1.0).then_inc(al_ln, 1)
                        act.wait_ge(al_ln, 3 * c + 2)
                        act.activation(x, x, ACT.Ln, bias=ones[:, 0:1]).then_inc(al_ln, 1)
                elif kind == "gstate":
                    r = step[1]
                    act.wait_ge(al_ready, G_HEADS)
                    if r:
                        act.wait_ge(gst_ready, 7 * r)
                    act.activation(gate_t[:, 0, :], gcum[:, r, :], ACT.Exp).then_inc(ge_ready, 1)
                    act.activation(gate_t[:, 1, :], gcum[:, r, :], ACT.Exp, scale=-1.0).then_inc(ge_ready, 1)
                    act.wait_ge(gd_ready, r + 1)
                    act.activation(up_t[:, 0, :], up_t[:, 0, :], ACT.Exp).then_inc(ge_ready, 1)
                    act.wait_ge(gke_done, r + 1)
                    act.activation(gket[:, :, :], aux[:, 3, :].rearrange("p (a b) -> p a b", a=NT), ACT.Copy).then_inc(gke_ready, 1)
                elif kind == "gout":
                    r = step[1]
                    for tt in range(NT):
                        act.wait_ge(tile_freed, t + tt // 2 + 1)
                        act.activation(sq[:, tt % 2, 0:G_DV], go[:, r, tt, :], ACT.Square,
                                       accum_out=head_sq[:, 4 * r + tt:4 * r + tt + 1]).then_inc(go_sq, 1)
                        act.wait_ge(go_sq, NT * r + tt + 1)
                    if r == G_HEADS - 1:
                        act.activation(head_root, head_sq, ACT.Sqrt, bias=eps[:, 0:1], scale=1.0 / G_DV).then_inc(root_ready, 1)
                elif kind == "gr":
                    act.wait_ge(tile_freed, t + 1)
                    act.activation(gate_t[:, step[1] % 2, :], gate_t[:, step[1] % 2, :], ACT.Silu).then_inc(gate_act, 1)
                elif kind == "gt":
                    split_to_hi(step, 0, gy_hi[:, step[1], :], up_t[:, step[1] % 2, :])
                elif kind == "gwout":
                    norm_chunk(5, step[1], col("l0_norm2", step[1]), t)
                split_slabs(n + PROJECTS.get(kind, (0, 0))[0] + RING)
            root(9)
            ffn_up(2, "up3", conv=True)
            ffn_down("down3", 6, lambda m: None)
            root(10)

        @block.vector
        def _(dve):
            step_no = [0]

            def link(ins):
                step_no[0] += 1
                ins.then_inc(dve_step, 1)
                dve.wait_ge(dve_step, step_no[0])

            def col(name, c):
                return cols[:, COL[name] + c:COL[name] + c + 1]

            def norm_chunk(k, c, gain):
                if gain is not None:
                    dve.wait_ge(u_hi_ready, KD * k + c + 1)
                    dve.scalar_tensor_tensor(u_lo[:, c, :], h[:, c, :], gain, u_hi[:, c, :].bitcast(F32),
                                             ALU.mult, ALU.subtract).then_inc(u_ready, 1)
                e = SQ[k] + c
                dve.wait_ge(sq_ready, e + 1)
                add_squares(ssum, e, c == 0)

            def add_squares(total, e, first):
                if first:
                    dve.tensor_copy(total[:, :], sq[:, e % 2, :]).then_inc(sq_added, 1)
                else:
                    dve.wait_ge(sq_added, e)
                    dve.tensor_tensor(total[:, :], total[:, :], sq[:, e % 2, :], ALU.add).then_inc(sq_added, 1)

            def inverse_root(dst, ms, scale, epsilon, x, root):
                link(dve.tensor_scalar(x, ms, scale, epsilon, ALU.mult, ALU.add))
                link(dve.reciprocal(root, root))
                link(dve.tensor_tensor(x, x, root, ALU.mult))
                link(dve.tensor_tensor(x, x, root, ALU.mult))
                link(dve.tensor_scalar(x, x, -0.5, 1.5, ALU.mult, ALU.add))
                return dve.tensor_tensor(dst, x, root, ALU.mult)

            def rstd_of_norm(roots, count):
                dve.wait_ge(root_ready, roots)
                inverse_root(rstd[:, :], aux[:, 0, :], 1.0 / D, NORM_EPS, sq[:, 0, :], sq[:, 1, :]).then_inc(rstd_ready, 1)
                dve.wait_ge(rstd_ready, count)

            def ffn_up(f, name):
                t0 = plan.first[name][1]
                with dve.Fori(0, KF // 2) as i:
                    for b in range(2):
                        dve.wait_ge(tile_done, i * 4 + (t0 + 2 * b + 1))
                        dve.tensor_tensor(gate_t[:, b, :], acc[:, (t0 + 2 * b) % BANKS, :], rstd[:, :], ALU.mult).then_inc(tile_freed, 1)
                        dve.wait_ge(tile_done, i * 4 + (t0 + 2 * b + 2))
                        dve.tensor_tensor(up_t[:, b, :], acc[:, (t0 + 2 * b + 1) % BANKS, :], rstd[:, :], ALU.mult).then_inc(tile_freed, 1)
                        dve.wait_ge(gate_act, i * 2 + (GATES_FFN[f] + b + 1))
                        dve.wait_ge(tile_freed, i * 4 + (t0 + 2 * b + 2))
                        dve.tensor_tensor(up_t[:, b, :], gate_t[:, b, :], up_t[:, b, :], ALU.mult).then_inc(prod_ready, 1)
                        dve.wait_ge(prod_hi, i * 2 + (f * KF + b + 1))
                        dve.tensor_tensor(hid_lo[:, i * 2 + b, :], up_t[:, b, :], hid_hi[:, i * 2 + b, :].bitcast(F32),
                                          ALU.subtract).then_inc(hid_ready, 1)

            def conv_up(f, name):
                t0 = plan.first[name][1]
                dve.memset(z_gate[:, 0:2], 0.0)
                dve.memset(z_up[:, 0:2], 0.0)

                def conv_col(name, i2, b, off):
                    return cols[:, bass.ds(i2 + (COL[name] + off + b), 1)]

                with dve.Fori(0, KF // 2) as i:
                    for b in range(2):
                        for part, z in enumerate((z_gate, z_up)):
                            c = 2 * b + part
                            dve.wait_ge(tile_done, i * 4 + (t0 + c + 1))
                            dve.tensor_tensor(z[:, 2:2 + S], acc[:, (t0 + c) % BANKS, :], rstd[:, :], ALU.mult).then_inc(tile_freed, 1)
                            dve.wait_ge(tile_freed, i * 4 + (t0 + c + 1))
                            dve.wait_ge(conv_set, i * 4 + (c + 1))
                            dve.scalar_tensor_tensor(tmp[:, part, :], z[:, 1:1 + S], conv_col("conv_w1", i * 2, b, part * KF),
                                                     tmp[:, part, :], ALU.mult, ALU.add).then_inc(conv_step, 1)
                            dve.wait_ge(conv_step, i * 4 + (c + 1))
                            dve.scalar_tensor_tensor(tmp[:, part, :], z[:, 0:S], conv_col("conv_w0", i * 2, b, part * KF),
                                                     tmp[:, part, :], ALU.mult, ALU.add).then_inc(conv_done, 1)
                        dve.wait_ge(gate_act, i * 2 + (GATES_FFN[f] + b + 1))
                        dve.wait_ge(conv_done, i * 4 + (2 * b + 2))
                        dve.tensor_tensor(tmp[:, 1, :], tmp[:, 0, :], tmp[:, 1, :], ALU.mult).then_inc(prod_ready, 1)
                        dve.wait_ge(prod_hi, i * 2 + (f * KF + b + 1))
                        dve.tensor_tensor(hid_lo[:, i * 2 + b, :], tmp[:, 1, :], hid_hi[:, i * 2 + b, :].bitcast(F32),
                                          ALU.subtract).then_inc(hid_ready, 1)

            def ffn_down(name, k, gain, half):
                t0 = plan.first[name][1]
                for m in range(KD):
                    dve.wait_ge(tile_done, t0 + m + 1)
                    dve.scalar_tensor_tensor(h[:, m, :], acc[:, (t0 + m) % BANKS, :], half, h[:, m, :],
                                             ALU.mult, ALU.add).then_inc(tile_freed, 1)
                    norm_chunk(k, m, gain(m))

            def lo_part(step, half, dst, src, hi):
                dve.wait_ge(split_hi, nth(split_steps, (step, half)) + 1)
                dve.tensor_tensor(dst, src, hi.bitcast(F32), ALU.subtract).then_inc(split_ready, 1)

            dve.wait_ge(vec_loaded, 32)
            for c in range(KD):
                norm_chunk(0, c, col("ffn1_norm", c))
            rstd_of_norm(1, 1)
            ffn_up(0, "up1")
            ffn_down("down1", 1, lambda m: col("mix_norm", m), 0.5)
            rstd_of_norm(2, 2)
            link(inverse_root(rstd_tok[:, :], aux[:, 1, 0:NT], 1.0 / D, NORM_EPS, small[:, 8:8 + NT], small[:, 0:NT]))

            dve.wait_ge(pos_loaded, 16)
            for i, (inv, quarter) in enumerate(((C_INV_A, 0.25), (C_INV_A, 0.0), (C_INV_R, 0.25), (C_INV_R, 0.0))):
                angle, turns_int, turns, r = tmp[:, 1, :], work[:, :].bitcast(I32), wts[:, 0:S], tmp[:, 2 + i % 2, :]
                link(dve.tensor_scalar(angle, tmp[:, 0, :].bitcast(I32), consts[:, inv:inv + 1], None, ALU.mult))
                link(dve.tensor_scalar(turns_int, angle, 1.0 / TWO_PI, quarter, ALU.mult, ALU.add))
                link(dve.tensor_copy(turns, turns_int))
                if i >= 2:
                    dve.wait_ge(table_ready, i - 1)
                link(dve.scalar_tensor_tensor(r, turns, -PI_A, angle, ALU.mult, ALU.add))
                link(dve.scalar_tensor_tensor(r, turns, -PI_B, r, ALU.mult, ALU.add))
                link(dve.scalar_tensor_tensor(r, turns, -PI_C, r, ALU.mult, ALU.add))
                link(dve.tensor_scalar(r, r, quarter * TWO_PI, PI_MAX, ALU.add, ALU.min))
                dve.tensor_scalar(r, r, -PI_MAX, None, ALU.max).then_inc(angle_ready, 1)
            dve.wait_ge(table_ready, 4)

            for step in MIX:
                kind = step[0]
                n, t = plan.first[step]
                bank = acc[:, t % BANKS, :]
                if kind in PROJECTS and kind != "attend":
                    dve.wait_ge(tile_done, t + 1)
                if kind == "avw":
                    link(dve.tensor_tensor(avt[:, :, :], bank[:, 0:NT * 72].rearrange("p (a b) -> p a b", a=NT),
                                           rstd_tok[:, :].unsqueeze(2).to_broadcast([P, NT, 72]), ALU.mult))
                    dve.tensor_scalar(avt[:, :, A_DIM:72], avt[:, :, A_DIM:72], A_HEADS ** -0.5, None, ALU.mult).then_inc(tile_freed, 1)
                elif kind == "rv":
                    v = rv[:, step[1] % 2, :, :]
                    for i in range(2):
                        dve.wait_ge(tile_done, t + i + 1)
                        part = v[:, 2 * i:2 * i + 2, :]
                        dve.tensor_tensor(part, acc[:, (t + i) % BANKS, :].rearrange("p (a b) -> p a b", a=2),
                                          rstd_tok[:, 2 * i:2 * i + 2].unsqueeze(2).to_broadcast([P, 2, R_V]), ALU.mult).then_inc(tile_freed, 1)
                        dve.wait_ge(tile_freed, t + i + 1)
                        link(dve.reduce_sum(small[:, 56:58], part, AX_X))
                        link(dve.tensor_scalar(small[:, 56:58], small[:, 56:58], -1.0 / R_V, None, ALU.mult))
                        dve.tensor_tensor(part, part, small[:, 56:58].unsqueeze(2).to_broadcast([P, 2, R_V]), ALU.add).then_inc(rv_ready, 1)
                elif kind in ("rg", "ga", "gb"):
                    buf = {"rg": lambda: srg[:, step[1] % 2, step[2], :], "ga": lambda: up_t[:, 0, :], "gb": lambda: up_t[:, 1, :]}[kind]()
                    dve.tensor_tensor(buf, bank, rstd[:, :], ALU.mult).then_inc(tile_freed, 1)
                elif kind in ROPE:
                    z = nth(rope_steps, step)
                    cos, sin = (cos_r, sin_r) if kind in ("rq", "rk") else (cos_a, sin_a)
                    dst = {"kk": lambda: wts[:, 0:S], "iq": lambda: q8[:, step[1], :], "aq": lambda: q8[:, step[1], :],
                           "rq": lambda: rqk[:, 0, :], "rk": lambda: rqk[:, 1, :]}[kind]()
                    x, y = gate_t[:, z % 2, :], up_t[:, z % 2, :]
                    dve.tensor_tensor(x, bank, rstd[:, :], ALU.mult).then_inc(tile_freed, 1)
                    dve.wait_ge(tile_freed, t + 1)
                    link(dve.tensor_tensor(dst, x, cos[:, :], ALU.mult))
                    dmas = sum(2 if s[0] in ("rq", "rk") else 4 for s in rope_steps[z % 2:z + 1:2])
                    dve.wait_ge(swapped[z % 2], 16 * dmas)
                    link(dve.tensor_tensor(y, y, sin[:, :], ALU.mult))
                    if kind == "kk":
                        dve.tensor_tensor(ikd[0:64, :], dst[0:64, :], y[0:64, :], ALU.add)
                        dve.tensor_tensor(akd[64:128, :], dst[64:128, :], y[64:128, :], ALU.add).then_inc(rope_ready, 1)
                    else:
                        dve.tensor_tensor(dst, dst, y, ALU.add).then_inc(rope_ready, 1)
                elif kind == "index":
                    b = step[1]
                    nk = (b + 1) * P
                    score = work[:, 0:nk]
                    for hd in range(A_HEADS):
                        j = index_units[b] + hd
                        w = avt[:, b, A_DIM + hd:A_DIM + hd + 1]
                        dve.wait_ge(idx_relu, j + 1)
                        if hd == 0:
                            dve.tensor_scalar(score, sq[:, j % 2, 0:nk], w, None, ALU.mult).then_inc(idx_added, 1)
                        else:
                            dve.wait_ge(idx_added, j)
                            dve.scalar_tensor_tensor(score, sq[:, j % 2, 0:nk], w, score, ALU.mult, ALU.add).then_inc(idx_added, 1)
                    dve.wait_ge(idx_added, index_units[b] + A_HEADS)
                    link(dve.memset(work[0:CHUNK, nk - CHUNK:nk], NEG_BIG))
                    for _ in range(TOPK // 8):
                        link(dve.max(top8, score))
                        link(dve.match_replace(score, top8, score, TAKEN))
                    link(dve.tensor_scalar(bias[:, bias_at[b]:bias_at[b] + nk], score, TAKEN, NEG_BIG, ALU.not_equal, ALU.mult))
                elif kind == "rscore":
                    r = step[1]
                    dve.wait_ge(dec_loaded, 16 * (r + 1))
                    for jt in range(NT):
                        nq = S - jt * P
                        dve.wait_ge(rs_done, NT * r + jt + 1)
                        dve.tensor_tensor(wts[:, wts_at[jt]:wts_at[jt] + nq], aux[:, 2 + jt % 2, 0:nq], dec[:, 0:nq], ALU.mult).then_inc(rw_ready, 1)
                elif kind == "rnorm":
                    r = step[1]
                    dve.wait_ge(ry_sq, 2 * r + 2)
                    dve.tensor_tensor(ssum[:, :], sq[:, 0, :], sq[:, 1, :], ALU.add).then_inc(ry_sum, 1)
                    dve.wait_ge(root_ready, 3 + r)
                    link(inverse_root(ssum[:, :], aux[:, 2, :], 1.0 / R_V, GN_EPS, sq[:, 0, :], sq[:, 1, :]))
                    for half in range(2):
                        dve.tensor_tensor(sq[:, half, :], aux[:, half, :], ssum[:, :], ALU.mult).then_inc(ry_freed, 1)
                        dve.wait_ge(ry_freed, 2 * r + half + 1)
                        dve.wait_ge(gate_act, gates_before(("rg", r, half)) + 1)
                        dve.scalar_tensor_tensor(sq[:, half, :], sq[:, half, :], col("ret_gn", 2 * r + half), srg[:, r % 2, half, :],
                                                 ALU.mult, ALU.mult).then_inc(split_in, 1)
                    for half in range(2):
                        lo_part(step, half, yr_lo[:, 2 * r + half, :], sq[:, half, :], yr_hi[:, 2 * r + half, :])
                elif kind == "logits":
                    b, i = step[1], nth(logit_steps, step)
                    nk = (b + 1) * P
                    if b == 0:
                        link(dve.memset(bias[:, 0:P], 0.0))
                        link(dve.memset(bias[0:CHUNK, CHUNK:P], NEG_BIG))
                    at = 8 * (i % 2)
                    for hd in range(A_HEADS):
                        j = A_HEADS * i + hd
                        dve.wait_ge(lg_done, j + 1)
                        dve.tensor_tensor_reduce(out=probs_of(b, hd), in0=aux[:, j % 2, 0:nk], in1=bias[:, bias_at[b]:bias_at[b] + nk],
                                                 scale=A_DIM ** -0.5, scalar=TAKEN, op0=ALU.add, op1=ALU.max,
                                                 accum_out=row_max[:, at + hd:at + hd + 1]).then_inc(lg_read, 1)
                    dve.wait_ge(lg_read, A_HEADS * (i + 1))
                    dve.tensor_scalar(neg_max[:, at:at + 8], row_max[:, at:at + 8], -1.0, None, ALU.mult).then_inc(neg_ready, 1)
                elif kind == "attend":
                    b = step[1]
                    i = nth(logit_steps, ("logits", b))
                    at = 8 * (i % 2)
                    dve.wait_ge(exp_done, A_HEADS * (i + 1))
                    link(dve.reciprocal(row_inv[:, at:at + 8], row_sum[:, at:at + 8]))
                    for hd in range(A_HEADS):
                        dve.tensor_scalar(probs_of(b, hd), probs_of(b, hd), row_inv[:, at + hd:at + hd + 1], None, ALU.mult).then_inc(p_ready, 1)
                    dve.wait_ge(tile_done, t + 1)
                    dve.tensor_copy(tmp[:, 0, :], bank).then_inc(tile_freed, 1)
                    dve.wait_ge(tile_freed, t + 1)
                    lo_part(step, 0, ya_lo[:, :, blk(b)], tmp[:, 0, :].rearrange("p (c q) -> p c q", c=4), ya_hi[:, :, blk(b)])
                elif kind == "wa":
                    if step[1]:
                        dve.wait_ge(split_ready, nth(split_steps, (("wb", step[1] - 1), 0)) + 1)
                    for i in range(2):
                        dve.wait_ge(tile_done, t + i + 1)
                        dve.tensor_copy(gate_t[:, i, :], acc[:, (t + i) % BANKS, :]).then_inc(tile_freed, 1)
                elif kind == "wb":
                    m = step[1]
                    x = gate_t[:, m % 2, :]
                    dve.wait_ge(gate_act, gates_before(("gb", m)) + 1)
                    dve.tensor_tensor(sq[:, 0, :], bank, up_t[:, 1, :], ALU.mult).then_inc(tile_freed, 1)
                    link(dve.tensor_tensor(x, x, up_t[:, 0, :], ALU.mult))
                    dve.wait_ge(tile_freed, t + 1)
                    dve.tensor_tensor(x, x, sq[:, 0, :], ALU.add).then_inc(split_in, 1)
                    lo_part(step, 0, mg_lo[:, m, :], x, mg_hi[:, m, :])
                elif kind == "wout":
                    m = step[1]
                    dve.tensor_tensor(h[:, m, :], bank, h[:, m, :], ALU.add).then_inc(tile_freed, 1)
                    norm_chunk(2, m, col("ffn2_norm", m))
            rstd_of_norm(7, 3)
            ffn_up(1, "up2")
            ffn_down("down2", 3, lambda m: col("ple_norm", m), 0.5)
            link(dve.tensor_tensor(small[:, 48:48 + KD], cols[:, COL["final_norm"]:COL["final_norm"] + KD],
                                   cols[:, COL["l0_norm1"]:COL["l0_norm1"] + KD], ALU.mult))
            rstd_of_norm(8, 4)
            for c in range(2):
                dve.wait_ge(p_split, c + 1)
                dve.tensor_tensor(p_lo[:, c, :], p_raw[:, c, :], p_hi[:, c, :].bitcast(F32), ALU.subtract).then_inc(hid_ready, 1)

            def ple_add(m):
                dve.wait_ge(gate_act, gates_before(("pgate", m)) + 1)
                link(dve.tensor_tensor(gate_t[:, m % 2, :], gate_t[:, m % 2, :], proj[:, m, :], ALU.mult))
                dve.tensor_tensor(h[:, m, :], h[:, m, :], gate_t[:, m % 2, :], ALU.add).then_inc(h_updated, 1)
                for e, total in ((0, ssum), (1, ssum2)):
                    dve.wait_ge(sq_ready, SQ[4] + 2 * m + e + 1)
                    add_squares(total, SQ[4] + 2 * m + e, m == 0)

            for step in PLE_STEPS:
                n, t = plan.first[step]
                dve.wait_ge(tile_done, t + 1)
                if step[0] == "pgate":
                    m = step[1]
                    dve.tensor_tensor(gate_t[:, m % 2, :], acc[:, t % BANKS, :], rstd[:, :], ALU.mult).then_inc(tile_freed, 1)
                    if m >= 2:
                        ple_add(m)
                else:
                    for i in range(4):
                        dve.wait_ge(tile_done, t + i + 1)
                        dve.tensor_copy(proj[:, 4 * step[1] + i, :], acc[:, (t + i) % BANKS, :]).then_inc(tile_freed, 1)
                    if step[1] == 1:
                        dve.wait_ge(tile_freed, t + 4)
                        ple_add(0)
                        ple_add(1)
            for m in range(KD):
                dve.wait_ge(u_hi_ready, KD * 4 + m + 1)
                dve.scalar_tensor_tensor(u_lo[:, m, :], h[:, m, :], small[:, 48 + m:49 + m], u_hi[:, m, :].bitcast(F32),
                                         ALU.mult, ALU.subtract).then_inc(u_ready, 1)

            dve.wait_ge(root_ready, 9)
            link(inverse_root(gres[:, :], aux[:, 0, :], 1.0 / D, NORM_EPS, sq[:, 0, :], sq[:, 1, :]))
            link(inverse_root(small[:, 160:160 + NT], aux[:, 2, 0:NT], 1.0 / D, NORM_EPS, small[:, 8:8 + NT], small[:, 0:NT]))
            link(dve.tensor_tensor(up_t[:, 0, :], gres[:, :], gres[:, :], ALU.mult))
            link(dve.tensor_tensor(up_t[:, 0, :], aux[:, 1, :], up_t[:, 0, :], ALU.mult))
            link(dve.tensor_tensor(small[:, 12:12 + NT], small[:, 160:160 + NT], small[:, 160:160 + NT], ALU.mult))
            dve.tensor_tensor(small[:, 12:12 + NT], aux[:, 2, NT:2 * NT], small[:, 12:12 + NT], ALU.mult).then_inc(ms2_ready, 1)
            dve.wait_ge(root_ready, 10)
            link(inverse_root(rstd[:, :], up_t[:, 0, :], 1.0 / D, NORM_EPS, sq[:, 0, :], up_t[:, 1, :]))
            link(inverse_root(rstd_tok[:, :], small[:, 12:12 + NT], 1.0 / D, NORM_EPS, small[:, 8:8 + NT], small[:, 4:4 + NT]))
            link(dve.tensor_tensor(rstd_tok[:, :], rstd_tok[:, :], small[:, 160:160 + NT], ALU.mult))
            dve.tensor_tensor(rstd[:, :], rstd[:, :], gres[:, :], ALU.mult).then_inc(rstd_ready, 1)
            dve.wait_ge(rstd_ready, 5)
            def residual(c):
                dve.scalar_tensor_tensor(h[:, c, :], h[:, c, :], col("final_norm", c), gres[:, :], ALU.mult, ALU.mult)
            keep = ssum
            link(dve.memset(keep[:, :], 1.0))
            link(dve.memset(keep[:, 0:S:CHUNK], 0.0))
            dve.memset(gsc[:, :, :], 0.0)

            for step in GLA:
                kind = step[0]
                n, t = plan.first[step]
                bank = acc[:, t % BANKS, :]
                if kind in PROJECTS:
                    dve.wait_ge(tile_done, t + 1)
                if kind == "alow":
                    dve.tensor_tensor(alow_t[0:G_RANK, :], bank[0:G_RANK, :], rstd[0:G_RANK, :], ALU.mult).then_inc(tile_freed, 1)
                elif kind == "alpha":
                    def log_alpha(c):
                        dve.wait_ge(al_ln, 3 * c + 3)
                        link(dve.scalar_tensor_tensor(gcum[:, c, :], gcum[:, c, :], 0.0, gate_t[:, c % 2, :], ALU.min, ALU.subtract))
                        link(dve.tensor_scalar(up_t[:, c % 2, :], gcum[:, c, :], 1.0 / G_TAU, None, ALU.mult))
                        dve.tensor_tensor_scan(gcum[:, c, :], keep[:, :], up_t[:, c % 2, :], 0.0, ALU.mult, ALU.add).then_inc(al_ready, 1)
                    for c in range(G_HEADS):
                        dve.wait_ge(tile_done, t + c + 1)
                        dve.tensor_scalar(gcum[:, c, :], acc[:, (t + c) % BANKS, :], col("b_alpha", c), None, ALU.add).then_inc(tile_freed, 1)
                    for c in range(G_HEADS):
                        log_alpha(c)
                    for c in range(KD):
                        residual(c)
                elif kind in ("gk", "gq"):
                    dve.tensor_tensor(gkq[:, 1 if kind == "gq" else 0, :], bank, rstd[:, :], ALU.mult).then_inc(tile_freed, 1)
                elif kind == "gv":
                    for i in range(2):
                        dve.wait_ge(tile_done, t + i + 1)
                        dve.tensor_tensor(gvt[:, step[1] % 2, 2 * i:2 * i + 2, :], acc[:, (t + i) % BANKS, :].rearrange("p (a b) -> p a b", a=2),
                                          rstd_tok[:, 2 * i:2 * i + 2].unsqueeze(2).to_broadcast([P, 2, G_DV]), ALU.mult).then_inc(tile_freed, 1)
                elif kind == "gstate":
                    r = step[1]
                    cum = gcum[:, r, :].rearrange("p (n c) -> p n c", c=CHUNK)
                    dve.wait_ge(al_ready, G_HEADS)
                    dve.tensor_tensor(up_t[:, 0, :].rearrange("p (n c) -> p n c", c=CHUNK), cum[:, :, CHUNK - 1:CHUNK].to_broadcast([P, S // CHUNK, CHUNK]),
                                      cum, ALU.subtract).then_inc(gd_ready, 1)
                    dve.wait_ge(tile_freed, plan.first[("gq", r)][1] + 1)
                    dve.wait_ge(ge_ready, 3 * r + 2)
                    dve.scalar_tensor_tensor(gqd[:, :], gkq[:, 1, :], G_DK ** -0.5, gate_t[:, 0, :], ALU.mult, ALU.mult)
                    dve.tensor_tensor(gki[:, :], gkq[:, 0, :], gate_t[:, 1, :], ALU.mult)
                    dve.wait_ge(ge_ready, 3 * r + 3)
                    dve.tensor_tensor(up_t[:, 1, :], gkq[:, 0, :], up_t[:, 0, :], ALU.mult).then_inc(gqk_ready, 1)
                    dve.wait_ge(gs_done, r + 1)
                    for e in range(2):
                        rows = slice(e * CHUNK, (e + 1) * CHUNK)
                        ins = dve.tensor_tensor(gsc[rows, :, rows], aux[rows, 2, 0:NT * CHUNK].rearrange("p (a b) -> p a b", a=NT),
                                                consts[rows, C_MASK:C_MASK + CHUNK].unsqueeze(1).to_broadcast([CHUNK, NT, CHUNK]), ALU.mult)
                    ins.then_inc(gsc_ready, 1)
                    for n in range(7):
                        kv = state_bank(n)
                        dve.wait_ge(gkv_done, 7 * r + (4 if n < 4 else 7))
                        if n == 0:
                            dve.tensor_copy(gst[:, 0, :], kv).then_inc(gst_ready, 1)
                        else:
                            end = n * CHUNK + CHUNK - 1
                            dve.wait_ge(gst_ready, 7 * r + n)
                            dve.scalar_tensor_tensor(gst[:, n, :], gst[:, n - 1, :], gate_t[:, 0, end:end + 1], kv, ALU.mult, ALU.add).then_inc(gst_ready, 1)
                elif kind == "gout":
                    r = step[1]
                    for i in range(2):
                        dve.wait_ge(tile_done, t + i + 1)
                        dve.tensor_copy(go[:, r, 2 * i:2 * i + 2, :], acc[:, (t + i) % BANKS, :].rearrange("p (a b) -> p a b", a=2)).then_inc(tile_freed, 1)
                    if r == G_HEADS - 1:
                        dve.wait_ge(root_ready, 11)
                        link(inverse_root(head_rstd, head_sq, 1.0 / G_DV, NORM_EPS, head_x, head_root))
                        for r in range(G_HEADS):
                            for tt in range(NT):
                                ins = dve.tensor_scalar(go[:, r, tt, :], go[:, r, tt, :], head_rstd[:, NT * r + tt:NT * r + tt + 1], None, ALU.mult)
                            ins.then_inc(gon_ready, 1)
                elif kind == "gr":
                    if step[1] == 0:
                        dve.wait_ge(gst_ready, 7 * G_HEADS)
                    dve.tensor_tensor(gate_t[:, step[1] % 2, :], bank, rstd[:, :], ALU.mult).then_inc(tile_freed, 1)
                elif kind == "gt":
                    c = step[1]
                    dve.wait_ge(gt_done, c + 1)
                    dve.wait_ge(gate_act, gates_before(("gr", c)) + 1)
                    dve.scalar_tensor_tensor(up_t[:, c % 2, :], aux[:, 2 + c % 2, :], col("gla_out_norm", c), gate_t[:, c % 2, :],
                                             ALU.mult, ALU.mult).then_inc(split_in, 1)
                    lo_part(step, 0, gy_lo[:, c, :], up_t[:, c % 2, :], gy_hi[:, c, :])
                elif kind == "gwout":
                    m = step[1]
                    dve.tensor_tensor(h[:, m, :], bank, h[:, m, :], ALU.add).then_inc(tile_freed, 1)
                    norm_chunk(5, m, col("l0_norm2", m))
            rstd_of_norm(12, 6)
            conv_up(2, "up3")
            ffn_down("down3", 6, lambda m: None, 1.0)
            rstd_of_norm(13, 7)
            for c in range(KD):
                dve.scalar_tensor_tensor(h[:, c, :], h[:, c, :], col("final_norm_2", c), rstd[:, :], ALU.mult, ALU.mult).then_inc(out_ready, 1)

        @block.tensor
        def _(pe):
            free_when = {}

            def claim(bank):
                if bank in free_when:
                    pe.wait_ge(*free_when[bank])

            def slabs_ready(n):
                pe.wait_ge(lo_ready, n + 1)

            def free_bank(t):
                if t >= BANKS:
                    pe.wait_ge(tile_freed, t - BANKS + 1)
                return acc[:, t % BANKS, :]

            def mm3(o, w, x_hi, x_lo, first, last):
                slot, columns = w
                pe.matmul(o, w_lo[:, slot, columns], x_hi, start=first, stop=False)
                pe.matmul(o, w_hi[:, slot, columns], x_lo, start=False, stop=False)
                return pe.matmul(o, w_hi[:, slot, columns], x_hi, start=False, stop=last)

            def sums(k, second=False):
                pe.wait_ge(sq_added, SQ[k + 1])
                claim(0)
                last = pe.matmul(aux[:, 0, :], ones[:, :], ssum[:, :], start=True, stop=True)
                if k == 4:
                    claim(1)
                    pe.matmul(aux[:, 1, :], ones[:, :], ssum2[:, :], start=True, stop=True)
                if k in (1, 4):
                    claim(1 if k == 1 else 2)
                    for i, total in enumerate((ssum, ssum2) if k == 4 else (ssum,)):
                        for tt in range(NT):
                            last = pe.matmul(aux[:, 1 if k == 1 else 2, i * NT + tt:i * NT + tt + 1], total[:, blk(tt)], ones[:, 0:1], start=True, stop=True)
                last.then_inc(stat_done, 1)
                for bank in range(3):
                    free_when[bank] = (rstd_ready, k + 1)

            def fm_tile(t, blocks, x_hi, x_lo, ready=None):
                o = free_bank(t)
                seen = None
                for k, (n, b) in enumerate(blocks):
                    if n != seen:
                        slabs_ready(n)
                        seen = n
                    if ready is not None:
                        pe.wait_ge(*ready(k))
                    last = mm3(o, (n % RING, blk(b)), x_hi[:, k, :], x_lo[:, k, :], k == 0, k == len(blocks) - 1)
                last.then_inc(tile_done, 1)

            def token_tiles(t, n, width, per_tile, per_slab):
                for i in range(NT // per_tile):
                    free_bank(t + i)
                    for tt in range(i * per_tile, (i + 1) * per_tile):
                        o = acc[:, (t + i) % BANKS, (tt % per_tile) * width:(tt % per_tile + 1) * width]
                        for k in range(KD):
                            slot = (n + k // per_slab) % RING
                            columns = slice((k % per_slab) * width, (k % per_slab + 1) * width)
                            slabs_ready(n + k // per_slab)
                            pe.matmul(o, u_lo[:, k, blk(tt)], w_hi[:, slot, columns], start=k == 0, stop=False)
                            pe.matmul(o, u_hi[:, k, blk(tt)], w_lo[:, slot, columns], start=False, stop=False)
                            last = pe.matmul(o, u_hi[:, k, blk(tt)], w_hi[:, slot, columns], start=False, stop=k == KD - 1)
                    last.then_inc(tile_done, 1)

            def ffn_up(k, name):
                n0, t0 = plan.first[name]
                for j in range(RING):
                    fm_tile(t0 + j, [(n0 + j, b) for b in range(KD)], u_hi, u_lo, (lambda c: (u_ready, KD * k + c + 1)) if j == 0 else None)
                    if j == 0:
                        sums({0: 0, 2: 2, 5: 5}[k])
                with pe.Fori(1, 2 * KF // RING) as i:
                    for j in range(RING):
                        pe.wait_ge(lo_ready, i * RING + (n0 + j + 1))
                        pe.wait_ge(tile_freed, i * RING + (t0 + j - BANKS + 1))
                        for b in range(KD):
                            last = mm3(acc[:, (t0 + j) % BANKS, :], ((n0 + j) % RING, blk(b)), u_hi[:, b, :], u_lo[:, b, :], b == 0, b == KD - 1)
                        last.then_inc(tile_done, 1)

            def ffn_down(f, name):
                n0, t0 = plan.first[name]
                with pe.Fori(0, 2) as i:
                    for m in range(4):
                        o = acc[:, (t0 + m) % BANKS, :]
                        pe.wait_ge(tile_freed, i * 4 + (t0 + m - BANKS + 1))
                        for k in range(KF):
                            j = DOWN_SLABS * m + k // 8
                            if k % 8 == 0:
                                pe.wait_ge(lo_ready, i * (4 * DOWN_SLABS) + (n0 + j + 1))
                            if k == KF - 1:
                                pe.wait_ge(hid_ready, HIDDEN[f])
                            last = mm3(o, ((n0 + j) % RING, blk(k % 8)), hid_hi[:, k, :], hid_lo[:, k, :], k == 0, k == KF - 1)
                            if k % 8 == 7:
                                last.then_inc(slab_used, 1)
                        last.then_inc(tile_done, 1)

            HIDDEN = [KF, 2 * KF, 3 * KF + 2]
            pe.wait_ge(consts_set, 3)
            ffn_up(0, "up1")
            ffn_down(0, "down1")

            for step in MIX:
                kind = step[0]
                n, t = plan.first[step]
                if kind == "avw":
                    pe.wait_ge(u_ready, KD * 2)
                    token_tiles(t, n, 72, NT, KD)
                    sums(1)
                elif kind == "rv":
                    token_tiles(t, n, R_V, 2, 4)
                elif kind in ("rg", "kk", "iq", "rq", "rk", "aq", "ga", "gb"):
                    fm_tile(t, [(n, b) for b in range(KD)], u_hi, u_lo)
                elif kind == "index":
                    b = step[1]
                    nk = (b + 1) * P
                    pe.wait_ge(rope_ready, nth(rope_steps, ("iq", 3)) + 1)
                    pe.wait_ge(keys_copied, 32)
                    for hd in range(A_HEADS):
                        j = index_units[b] + hd
                        rows = slice(64 * (hd % 2), 64 * (hd % 2) + 64)
                        claim(2 + j % 2)
                        pe.matmul(aux[:, 2 + j % 2, 0:nk], q8[rows, hd // 2, blk(b)], ikd[rows, 0:nk], start=True, stop=True).then_inc(idx_scored, 1)
                        free_when[2 + j % 2] = (idx_relu, j + 1)
                elif kind == "rscore":
                    r = step[1]
                    pe.wait_ge(rope_ready, nth(rope_steps, ("rk", r)) + 1)
                    for jt in range(NT):
                        nq = S - jt * P
                        claim(2 + jt % 2)
                        pe.matmul(aux[:, 2 + jt % 2, 0:nq], rqk[:, 1, blk(jt)], rqk[:, 0, jt * P:S], start=True, stop=True).then_inc(rs_done, 1)
                        free_when[2 + jt % 2] = (rw_ready, NT * r + jt + 1)
                elif kind == "ry":
                    r = step[1]
                    pe.wait_ge(rv_ready, 2 * r + 2)
                    claim(0)
                    claim(1)
                    for jt in range(NT):
                        pe.wait_ge(rw_ready, NT * r + jt + 1)
                        nq = S - jt * P
                        for half in range(2):
                            last = pe.matmul(aux[:, half, jt * P:S], rv[:, r % 2, jt, blk(half)], wts[:, wts_at[jt]:wts_at[jt] + nq],
                                             start=jt == 0, stop=jt == NT - 1)
                    last.then_inc(ry_done, 1)
                    free_when[0] = (ry_freed, 2 * r + 1)
                    free_when[1] = (ry_freed, 2 * r + 2)
                elif kind == "rnorm":
                    r = step[1]
                    pe.wait_ge(ry_sum, r + 1)
                    claim(2)
                    pe.matmul(aux[:, 2, :], ones[:, :], ssum[:, :], start=True, stop=True).then_inc(stat_done, 1)
                    free_when[2] = (ry_freed, 2 * r + 1)
                elif kind == "logits":
                    b, i = step[1], nth(logit_steps, step)
                    nk = (b + 1) * P
                    pe.wait_ge(rope_ready, len(rope_steps))
                    for hd in range(A_HEADS):
                        j = A_HEADS * i + hd
                        rows = slice(64 * (hd % 2), 64 * (hd % 2) + 64)
                        claim(j % 2)
                        pe.matmul(aux[:, j % 2, 0:nk], q8[rows, hd // 2, blk(b)], akd[rows, 0:nk], start=True, stop=True).then_inc(lg_done, 1)
                        free_when[j % 2] = (lg_read, j + 1)
                elif kind == "attend":
                    b = step[1]
                    base = pt_base[step]
                    groups = [(parity, kt) for parity in range(2) for kt in range(b + 1)]

                    def turn(g):
                        parity, kt = groups[g]
                        claim(2 + (base + g) % 2)
                        if parity == 0 and kt == 0:
                            pe.wait_ge(p_ready, A_HEADS * (nth(attend_steps, step) + 1))
                        for i in range(4):
                            last = pe.transpose(aux[:, 2 + (base + g) % 2, blk(i)], probs_of(b, 2 * i + parity)[:, blk(kt)], ident)
                        last.then_inc(pt_done, 1)
                        free_when[2 + (base + g) % 2] = (pt_ready, base + g + 1)

                    o = free_bank(t)
                    turn(0)
                    for g, (parity, kt) in enumerate(groups):
                        if g + 1 < len(groups):
                            turn(g + 1)
                        pe.wait_ge(pt_ready, base + g + 1)
                        last = pe.matmul(o[64 * parity:64 * parity + 64, :], avt[:, kt, 0:A_DIM], pt[:, (base + g) % 2, :],
                                         start=kt == 0, stop=kt == b)
                    last.then_inc(tile_done, 1)
                elif kind == "wa":
                    pe.wait_ge(split_ready, nth(split_steps, (("attend", 1), 0)) + 1)
                    for i in range(2):
                        fm_tile(t + i, [(n, 4 * i + b) for b in range(4)], ya_hi, ya_lo)
                elif kind == "wb":
                    fm_tile(t, [(n, b) for b in range(KD)], yr_hi, yr_lo)
                elif kind == "wout":
                    fm_tile(t, [(n, b) for b in range(KD)], mg_hi, mg_lo,
                            (lambda c: (split_ready, nth(split_steps, (("wb", c), 0)) + 1)) if step[1] == 0 else None)
            ffn_up(2, "up2")
            ffn_down(1, "down2")

            for step in PLE_STEPS:
                n, t = plan.first[step]
                if step[0] == "pgate":
                    fm_tile(t, [(n, b) for b in range(KD)], u_hi, u_lo, (lambda c: (u_ready, KD * 3 + c + 1)) if step[1] == 0 else None)
                    if step[1] == 0:
                        sums(3)
                else:
                    pe.wait_ge(hid_ready, 2 * KF + 2)
                    for i in range(4):
                        fm_tile(t + i, [(n, 2 * i), (n, 2 * i + 1)], p_hi, p_lo)

            for step in GLA:
                kind = step[0]
                n, t = plan.first[step]
                if kind == "alow":
                    o = free_bank(t)
                    slabs_ready(n)
                    for k in range(KD):
                        pe.wait_ge(u_ready, KD * 4 + k + 1)
                        last = mm3(o[0:G_RANK, :], (n % RING, slice(k * G_RANK, (k + 1) * G_RANK)), u_hi[:, k, :], u_lo[:, k, :], k == 0, k == KD - 1)
                    last.then_inc(tile_done, 1)
                    sums(4)
                elif kind == "alpha":
                    pe.wait_ge(tile_freed, plan.first[("alow",)][1] + 1)
                    pe.wait_ge(pt_loaded, 32)
                    for c in range(G_HEADS):
                        free_bank(t + c)
                        pe.matmul(acc[:, (t + c) % BANKS, :], walpha[0:G_RANK, blk(c)], alow_t[0:G_RANK, :], start=True, stop=True).then_inc(tile_done, 1)
                elif kind == "gv":
                    token_tiles(t, n, G_DV, 2, 4)
                elif kind in ("gk", "gq", "gr"):
                    fm_tile(t, [(n, b) for b in range(KD)], u_hi, u_lo)
                elif kind == "gstate":
                    r = step[1]
                    pe.wait_ge(gqk_ready, r + 1)
                    claim(3)
                    for tt in range(NT):
                        last = pe.transpose(aux[:, 3, blk(tt)], up_t[:, 1, blk(tt)], ident)
                    last.then_inc(gke_done, 1)
                    free_when[3] = (gke_ready, r + 1)
                    claim(2)
                    for tt in range(NT):
                        for e in range(2):
                            tok = slice(tt * P + e * CHUNK, tt * P + (e + 1) * CHUNK)
                            last = pe.matmul(aux[e * CHUNK:(e + 1) * CHUNK, 2, tt * CHUNK:(tt + 1) * CHUNK], gki[:, tok], gqd[:, tok], start=True, stop=True)
                    last.then_inc(gs_done, 1)
                    free_when[2] = (gsc_ready, r + 1)
                    pe.wait_ge(gke_ready, r + 1)
                    pe.wait_ge(tile_freed, plan.first[("gv", r)][1] + 2)
                    for c in range(7):
                        tt, rows = c // 2, slice((c % 2) * CHUNK, (c % 2 + 1) * CHUNK)
                        if c in (0, 1, 4, 5):
                            claim(c % 2)
                        pe.matmul(state_bank(c), gket[rows, tt, :], gvt[rows, r % 2, tt, :], start=True, stop=True).then_inc(gkv_done, 1)
                        free_when[c % 2] = (gst_ready, 7 * r + c + 1)
                elif kind == "gout":
                    r = step[1]
                    pe.wait_ge(gsc_ready, r + 1)
                    for tt in range(NT):
                        if tt % 2 == 0:
                            free_bank(t + tt // 2)
                        o = acc[:, (t + tt // 2) % BANKS, (tt % 2) * G_DV:(tt % 2 + 1) * G_DV]
                        last = pe.matmul(o, gsc[:, tt, :], gvt[:, r % 2, tt, :], start=True, stop=True)
                        for e in range(2):
                            c = 2 * tt + e
                            if c:
                                pe.wait_ge(gst_ready, 7 * r + c)
                                last = pe.matmul(o[e * CHUNK:(e + 1) * CHUNK, :], gqd[:, c * CHUNK:(c + 1) * CHUNK], gst[:, c - 1, :],
                                                 start=False, stop=True, skip_group_check=True)
                        if tt % 2:
                            last.then_inc(tile_done, 1)
                elif kind == "gt":
                    c = step[1]
                    pe.wait_ge(gon_ready, c // 2 + 1)
                    claim(2 + c % 2)
                    for tt in range(NT):
                        last = pe.transpose(aux[:, 2 + c % 2, blk(tt)], go[:, c // 2, tt, blk(c % 2)], ident)
                    last.then_inc(gt_done, 1)
                    free_when[2 + c % 2] = (split_in, nth(made_steps, (step, 0)) + 1)
                elif kind == "gwout":
                    fm_tile(t, [(n, b) for b in range(KD)], gy_hi, gy_lo,
                            (lambda c: (split_ready, nth(split_steps, (("gt", c), 0)) + 1)) if step[1] == 0 else None)
            ffn_up(5, "up3")
            ffn_down(2, "down3")
            sums(6)


def _blocks(w):
    k, m = w.shape
    return w.reshape(k // P, P, m // P, P).transpose(2, 1, 0, 3).reshape(m // P, P, k)


def _moving(w):
    k, m = w.shape
    return w.reshape(k // P, P, m).transpose(1, 0, 2).reshape(P, k // P * m)


def _pairs(a, b):
    return np.stack([_blocks(a), _blocks(b)], 1).reshape(-1, P, a.shape[0])


def _halves(w):
    return _moving(w).reshape(P, 2, SLAB).transpose(1, 0, 2)


def _shape_constants():
    consts = np.zeros((P, NCONST), np.float32)
    p = np.arange(P)
    consts[:, C_ID:C_ID + P] = np.eye(P)
    consts[:, C_MASK:C_MASK + CHUNK] = (p % CHUNK)[:, None] <= np.arange(CHUNK)[None, :]
    inv_a, inv_r = (10000.0 ** (-np.arange(n) / n) for n in (32, 64))
    consts[:, C_INV_A] = inv_a[p % 32]
    consts[:, C_INV_R] = inv_r[p % 64]
    consts[:, C_SGN_A] = np.where(p % 64 < 32, -1.0, 1.0)
    consts[:, C_SGN_R] = np.where(p < 64, -1.0, 1.0)
    log_gamma = np.log1p(-np.exp2(-5.0 - np.arange(R_HEADS)))
    i, j = np.arange(S)[None, :], p[:, None]
    seen = (i >= P) | (j < (i // CHUNK + 1) * CHUNK)
    decay = np.exp(log_gamma[:, None, None] * np.abs(i - j)) * seen * R_QK ** -0.5
    return consts, decay.astype(np.float32)


def kernel(**inputs):
    import concourse.bacc as bacc
    from concourse.bass_utils import run_bass_kernel_spmd as run

    a = {k: np.asarray(v) for k, v in inputs.items()}
    consts, decay = _shape_constants()
    w_in = a["w_in"][0]
    at, z = 0, {}
    for name, n in (("aq", 512), ("ak", 64), ("av", 64), ("iq", 512), ("ik", 64), ("iw", 8), ("rq", 512), ("rk", 512),
                    ("rv", 1024), ("rg", 1024), ("ga", 1024), ("gb", 1024)):
        z[name] = w_in[:, at:at + n]
        at += n
    z["kk"] = np.concatenate([z["ik"], z["ak"]], 1)
    tiles = {k: _blocks(z[k]) for k in ("aq", "iq", "rq", "rk", "rg", "ga", "gb", "kk")}
    tiles["wb"] = _blocks(a["w_branch_b"][0])
    tiles["wout"] = _blocks(a["w_out"][0])
    wa = _blocks(a["w_branch_a"][0])
    mix = []
    for step in MIX[1:]:
        kind = step[0]
        if kind == "rv":
            mix += list(_halves(z["rv"][:, step[1] * R_V:(step[1] + 1) * R_V]))
        elif kind == "rg":
            mix.append(tiles["rg"][2 * step[1] + step[2]])
        elif kind == "wa":
            mix.append(np.concatenate([wa[step[1]], wa[step[1] + 1]], 1))
        elif kind in tiles:
            mix.append(tiles[kind][step[1] if len(step) > 1 else 0])
    g_in = a["l0_gla_w_in_2"]
    gq, gk, gv, gr, glow = (g_in[:, i:j] for i, j in ((0, 512), (512, 1024), (1024, 2048), (2048, 3072), (3072, 3088)))
    gt = {"gq": _blocks(gq), "gk": _blocks(gk), "gr": _blocks(gr), "gwout": _blocks(a["l0_gla_w_out_2"])}
    gla = []
    for step in GLA[1:]:
        if step[0] == "gv":
            gla += list(_halves(gv[:, step[1] * G_DV:(step[1] + 1) * G_DV]))
        elif step[0] in gt:
            gla.append(gt[step[0]][step[1]])
    pgate = _blocks(a["w_ple_gate"][0])
    pproj = _blocks(a["w_ple_proj"][0]).transpose(1, 0, 2).reshape(P, 2, SLAB)
    ple = [pproj[:, s[1]] if s[0] == "pproj" else pgate[s[1]] for s in PLE_STEPS]
    up3 = a["l0_ffn_w_up_2"]

    def columns(v):
        return v.reshape(-1, P).T

    conv = a["l0_ffn_conv_w_2"]
    vectors = {"ffn1_norm": a["ffn1_norm"], "mix_norm": a["mix_norm"], "ret_gn": a["ret_gn"], "ffn2_norm": a["ffn2_norm"],
               "ple_norm": a["ple_norm"], "final_norm": a["final_norm"], "l0_norm1": a["l0_norm1_2"],
               "gla_out_norm": a["l0_gla_out_norm_2"], "l0_norm2": a["l0_norm2_2"], "final_norm_2": a["final_norm_2"],
               "b_alpha": a["l0_gla_b_alpha_2"], "conv_w0": conv[0], "conv_w1": conv[1], "conv_w2": conv[2],
               "conv_b": a["l0_ffn_conv_b_2"]}
    arrays = {
        "xT": a["x"][0].T.reshape(KD, P, S),
        "pT": a["p"][0, 0].T.reshape(2, P, S).transpose(1, 0, 2),
        "positions": np.broadcast_to(a["positions"], (P, S)),
        "vectors": np.concatenate([columns(vectors[name]) for name, _ in VECTORS], 1),
        "consts": consts,
        "decay": decay,
        "w_up1": _pairs(a["ffn1_w_gate"][0], a["ffn1_w_up"][0]),
        "w_down1": _blocks(a["ffn1_w_down"][0]),
        "w_avw": _moving(np.concatenate([z["av"], z["iw"]], 1)),
        "w_mix": np.stack(mix),
        "w_up2": _pairs(a["ffn2_w_gate"][0], a["ffn2_w_up"][0]),
        "w_down2": _blocks(a["ffn2_w_down"][0]),
        "w_ple": np.stack(ple),
        "w_alow": _moving(glow),
        "w_alpha": a["l0_gla_w_alpha_up_2"],
        "w_gla": np.stack(gla),
        "w_up3": _pairs(up3[:, :FF], up3[:, FF:]),
        "w_down3": _blocks(a["l0_ffn_w_down_2"]),
    }
    nc = bacc.Bacc("TRN2", target_bir_lowering=False, num_devices=1)
    feeds, A = {}, {}
    for name, v in arrays.items():
        v = np.ascontiguousarray(v)
        feeds[f"in_{name}"] = v
        A[name] = nc.dram_tensor(f"in_{name}", v.shape, mybir.dt.from_np(v.dtype), kind="ExternalInput").ap()
    out = nc.dram_tensor("out_xT", (KD, P, S), F32, kind="ExternalOutput").ap()
    layer_program(nc, A, out)
    r = run(nc, [feeds], core_ids=[0])
    return r.results[0]["out_xT"].reshape(D, S).T.reshape(1, S, D)
```

```python
from contextlib import ExitStack

import numpy as np
import concourse.bass as bass
from concourse import mybir

F32 = mybir.dt.float32
F32R = mybir.dt.float32r
I32 = mybir.dt.int32
ALU = mybir.AluOpType
ACT = mybir.ActivationFunctionType
AX_X = mybir.AxisListType.X

P = 128
S = 512
NT = S // P
D = 1024
KD = D // P
FF = 2816
KF = FF // P
CHUNK = 64
TOPK = min(256, S // 4)
TOPK_STEPS = 8
A_HEADS, A_DIM = 8, 64
R_HEADS, R_QK, R_V = 4, 128, 256
G_HEADS, G_DK, G_DV, G_RANK, G_TAU = 4, 128, 256, 16, 16.0
PLE = 256
NORM_EPS, GN_EPS = 1e-6, 1e-5
NEG_BIG = -1e30
TAKEN = -3.0e38

RING = 4
BANKS = 4
SLAB = 8 * P
DOWN_SLABS = 3
DOWN_LAST = (KF - 2 * 8) * P

TWO_PI = 2.0 * np.pi
PI_A = 6.28125
PI_B = float(np.float32(np.floor((TWO_PI - PI_A) * 2 ** 21) / 2 ** 21))
PI_C = float(np.float32(TWO_PI - PI_A - PI_B))
PI_MAX = 3.1415925

VECTORS = [("ffn1_norm", KD), ("mix_norm", KD), ("ret_gn", KD), ("ffn2_norm", KD), ("ple_norm", KD),
           ("final_norm", KD), ("l0_norm1", KD), ("gla_out_norm", KD), ("l0_norm2", KD), ("final_norm_2", KD),
           ("b_alpha", 4), ("conv_w0", 2 * KF), ("conv_w1", 2 * KF), ("conv_w2", 2 * KF), ("conv_b", 2 * KF)]
COL = {name: sum(n for _, n in VECTORS[:i]) for i, (name, _) in enumerate(VECTORS)}
NCOLS = sum(n for _, n in VECTORS)
C_ID, C_MASK, C_INV_A, C_INV_R, C_SGN_A, C_SGN_R, NCONST = 0, P, P + CHUNK, P + CHUNK + 1, P + CHUNK + 2, P + CHUNK + 3, P + CHUNK + 4

MIX = [("rg", 0, 0), ("avw",), ("kk",), ("iq", 0), ("rot", "kk"), ("iq", 1), ("rot", "iq", 0), ("iq", 2),
       ("rot", "iq", 1), ("iq", 3), ("rot", "iq", 2),
       ("rg", 0, 1), ("rot", "iq", 3),
       ("rq", 0),
       ("rk", 0), ("index", 3, 0), ("rot", "rq", 0),
       ("rv", 0), ("index", 3, 1), ("index", 3, 2), ("rot", "rk", 0),
       ("rg", 1, 0), ("index", 3, 3),
       ("rg", 1, 1), ("rscore", 0), ("index", 2, 0), ("topk", 3, 0),
       ("rq", 1), ("ry", 0), ("rsq", 0), ("index", 2, 1), ("topk", 3, 1),
       ("rk", 1), ("rsum", 0), ("rot", "rq", 1), ("topk", 3, 2),
       ("rv", 1), ("rfin", 0), ("topk", 3, 3), ("rot", "rk", 1),
       ("rg", 2, 0), ("rlo", 0), ("index", 2, 2), ("topk", 3, 4),
       ("rg", 2, 1), ("rscore", 1), ("index", 2, 3), ("topk", 3, 5),
       ("rq", 2), ("ry", 1), ("rsq", 1), ("index", 1, 0), ("topk", 3, 6),
       ("rk", 2), ("rsum", 1), ("rot", "rq", 2), ("topk", 3, 7),
       ("rv", 2), ("rfin", 1), ("topk", 2, 0), ("rot", "rk", 2),
       ("rg", 3, 0), ("rlo", 1), ("index", 1, 1), ("index", 1, 2), ("topk", 2, 1),
       ("rq", 3), ("rscore", 2), ("index", 1, 3), ("topk", 2, 2),
       ("rk", 3), ("ry", 2), ("rsq", 2), ("topk", 2, 3), ("rot", "rq", 3),
       ("aq", 0), ("rsum", 2), ("topk", 2, 4), ("rot", "rk", 3),
       ("aq", 1), ("rfin", 2), ("rot", "aq", 0),
       ("aq", 2), ("rlo", 2), ("rot", "aq", 1), ("topk", 2, 5),
       ("aq", 3), ("rscore", 3), ("rot", "aq", 2), ("topk", 2, 6),
       ("rv", 3), ("rot", "aq", 3), ("topk", 2, 7), ("topk", 1, 0),
       ("rg", 3, 1), ("ry", 3), ("rsq", 3), ("topk", 1, 1),
       ("logits", 3), ("rsum", 3), ("topk", 1, 2),
       ("ga", 0), ("rfin", 3), ("logits", 0),
       ("gb", 0), ("rlo", 3), ("attend", 3), ("topk", 1, 3), ("topk", 1, 4),
       ("logits", 2), ("wb", 0), ("topk", 1, 5), ("attend", 0), ("topk", 1, 6), ("topk", 1, 7),
       ("logits", 1), ("attend", 2), ("attend", 1), ("wa", 0), ("mg", 0)]
for _m in range(1, KD):
    MIX += [("ga", _m), ("gb", _m), ("wb", _m)] + ([("wa", _m)] if _m % 2 == 0 else []) + [("mg", _m)]
MIX += [("wout", m) for m in range(KD)]

PLE_STEPS = [("pgate", 0), ("pgate", 1), ("pproj", 0), ("pproj", 1)] + [("pgate", m) for m in range(2, KD)]

GLA = [("alow",), ("gv", 0), ("alpha",), ("gk", 0), ("cum",), ("gq", 0), ("gpre", 0)]
for _r in range(1, G_HEADS):
    GLA += [("gv", _r), ("gsc", _r - 1), ("res", _r - 1), ("gk", _r), ("gkv", _r - 1), ("gq", _r), ("gout", _r - 1)]
    GLA += ([("gn", _r - 2)] if _r > 1 else []) + [("gpre", _r)]
GLA += [("gr", 0), ("gr", 1), ("gsc", 3), ("gt", 0), ("gr", 2), ("gkv", 3), ("gt", 1), ("gr", 3), ("gout", 3), ("gn", 2),
        ("gt", 2), ("gr", 4), ("res", 3), ("gt", 3), ("gn", 3), ("gr", 5), ("gt", 4), ("gr", 6), ("gt", 5), ("gr", 7),
        ("gt", 6), ("gt", 7)]
GLA += [("gwout", m) for m in range(KD)]

PROJECTS = {"avw": (1, 1), "rv": (2, 2), "rg": (1, 1), "kk": (1, 1), "iq": (1, 1), "rq": (1, 1), "rk": (1, 1),
            "aq": (1, 1), "attend": (0, 1), "wa": (1, 2), "ga": (1, 1), "gb": (1, 1), "wb": (1, 1), "wout": (1, 1),
            "pgate": (1, 1), "pproj": (1, 4), "alow": (1, 1), "alpha": (0, 4), "gk": (1, 1), "gq": (1, 1),
            "gv": (2, 2), "gr": (1, 1), "gout": (0, 2), "gwout": (1, 1)}
ROPE = ("kk", "iq", "aq", "rq", "rk")


class Plan:

    def __init__(self):
        self.slabs = self.tiles = self.mids = 0
        self.release = []
        self.width = []
        self.first = {}

    def up(self, name):
        self.first[name] = (self.slabs, self.tiles)
        for _ in range(2 * KF):
            self.tiles += 1
            self.release.append(("tile", self.tiles))
            self.width.append(SLAB)
        self.slabs += 2 * KF

    def down(self, name):
        self.first[name] = (self.slabs, self.tiles)
        for _ in range(KD):
            self.tiles += 1
            for s in range(DOWN_SLABS - 1):
                self.mids += 1
                self.release.append(("mid", self.mids))
                self.width.append(SLAB)
            self.release.append(("tile", self.tiles))
            self.width.append(DOWN_LAST)
        self.slabs += KD * DOWN_SLABS

    def steps(self, name, steps):
        self.first[name] = (self.slabs, self.tiles)
        for step in steps:
            slabs, tiles = PROJECTS.get(step[0], (0, 0))
            self.first[step] = (self.slabs, self.tiles)
            self.tiles += tiles
            for _ in range(slabs):
                self.release.append(("tile", self.tiles))
                self.width.append({"avw": KD * 72, "alow": KD * G_RANK}.get(step[0], SLAB))
            self.slabs += slabs


def layer_program(nc, A, out):
    plan = Plan()
    plan.up("up1")
    plan.down("down1")
    plan.steps("mix", MIX)
    plan.up("up2")
    plan.down("down2")
    plan.steps("ple", PLE_STEPS)
    plan.steps("gla", GLA)
    plan.up("up3")
    plan.down("down3")
    N = plan.slabs

    with ExitStack() as ctx:
        def sb(name, shape, dt=F32, on=ctx):
            return on.enter_context(nc.sbuf_tensor(name, shape, dt))

        def sem(name):
            return ctx.enter_context(nc.semaphore(name))

        w_raw = sb("w_raw", [P, RING, SLAB])
        w_hi = sb("w_hi", [P, RING, SLAB], F32R)
        w_lo = sb("w_lo", [P, RING, SLAB], F32R)
        h = sb("h", [P, KD, S])
        u_hi = sb("u_hi", [P, KD, S], F32R)
        u_lo = sb("u_lo", [P, KD, S], F32R)
        tmp = sb("tmp", [P, 6, S])
        side = sb("side", [P, 2, S])
        ssum = sb("ssum", [P, S])
        rstd = sb("rstd", [P, S])
        ones = sb("ones", [P, P])
        cols = sb("cols", [P, NCOLS])
        consts = sb("consts", [P, NCONST])
        eps = sb("eps", [P, 2])
        rstd_tok = sb("rstd_tok", [P, NT])
        small = sb("small", [P, 176])
        gate_t, up_t, sq = tmp[:, 0:2, :], tmp[:, 2:4, :], tmp[:, 4:6, :]
        gres, ssum2 = side[:, 0, :], side[:, 1, :]
        pt = sq
        cos_a, sin_a = side[:, 0, :], side[:, 1, :]
        neg_max, row_sum, row_max, row_inv = (small[:, c:c + 16] for c in (16, 32, 64, 80))
        top8 = small[:, 168:176]
        head_sq, head_root, head_x, head_rstd = (small[:, c:c + 16] for c in (96, 112, 128, 144))
        ident = consts[:, C_ID:C_ID + P]

        with ExitStack() as region:
            hid_hi = sb("hid_hi", [P, KF, S], F32R, region)
            hid_lo = sb("hid_lo", [P, KF, S], F32R, region)
        with ExitStack() as region:
            yr_hi = sb("yr_hi", [P, KD, S], F32R, region)
            yr_lo = sb("yr_lo", [P, KD, S], F32R, region)
            with ExitStack() as inner:
                q8 = sb("q8", [P, 4, S], F32, inner)
                ikd = sb("ikd", [P, S], F32, inner)
                akd = sb("akd", [P, S], F32, inner)
                bias = sb("bias", [P, NT * (NT + 1) // 2 * P], F32, inner)
                avt = sb("avt", [P, NT, 72], F32, inner)
                with ExitStack() as sub:
                    cos_r = sb("cos_r", [P, S], F32, sub)
                    sin_r = sb("sin_r", [P, S], F32, sub)
                    rv = sb("rv", [P, 2, NT, R_V], F32, sub)
                    rqk = sb("rqk", [P, 2, S], F32, sub)
                    wts = sb("wts", [P, NT * (NT + 1) // 2 * P], F32, sub)
                    dec = sb("dec", [P, S], F32, sub)
                    srg = sb("srg", [P, 2, 2, S], F32, sub)
                    y_sq = sb("y_sq", [P, 2, S], F32, sub)
                with ExitStack() as sub:
                    probs = sb("probs", [P, 5 * 2 * S], F32, sub)
                    ya_hi = sb("ya_hi", [P, 4, S], F32R, sub)
                    ya_lo = sb("ya_lo", [P, 4, S], F32R, sub)
                    branch_b = sb("branch_b", [P, S], F32, sub)
            with ExitStack() as inner:
                mg_hi = sb("mg_hi", [P, KD, S], F32R, inner)
                mg_lo = sb("mg_lo", [P, KD, S], F32R, inner)
        with ExitStack() as region:
            gy_hi = sb("gy_hi", [P, KD, S], F32R, region)
            gy_lo = sb("gy_lo", [P, KD, S], F32R, region)
            gcum = sb("gcum", [P, G_HEADS, S], F32, region)
            with ExitStack() as inner:
                proj = sb("proj", [P, KD, S], F32, inner)
                p_raw = sb("p_raw", [P, 2, S], F32, inner)
                p_hi = sb("p_hi", [P, 2, S], F32R, inner)
                p_lo = sb("p_lo", [P, 2, S], F32R, inner)
            with ExitStack() as inner:
                gvt = sb("gvt", [P, 2, NT, G_DV], F32, inner)
                gkq = sb("gkq", [P, 2, S], F32, inner)
                gki = sb("gki", [P, S], F32, inner)
                gqd = sb("gqd", [P, S], F32, inner)
                gket = sb("gket", [P, NT, P], F32, inner)
                gsc = sb("gsc", [P, NT, P], F32, inner)
                gst = sb("gst", [P, 7, G_DV], F32, inner)
                go = sb("go", [P, G_HEADS, NT, G_DV], F32, inner)
                walpha = sb("walpha", [P, 4 * P], F32, inner)
                alow_t = sb("alow_t", [P, S], F32, inner)

        acc = ctx.enter_context(nc.psum_tensor("acc", [P, BANKS, S], F32))
        aux = ctx.enter_context(nc.psum_tensor("aux", [P, 4, S], F32))

        raw_loaded = [sem(f"raw_loaded{i}") for i in range(RING)]
        hi_ready = sem("hi_ready")
        lo_ready = sem("lo_ready")
        slab_used = sem("slab_used")
        tile_done = sem("tile_done")
        tile_freed = sem("tile_freed")
        x_loaded = [sem(f"x_loaded{i}") for i in range(KD)]
        vec_loaded = sem("vec_loaded")
        pos_loaded = sem("pos_loaded")
        consts_set = sem("consts_set")
        gate_act = sem("gate_act")
        prod_ready = sem("prod_ready")
        prod_hi = sem("prod_hi")
        hid_ready = sem("hid_ready")
        conv_set = sem("conv_set")
        conv_done = sem("conv_done")
        conv_step = sem("conv_step")
        u_hi_ready = sem("u_hi_ready")
        u_ready = sem("u_ready")
        sq_ready = sem("sq_ready")
        sq_added = sem("sq_added")
        stat_done = sem("stat_done")
        root_ready = sem("root_ready")
        rstd_ready = sem("rstd_ready")
        ms2_ready = sem("ms2_ready")
        dve_step = sem("dve_step")
        angle_ready = sem("angle_ready")
        table_ready = sem("table_ready")
        swapped = [sem("swapped0"), sem("swapped1")]
        rope_ready = sem("rope_ready")
        rotated = sem("rotated")
        keys_copied = sem("keys_copied")
        dec_loaded = sem("dec_loaded")
        idx_scored = sem("idx_scored")
        idx_relu = sem("idx_relu")
        idx_added = sem("idx_added")
        sel_ready = sem("sel_ready")
        rs_done = sem("rs_done")
        rw_ready = sem("rw_ready")
        rv_ready = sem("rv_ready")
        ry_done = sem("ry_done")
        ry_sq = sem("ry_sq")
        ry_sum = sem("ry_sum")
        ry_freed = sem("ry_freed")
        lg_done = sem("lg_done")
        lg_read = sem("lg_read")
        neg_ready = sem("neg_ready")
        exp_done = sem("exp_done")
        p_ready = sem("p_ready")
        pt_done = sem("pt_done")
        pt_ready = sem("pt_ready")
        split_in = sem("split_in")
        split_hi = sem("split_hi")
        split_ready = sem("split_ready")
        pt_loaded = sem("ple_loaded")
        h_updated = sem("h_updated")
        p_split = sem("p_split")
        gsc_ready = sem("gsc_ready")
        out_ready = sem("out_ready")
        al_ln = sem("al_ln")
        al_ready = sem("al_ready")
        ge_ready = sem("ge_ready")
        gd_ready = sem("gd_ready")
        gqk_ready = sem("gqk_ready")
        gke_done = sem("gke_done")
        gke_ready = sem("gke_ready")
        gs_done = sem("gs_done")
        gkv_done = sem("gkv_done")
        gst_ready = sem("gst_ready")
        gv_ready = sem("gv_ready")
        go_sq = sem("go_sq")
        gon_ready = sem("gon_ready")
        gt_done = sem("gt_done")
        out_stored = sem("out_stored")

        SQ = [0, 8, 16, 24, 32, 48, 56, 64]
        rope_steps = [s for s in MIX if s[0] in ROPE]
        gate_steps = [s for s in MIX + PLE_STEPS + GLA if s[0] in ("rg", "ga", "gb", "pgate", "gr")]
        split_steps = []
        for s in MIX:
            if s[0] == "rlo":
                split_steps += [(s, 0), (s, 1)]
            elif s[0] in ("attend", "mg"):
                split_steps += [(s, 0)]
        split_steps += [(("gt", c), 0) for c in range(KD)]
        made_steps = [s for s in split_steps if s[0][0] != "attend"]
        index_units = {b: A_HEADS * i for i, b in enumerate((3, 2, 1))}
        logit_steps = [s for s in MIX if s[0] == "logits"]
        attend_steps = [s for s in MIX if s[0] == "attend"]
        pt_base = {}
        for s in attend_steps:
            pt_base[s] = sum(2 * (t[1] + 1) for t in attend_steps[:attend_steps.index(s)])
        FFNS = 3

        def nth(steps, step):
            return steps.index(step)

        def splits_before(step):
            return sum(MIX.index(s) < MIX.index(step) for s, _ in split_steps if s in MIX)

        def gates_before(step):
            before = {"rg": 1, "ga": 1, "gb": 1, "pgate": 2, "gr": 2}[step[0]]
            return before * KF + nth(gate_steps, step)

        z_gate = tmp.rearrange("p a b -> p (a b)")[:, 2 * S:3 * S + 2]
        z_up = tmp.rearrange("p a b -> p (a b)")[:, 3 * S + 2:4 * S + 4]
        TABLES = [(C_INV_A, 0.25, cos_a, None), (C_INV_A, 0.0, sin_a, C_SGN_A),
                  (C_INV_R, 0.25, up_t[:, 0, :], None), (C_INV_R, 0.0, up_t[:, 1, :], C_SGN_R)]
        GATES_FFN = [0, KF + nth(gate_steps, ("pgate", 0)), 2 * KF + len(gate_steps)]
        bias_at = {0: 0, 1: P, 2: 3 * P, 3: 6 * P}
        wts_at = {0: 0, 1: 4 * P, 2: 7 * P, 3: 9 * P}
        probs_at = {3: 0, 0: 8 * S, 2: 0, 1: 6 * S}

        def probs_of(b, hd):
            n = (b + 1) * P
            return probs[:, probs_at[b] + hd * n:probs_at[b] + (hd + 1) * n]

        def state_bank(c):
            at = (c // 2) % 2 * G_DV
            return aux[:, c % 2, at:at + G_DV]

        def blk(b):
            return slice(b * P, (b + 1) * P)

        def load_count(n):
            return 16 * (n // RING + 1)

        block = ctx.enter_context(nc.Block())

        @block.sync
        def _(sp):
            def load(n, src):
                if n >= RING:
                    sp.wait_ge(lo_ready, n - RING + 1)
                sp.dma_start(w_raw[:, n % RING, 0:plan.width[n]], src).then_inc(raw_loaded[n % RING], 16)

            def load_up(name, w, first=0):
                n0 = plan.first[name][0]
                with sp.Fori(first // RING, 2 * KF // RING) as i:
                    for j in range(RING):
                        sp.wait_ge(lo_ready, i * RING + (n0 + j - RING + 1))
                        sp.dma_start(w_raw[:, (n0 + j) % RING, :], w[i * RING + j]).then_inc(raw_loaded[(n0 + j) % RING], 16)

            def load_down(name, w):
                n0 = plan.first[name][0]
                with sp.Fori(0, 2) as i:
                    for j in range(4 * DOWN_SLABS):
                        width, at = plan.width[n0 + j], (j % DOWN_SLABS) * SLAB
                        sp.wait_ge(lo_ready, i * (4 * DOWN_SLABS) + (n0 + j - RING + 1))
                        sp.dma_start(w_raw[:, (n0 + j) % RING, 0:width],
                                     w[i * 4 + j // DOWN_SLABS][:, at:at + width]).then_inc(raw_loaded[(n0 + j) % RING], 16)

            sp.dma_start(cols[:, :], A["vectors"]).then_inc(vec_loaded, 16)
            sp.dma_start(consts[:, :], A["consts"]).then_inc(vec_loaded, 16)
            for n in range(2):
                load(n, A["w_up1"][n])
            for c in range(KD):
                sp.dma_start(h[:, c, :], A["xT"][c]).then_inc(x_loaded[c], 16)
            for n in range(2, RING):
                load(n, A["w_up1"][n])
            load_up("up1", A["w_up1"], RING)
            load_down("down1", A["w_down1"])

            mix0, avw = plan.first["mix"][0], plan.first[("avw",)][0]
            mix_end = plan.first["up2"][0]
            loaded = [mix0]

            def load_mix(upto):
                while loaded[0] < min(upto, mix_end):
                    n = loaded[0]
                    load(n, A["w_avw"] if n == avw else A["w_mix"][n - mix0 - (n > avw)])
                    loaded[0] += 1
            load_mix(mix0 + 3)
            sp.wait_ge(tile_done, plan.first["mix"][1])
            sp.dma_start(dec[:, :], A["decay"][0]).then_inc(dec_loaded, 16)
            for step in MIX:
                n, t = plan.first[step]
                load_mix(n + 6)
                if step[0] in ROPE:
                    z = nth(rope_steps, step)
                    half = 64 if step[0] in ("rq", "rk") else 32
                    sp.wait_ge(tile_freed, t + 1)
                    for g in range(P // half):
                        to, of = g * half, (g ^ 1) * half
                        sp.dma_start(up_t[to:to + half, z % 2, :], gate_t[of:of + half, z % 2, :]).then_inc(swapped[z % 2], 16)
                if step == ("rot", "kk"):
                    sp.wait_ge(rope_ready, 1)
                    for rows in (slice(0, 64), slice(64, 128)):
                        sp.dma_start(ikd[rows, :], wts[0:64, 0:S]).then_inc(keys_copied, 16)
                        sp.dma_start(akd[rows, :], wts[64:128, 0:S]).then_inc(keys_copied, 16)
                if step[0] == "ry" and step[1] + 1 < R_HEADS:
                    sp.wait_ge(rw_ready, NT * (step[1] + 1))
                    sp.dma_start(dec[:, :], A["decay"][step[1] + 1]).then_inc(dec_loaded, 16)
            load_up("up2", A["w_up2"])
            load_down("down2", A["w_down2"])
            ple0 = plan.first["ple"][0]
            for n in range(ple0, ple0 + 4):
                load(n, A["w_ple"][n - ple0])
            sp.wait_ge(tile_done, plan.first["ple"][1])
            sp.dma_start(p_raw[:, :, :], A["pT"]).then_inc(pt_loaded, 16)
            for n in range(ple0 + 4, plan.first["gla"][0]):
                load(n, A["w_ple"][n - ple0])
            gla0 = plan.first["gla"][0]
            load(gla0, A["w_alow"])
            for n in range(gla0 + 1, gla0 + 3):
                load(n, A["w_gla"][n - gla0 - 1])
            sp.wait_ge(h_updated, KD)
            sp.dma_start(walpha[0:G_RANK, :], A["w_alpha"]).then_inc(pt_loaded, 16)
            for n in range(gla0 + 3, plan.first["up3"][0]):
                load(n, A["w_gla"][n - gla0 - 1])
            load_up("up3", A["w_up3"])
            load_down("down3", A["w_down3"])
            for c in range(KD):
                sp.wait_ge(out_ready, c + 1)
                sp.dma_start(out[c], h[:, c, :]).then_inc(out_stored, 16)
            sp.wait_ge(out_stored, 16 * KD)

        @block.gpsimd
        def _(pool):
            pool.memset(ones[:, :], 1.0).then_inc(consts_set, 1)
            pool.memset(eps[:, 0:1], NORM_EPS).then_inc(consts_set, 1)
            pool.memset(eps[:, 1:2], GN_EPS).then_inc(consts_set, 1)

            def lo_part(slot, width, count):
                pool.wait_ge(hi_ready, count)
                pool.tensor_tensor(w_lo[:, slot, 0:width], w_raw[:, slot, 0:width], w_hi[:, slot, 0:width].bitcast(F32),
                                   ALU.subtract).then_inc(lo_ready, 1)

            def lo_run(n0, n1):
                rounds = (n1 - n0) // RING
                if rounds:
                    with pool.Fori(0, rounds) as i:
                        for j in range(RING):
                            lo_part((n0 + j) % RING, SLAB, i * RING + (n0 + j + 1))
                for n in range(n0 + rounds * RING, n1):
                    lo_part(n % RING, SLAB, n + 1)

            def lo_down(n0):
                with pool.Fori(0, 2) as i:
                    for j in range(4 * DOWN_SLABS):
                        lo_part((n0 + j) % RING, plan.width[n0 + j], i * (4 * DOWN_SLABS) + (n0 + j + 1))

            def rotate(of):
                kind, z = of[0], nth(rope_steps, of)
                cos, sin = (cos_r[:, :], sin_r[:, :]) if kind in ("rq", "rk") else (cos_a, sin_a)
                dst = {"kk": lambda: wts[:, 0:S], "iq": lambda: q8[:, of[1], :], "aq": lambda: q8[:, of[1], :],
                       "rq": lambda: rqk[:, 0, :], "rk": lambda: rqk[:, 1, :]}[kind]()
                x, y = gate_t[:, z % 2, :], up_t[:, z % 2, :]
                pool.wait_ge(tile_freed, plan.first[of][1] + 1)
                if kind in ("rq", "rk") and of[1]:
                    pool.wait_ge(rs_done, NT * of[1])
                if kind == "aq":
                    pool.wait_ge(idx_scored, A_HEADS * len(index_units))
                pool.tensor_tensor(dst, x, cos, ALU.mult)
                pool.wait_ge(swapped[z % 2], 16 * sum(2 if s[0] in ("rq", "rk") else 4 for s in rope_steps[z % 2:z + 1:2]))
                pool.tensor_tensor(y, y, sin, ALU.mult).then_inc(rotated, 1)
                pool.wait_ge(rotated, z + 1)
                pool.tensor_tensor(dst, dst, y, ALU.add).then_inc(rope_ready, 1)

            def at(name):
                return plan.first[name][0]
            lo_run(0, at("down1"))
            lo_down(at("down1"))
            n = at("mix")
            for step in MIX:
                slabs = PROJECTS.get(step[0], (0, 0))[0]
                while n < plan.first[step][0] + slabs + RING and n < at("up2"):
                    lo_part(n % RING, plan.width[n], n + 1)
                    n += 1
                if step[0] == "rot":
                    rotate(step[1:])
            lo_run(at("up2"), at("down2"))
            lo_down(at("down2"))
            lo_run(at("ple"), at("gla"))
            lo_part(at("gla") % RING, plan.width[at("gla")], at("gla") + 1)
            lo_run(at("gla") + 1, at("down3"))
            lo_down(at("down3"))

        @block.scalar
        def _(act):
            done = [0]

            def hi_part(slot, width, count, used):
                act.wait_ge(raw_loaded[slot], count)
                if used is not None:
                    act.wait_ge(used[0], used[1])
                act.activation(w_hi[:, slot, 0:width], w_raw[:, slot, 0:width], ACT.Copy).then_inc(hi_ready, 1)

            def split_slabs(upto):
                while done[0] < min(upto, N):
                    n = done[0]
                    used = None
                    if n >= RING:
                        kind, count = plan.release[n - RING]
                        used = (tile_done if kind == "tile" else slab_used, count)
                    hi_part(n % RING, plan.width[n], load_count(n), used)
                    done[0] += 1

            def norm_chunk(k, c, gain, tile=None):
                if tile is not None:
                    act.wait_ge(tile_freed, tile + 1)
                if gain is not None:
                    act.activation(u_hi[:, c, :], h[:, c, :], ACT.Copy, scale=gain).then_inc(u_hi_ready, 1)
                e = SQ[k] + c
                if e >= 2:
                    act.wait_ge(sq_added, e - 1)
                act.activation(sq[:, e % 2, :], h[:, c, :], ACT.Square).then_inc(sq_ready, 1)

            def root(k):
                act.wait_ge(stat_done, k + 1)
                act.activation(sq[:, 1, :], aux[:, 0, :], ACT.Sqrt, bias=eps[:, 0:1], scale=1.0 / D).then_inc(root_ready, 1)

            def ffn_up(f, name, conv=False):
                n0, t0 = plan.first[name]

                def pair(b, i2, i4, split_a, split_b):
                    if conv:
                        act.wait_ge(tile_freed, i4 + (t0 + 2 * b + 1))
                        act.activation(tmp[:, 0, :], z_gate[:, 2:2 + S], ACT.Identity, scale=conv_col("conv_w2", i2, b, 0),
                                       bias=conv_col("conv_b", i2, b, 0)).then_inc(conv_set, 1)
                        act.wait_ge(conv_done, i4 + (2 * b + 1))
                        act.activation(tmp[:, 0, :], tmp[:, 0, :], ACT.Silu).then_inc(gate_act, 1)
                        split_a()
                        act.wait_ge(tile_freed, i4 + (t0 + 2 * b + 2))
                        act.activation(tmp[:, 1, :], z_up[:, 2:2 + S], ACT.Identity, scale=conv_col("conv_w2", i2, b, KF),
                                       bias=conv_col("conv_b", i2, b, KF)).then_inc(conv_set, 1)
                    else:
                        act.wait_ge(tile_freed, i4 + (t0 + 2 * b + 1))
                        act.activation(gate_t[:, b, :], gate_t[:, b, :], ACT.Silu).then_inc(gate_act, 1)
                        split_a()
                    act.wait_ge(prod_ready, i2 + (f * KF + b + 1))
                    src = tmp[:, 1, :] if conv else up_t[:, b, :]
                    act.activation(hid_hi[:, i2 + b, :], src, ACT.Copy).then_inc(prod_hi, 1)
                    split_b()

                rounds = KF // 2
                with act.Fori(0, rounds - 1) as i:
                    for b in range(2):
                        def ahead(j):
                            n = n0 + RING + j
                            hi_part(n % RING, SLAB, i * 16 + load_count(n), (tile_done, i * 4 + (t0 + j + 1)))
                        pair(b, i * 2, i * 4, lambda: ahead(2 * b), lambda: ahead(2 * b + 1))
                done[0] = n0 + 4 * rounds
                for b in range(2):
                    p = 2 * (rounds - 1) + b
                    pair(b, 2 * (rounds - 1), 4 * (rounds - 1), lambda: split_slabs(n0 + 2 * p + 5), lambda: split_slabs(n0 + 2 * p + 6))

            def ffn_down(name, k, gain):
                n0, t0 = plan.first[name]
                for m in range(KD):
                    split_slabs(n0 + DOWN_SLABS * (m + 1) + RING)
                    norm_chunk(k, m, gain(m), t0 + m)
                    if name == "down1" and 1 <= m <= len(TABLES):
                        table(m - 1)

            def table(i):
                dst, scale = TABLES[i][2:]
                act.wait_ge(angle_ready, i + 1)
                act.activation(dst, gate_t[:, 1, :], ACT.Sin, scale=1.0 if scale is None else consts[:, scale:scale + 1]).then_inc(table_ready, 1)

            def split_to_hi(step, half, dst, src):
                act.wait_ge(split_in, nth(made_steps, (step, half)) + 1)
                act.activation(dst, src, ACT.Copy).then_inc(split_hi, 1)

            def col(name, c):
                return cols[:, COL[name] + c:COL[name] + c + 1]

            def conv_col(name, i2, b, off):
                at = i2 + (COL[name] + off + b)
                return cols[:, at:at + 1] if isinstance(at, int) else cols[:, bass.ds(at, 1)]

            act.wait_ge(vec_loaded, 32)
            for c in range(KD):
                act.wait_ge(x_loaded[c], 16)
                norm_chunk(0, c, col("ffn1_norm", c))
                split_slabs(min(c + 1, RING))
            act.wait_ge(consts_set, 3)
            root(0)
            ffn_up(0, "up1")
            act.wait_ge(hid_ready, KF)
            act.dma_start(gate_t[:, 0, :].bitcast(I32), A["positions"]).then_inc(pos_loaded, 16)
            ffn_down("down1", 1, lambda m: col("mix_norm", m))
            act.wait_ge(stat_done, 2)
            act.activation(small[:, 0:NT], aux[:, 1, 0:NT], ACT.Sqrt, bias=eps[:, 0:1], scale=1.0 / D)
            act.activation(sq[:, 1, :], aux[:, 0, :], ACT.Sqrt, bias=eps[:, 0:1], scale=1.0 / D).then_inc(root_ready, 1)

            for step in MIX:
                kind = step[0]
                n, t = plan.first[step]
                if kind in ("rg", "ga", "gb"):
                    act.wait_ge(tile_freed, t + 1)
                    buf = {"rg": lambda: srg[:, step[1] % 2, step[2], :], "ga": lambda: up_t[:, 0, :], "gb": lambda: up_t[:, 1, :]}[kind]()
                    act.activation(buf, buf, ACT.Silu if kind == "rg" else ACT.Sigmoid).then_inc(gate_act, 1)
                elif kind == "index":
                    nk = (step[1] + 1) * P
                    for hd in range(2 * step[2], 2 * step[2] + 2):
                        j = index_units[step[1]] + hd
                        act.wait_ge(idx_scored, j + 1)
                        if j >= 2:
                            act.wait_ge(idx_added, j - 1)
                        act.activation(sq[:, j % 2, 0:nk], aux[:, 2 + j % 2, 0:nk], ACT.Relu, scale=A_DIM ** -0.5).then_inc(idx_relu, 1)
                elif kind == "rsq":
                    act.wait_ge(ry_done, step[1] + 1)
                    for half in range(2):
                        act.activation(y_sq[:, half, :], aux[:, half, :], ACT.Square).then_inc(ry_sq, 1)
                elif kind == "rsum":
                    act.wait_ge(stat_done, 3 + step[1])
                    act.activation(y_sq[:, 1, :], aux[:, 2, :], ACT.Sqrt, bias=eps[:, 1:2], scale=1.0 / R_V).then_inc(root_ready, 1)
                elif kind == "rlo":
                    for half in range(2):
                        split_to_hi(step, half, yr_hi[:, 2 * step[1] + half, :], y_sq[:, half, :])
                elif kind == "logits":
                    b, i = step[1], nth(logit_steps, step)
                    act.wait_ge(neg_ready, i + 1)
                    for hd in range(A_HEADS):
                        act.activation(probs_of(b, hd), probs_of(b, hd), ACT.Exp, bias=neg_max[:, 8 * (i % 2) + hd:8 * (i % 2) + hd + 1],
                                       accum_out=row_sum[:, 8 * (i % 2) + hd:8 * (i % 2) + hd + 1]).then_inc(exp_done, 1)
                elif kind == "attend":
                    b = step[1]
                    for g in range(2 * (b + 1)):
                        gg = pt_base[step] + g
                        act.wait_ge(pt_done, gg + 1)
                        act.activation(pt[:, gg % 2, :], aux[:, gg % 2, :], ACT.Copy).then_inc(pt_ready, 1)
                    act.wait_ge(tile_freed, t + 1)
                    act.activation(ya_hi[:, :, blk(b)], tmp[:, 0, :].rearrange("p (c q) -> p c q", c=4), ACT.Copy).then_inc(split_hi, 1)
                elif kind == "mg":
                    split_to_hi(step, 0, mg_hi[:, step[1], :], gate_t[:, step[1] % 2, :])
                elif kind == "wout":
                    norm_chunk(2, step[1], col("ffn2_norm", step[1]), t)
                split_slabs(n + PROJECTS.get(kind, (0, 0))[0] + RING)
            root(6)
            ffn_up(1, "up2")
            ffn_down("down2", 3, lambda m: col("ple_norm", m))
            root(7)

            act.wait_ge(pt_loaded, 16)
            for c in range(2):
                act.activation(p_hi[:, c, :], p_raw[:, c, :], ACT.Copy).then_inc(p_split, 1)

            def gla_squares(m):
                act.wait_ge(h_updated, m + 1)
                for e, scale in ((0, 1.0), (1, col("final_norm", m))):
                    act.wait_ge(sq_added, SQ[4] + 2 * m + e - 1)
                    act.activation(sq[:, e, :], h[:, m, :], ACT.Square, scale=scale).then_inc(sq_ready, 1)

            for step in PLE_STEPS:
                n, t = plan.first[step]
                if step[0] == "pgate":
                    m = step[1]
                    act.wait_ge(tile_freed, t + 1)
                    act.activation(gate_t[:, m % 2, :], gate_t[:, m % 2, :], ACT.Sigmoid).then_inc(gate_act, 1)
                    if 2 <= m < KD - 1:
                        gla_squares(m)
                elif step[1] == 1:
                    gla_squares(0)
                    gla_squares(1)
                split_slabs(n + PROJECTS[step[0]][0] + RING)
            act.wait_ge(tile_done, plan.first["gla"][1])
            for m in range(KD):
                act.wait_ge(h_updated, m + 1)
                act.activation(u_hi[:, m, :], h[:, m, :], ACT.Copy, scale=small[:, 48 + m:49 + m]).then_inc(u_hi_ready, 1)
            gla_squares(KD - 1)
            act.wait_ge(ms2_ready, 1)
            act.activation(sq[:, 1, :], sq[:, 0, :], ACT.Sqrt)
            act.activation(small[:, 4:4 + NT], small[:, 12:12 + NT], ACT.Sqrt).then_inc(root_ready, 1)
            act.activation(ssum2, gres, ACT.Sqrt).then_inc(root_ready, 1)

            for step in GLA:
                kind = step[0]
                n, t = plan.first[step]
                if kind == "alpha":
                    for c in range(G_HEADS):
                        act.wait_ge(tile_freed, t + c + 1)
                        act.activation(tmp[:, c, :], gcum[:, c, :], ACT.Abs).then_inc(al_ln, 1)
                    for c in range(G_HEADS):
                        act.wait_ge(al_ln, c + 1)
                        act.activation(tmp[:, c, :], tmp[:, c, :], ACT.Exp, scale=-1.0).then_inc(al_ln, 1)
                    for c in range(G_HEADS):
                        act.wait_ge(al_ln, G_HEADS + c + 1)
                        act.activation(tmp[:, c, :], tmp[:, c, :], ACT.Ln, bias=ones[:, 0:1]).then_inc(al_ln, 1)
                elif kind == "gpre":
                    r = step[1]
                    act.wait_ge(al_ready, G_HEADS)
                    if r:
                        act.wait_ge(gst_ready, 7 * r)
                    act.activation(gate_t[:, 0, :], gcum[:, r, :], ACT.Exp, scale=1.0 / G_TAU).then_inc(ge_ready, 1)
                    act.activation(gate_t[:, 1, :], gcum[:, r, :], ACT.Exp, scale=-1.0 / G_TAU).then_inc(ge_ready, 1)
                    act.wait_ge(gd_ready, r + 1)
                    act.activation(up_t[:, 0, :], up_t[:, 0, :], ACT.Exp, scale=1.0 / G_TAU).then_inc(ge_ready, 1)
                elif kind == "gsc":
                    r = step[1]
                    act.wait_ge(gke_done, r + 1)
                    if r:
                        act.wait_ge(gkv_done, 7 * r)
                    act.activation(gket[:, :, :], aux[:, 3, :].rearrange("p (a b) -> p a b", a=NT), ACT.Copy).then_inc(gke_ready, 1)
                elif kind == "gout":
                    r = step[1]
                    for tt in range(NT):
                        act.wait_ge(tile_freed, t + tt // 2 + 1)
                        if NT * r + tt >= 2:
                            act.wait_ge(go_sq, NT * r + tt - 1)
                        act.activation(sq[:, tt % 2, 0:G_DV], go[:, r, tt, :], ACT.Square,
                                       accum_out=head_sq[:, NT * r + tt:NT * r + tt + 1]).then_inc(go_sq, 1)
                    act.wait_ge(go_sq, NT * (r + 1))
                    act.activation(head_root[:, NT * r:NT * (r + 1)], head_sq[:, NT * r:NT * (r + 1)], ACT.Sqrt,
                                   bias=eps[:, 0:1], scale=1.0 / G_DV).then_inc(root_ready, 1)
                elif kind == "gr":
                    act.wait_ge(tile_freed, t + 1)
                    act.activation(gkq[:, step[1] % 2, :], gkq[:, step[1] % 2, :], ACT.Silu).then_inc(gate_act, 1)
                elif kind == "gt":
                    split_to_hi(step, 0, gy_hi[:, step[1], :], up_t[:, step[1] % 2, :])
                elif kind == "gwout":
                    norm_chunk(5, step[1], col("l0_norm2", step[1]), t)
                split_slabs(n + PROJECTS.get(kind, (0, 0))[0] + RING)
            root(9)
            ffn_up(2, "up3", conv=True)
            ffn_down("down3", 6, lambda m: None)
            root(10)

        @block.vector
        def _(dve):
            step_no = [0]

            def link(ins):
                step_no[0] += 1
                ins.then_inc(dve_step, 1)
                dve.wait_ge(dve_step, step_no[0])

            def col(name, c):
                return cols[:, COL[name] + c:COL[name] + c + 1]

            def norm_chunk(k, c, gain):
                if gain is not None:
                    dve.wait_ge(u_hi_ready, KD * k + c + 1)
                    dve.scalar_tensor_tensor(u_lo[:, c, :], h[:, c, :], gain, u_hi[:, c, :].bitcast(F32),
                                             ALU.mult, ALU.subtract).then_inc(u_ready, 1)
                e = SQ[k] + c
                dve.wait_ge(sq_ready, e + 1)
                add_squares(ssum, e, c == 0)

            def add_squares(total, e, first):
                if first:
                    dve.tensor_copy(total[:, :], sq[:, e % 2, :]).then_inc(sq_added, 1)
                else:
                    dve.wait_ge(sq_added, e)
                    dve.tensor_tensor(total[:, :], total[:, :], sq[:, e % 2, :], ALU.add).then_inc(sq_added, 1)

            def inverse_root(dst, ms, scale, epsilon, x, root):
                link(dve.tensor_scalar(x, ms, scale, epsilon, ALU.mult, ALU.add))
                return newton(dst, x, root)

            def newton(dst, x, root):
                link(dve.reciprocal(root, root))
                link(dve.tensor_tensor(x, x, root, ALU.mult))
                link(dve.tensor_tensor(x, x, root, ALU.mult))
                link(dve.tensor_scalar(x, x, -0.5, 1.5, ALU.mult, ALU.add))
                return dve.tensor_tensor(dst, x, root, ALU.mult)

            def rstd_of_norm(roots, count):
                dve.wait_ge(root_ready, roots)
                inverse_root(rstd[:, :], aux[:, 0, :], 1.0 / D, NORM_EPS, sq[:, 0, :], sq[:, 1, :]).then_inc(rstd_ready, 1)
                dve.wait_ge(rstd_ready, count)

            def ffn_up(f, name):
                t0 = plan.first[name][1]
                with dve.Fori(0, KF // 2) as i:
                    for b in range(2):
                        dve.wait_ge(tile_done, i * 4 + (t0 + 2 * b + 1))
                        dve.tensor_tensor(gate_t[:, b, :], acc[:, (t0 + 2 * b) % BANKS, :], rstd[:, :], ALU.mult).then_inc(tile_freed, 1)
                        dve.wait_ge(tile_done, i * 4 + (t0 + 2 * b + 2))
                        dve.tensor_tensor(up_t[:, b, :], acc[:, (t0 + 2 * b + 1) % BANKS, :], rstd[:, :], ALU.mult).then_inc(tile_freed, 1)
                        dve.wait_ge(gate_act, i * 2 + (GATES_FFN[f] + b + 1))
                        dve.wait_ge(tile_freed, i * 4 + (t0 + 2 * b + 2))
                        dve.tensor_tensor(up_t[:, b, :], gate_t[:, b, :], up_t[:, b, :], ALU.mult).then_inc(prod_ready, 1)
                        dve.wait_ge(prod_hi, i * 2 + (f * KF + b + 1))
                        dve.tensor_tensor(hid_lo[:, i * 2 + b, :], up_t[:, b, :], hid_hi[:, i * 2 + b, :].bitcast(F32),
                                          ALU.subtract).then_inc(hid_ready, 1)

            def conv_up(f, name):
                t0 = plan.first[name][1]
                dve.memset(z_gate[:, 0:2], 0.0)
                dve.memset(z_up[:, 0:2], 0.0)

                def conv_col(name, i2, b, off):
                    return cols[:, bass.ds(i2 + (COL[name] + off + b), 1)]

                with dve.Fori(0, KF // 2) as i:
                    for b in range(2):
                        for part, z in enumerate((z_gate, z_up)):
                            c = 2 * b + part
                            dve.wait_ge(tile_done, i * 4 + (t0 + c + 1))
                            dve.tensor_tensor(z[:, 2:2 + S], acc[:, (t0 + c) % BANKS, :], rstd[:, :], ALU.mult).then_inc(tile_freed, 1)
                            dve.wait_ge(tile_freed, i * 4 + (t0 + c + 1))
                            dve.wait_ge(conv_set, i * 4 + (c + 1))
                            dve.scalar_tensor_tensor(tmp[:, part, :], z[:, 1:1 + S], conv_col("conv_w1", i * 2, b, part * KF),
                                                     tmp[:, part, :], ALU.mult, ALU.add).then_inc(conv_step, 1)
                            dve.wait_ge(conv_step, i * 4 + (c + 1))
                            dve.scalar_tensor_tensor(tmp[:, part, :], z[:, 0:S], conv_col("conv_w0", i * 2, b, part * KF),
                                                     tmp[:, part, :], ALU.mult, ALU.add).then_inc(conv_done, 1)
                        dve.wait_ge(gate_act, i * 2 + (GATES_FFN[f] + b + 1))
                        dve.wait_ge(conv_done, i * 4 + (2 * b + 2))
                        dve.tensor_tensor(tmp[:, 1, :], tmp[:, 0, :], tmp[:, 1, :], ALU.mult).then_inc(prod_ready, 1)
                        dve.wait_ge(prod_hi, i * 2 + (f * KF + b + 1))
                        dve.tensor_tensor(hid_lo[:, i * 2 + b, :], tmp[:, 1, :], hid_hi[:, i * 2 + b, :].bitcast(F32),
                                          ALU.subtract).then_inc(hid_ready, 1)

            def table(i):
                inv, quarter = TABLES[i][:2]
                angle, turns = gate_t[:, 1, :], rstd[:, :]
                if i == 0:
                    dve.wait_ge(pos_loaded, 16)
                else:
                    dve.wait_ge(table_ready, i)
                link(dve.tensor_scalar(angle, gate_t[:, 0, :].bitcast(I32), consts[:, inv:inv + 1], None, ALU.mult))
                link(dve.tensor_scalar(turns.bitcast(I32), angle, 1.0 / TWO_PI, quarter, ALU.mult, ALU.add))
                link(dve.tensor_copy(turns, turns.bitcast(I32)))
                for part in (PI_A, PI_B, PI_C):
                    link(dve.scalar_tensor_tensor(angle, turns, -part, angle, ALU.mult, ALU.add))
                link(dve.tensor_scalar(angle, angle, quarter * TWO_PI, PI_MAX, ALU.add, ALU.min))
                dve.tensor_scalar(angle, angle, -PI_MAX, None, ALU.max).then_inc(angle_ready, 1)

            def ffn_down(name, k, gain, half):
                t0 = plan.first[name][1]
                for m in range(KD):
                    dve.wait_ge(tile_done, t0 + m + 1)
                    dve.scalar_tensor_tensor(h[:, m, :], acc[:, (t0 + m) % BANKS, :], half, h[:, m, :],
                                             ALU.mult, ALU.add).then_inc(tile_freed, 1)
                    norm_chunk(k, m, gain(m))
                    if name == "down1" and m < len(TABLES):
                        table(m)

            def lo_part(step, half, dst, src, hi):
                dve.wait_ge(split_hi, nth(split_steps, (step, half)) + 1)
                dve.tensor_tensor(dst, src, hi.bitcast(F32), ALU.subtract).then_inc(split_ready, 1)

            dve.wait_ge(vec_loaded, 32)
            for c in range(KD):
                norm_chunk(0, c, col("ffn1_norm", c))
            rstd_of_norm(1, 1)
            ffn_up(0, "up1")
            ffn_down("down1", 1, lambda m: col("mix_norm", m), 0.5)
            rstd_of_norm(2, 2)
            link(inverse_root(rstd_tok[:, :], aux[:, 1, 0:NT], 1.0 / D, NORM_EPS, small[:, 8:8 + NT], small[:, 0:NT]))

            dve.wait_ge(table_ready, 4)
            dve.tensor_copy(cos_r[:, :], up_t[:, 0, :])
            link(dve.tensor_copy(sin_r[:, :], up_t[:, 1, :]))

            for step in MIX:
                kind = step[0]
                n, t = plan.first[step]
                bank = acc[:, t % BANKS, :]
                if kind in PROJECTS and kind != "attend":
                    dve.wait_ge(tile_done, t + 1)
                if kind == "avw":
                    link(dve.tensor_tensor(avt[:, :, :], bank[:, 0:NT * 72].rearrange("p (a b) -> p a b", a=NT),
                                           rstd_tok[:, :].unsqueeze(2).to_broadcast([P, NT, 72]), ALU.mult))
                    dve.tensor_scalar(avt[:, :, A_DIM:72], avt[:, :, A_DIM:72], A_HEADS ** -0.5, None, ALU.mult).then_inc(tile_freed, 1)
                elif kind == "rv":
                    v = rv[:, step[1] % 2, :, :]
                    for i in range(2):
                        dve.wait_ge(tile_done, t + i + 1)
                        part = v[:, 2 * i:2 * i + 2, :]
                        dve.tensor_tensor(part, acc[:, (t + i) % BANKS, :].rearrange("p (a b) -> p a b", a=2),
                                          rstd_tok[:, 2 * i:2 * i + 2].unsqueeze(2).to_broadcast([P, 2, R_V]), ALU.mult).then_inc(tile_freed, 1)
                        dve.wait_ge(tile_freed, t + i + 1)
                        link(dve.reduce_sum(small[:, 56:58], part, AX_X))
                        link(dve.tensor_scalar(small[:, 56:58], small[:, 56:58], -1.0 / R_V, None, ALU.mult))
                        dve.tensor_tensor(part, part, small[:, 56:58].unsqueeze(2).to_broadcast([P, 2, R_V]), ALU.add).then_inc(rv_ready, 1)
                elif kind in ("rg", "ga", "gb"):
                    buf = {"rg": lambda: srg[:, step[1] % 2, step[2], :], "ga": lambda: up_t[:, 0, :], "gb": lambda: up_t[:, 1, :]}[kind]()
                    dve.tensor_tensor(buf, bank, rstd[:, :], ALU.mult).then_inc(tile_freed, 1)
                elif kind in ROPE:
                    z = nth(rope_steps, step)
                    if z >= 2:
                        dve.wait_ge(rope_ready, z - 1)
                    dve.tensor_tensor(gate_t[:, z % 2, :], bank, rstd[:, :], ALU.mult).then_inc(tile_freed, 1)
                elif kind == "index":
                    b = step[1]
                    nk = (b + 1) * P
                    score = bias[:, bias_at[b]:bias_at[b] + nk]
                    for hd in range(2 * step[2], 2 * step[2] + 2):
                        j = index_units[b] + hd
                        w = avt[:, b, A_DIM + hd:A_DIM + hd + 1]
                        dve.wait_ge(idx_relu, j + 1)
                        if hd == 0:
                            dve.tensor_scalar(score, sq[:, j % 2, 0:nk], w, None, ALU.mult).then_inc(idx_added, 1)
                        else:
                            dve.wait_ge(idx_added, j)
                            dve.scalar_tensor_tensor(score, sq[:, j % 2, 0:nk], w, score, ALU.mult, ALU.add).then_inc(idx_added, 1)
                elif kind == "topk":
                    b = step[1]
                    nk = (b + 1) * P
                    score = bias[:, bias_at[b]:bias_at[b] + nk]
                    if step[2] == 0:
                        dve.wait_ge(idx_added, index_units[b] + A_HEADS)
                        link(dve.memset(score[0:CHUNK, nk - CHUNK:nk], NEG_BIG))
                    for _ in range(TOPK // 8 // TOPK_STEPS):
                        link(dve.max(top8, score))
                        link(dve.match_replace(score, top8, score, TAKEN))
                    if step[2] == TOPK_STEPS - 1:
                        link(dve.tensor_scalar(score, score, TAKEN, NEG_BIG, ALU.not_equal, ALU.mult))
                elif kind == "rscore":
                    r = step[1]
                    dve.wait_ge(dec_loaded, 16 * (r + 1))
                    for jt in range(NT):
                        nq = S - jt * P
                        dve.wait_ge(rs_done, NT * r + jt + 1)
                        dve.tensor_tensor(wts[:, wts_at[jt]:wts_at[jt] + nq], aux[:, 2 + jt % 2, 0:nq], dec[:, 0:nq], ALU.mult).then_inc(rw_ready, 1)
                elif kind == "rsq":
                    dve.wait_ge(ry_sq, 2 * step[1] + 2)
                    dve.tensor_tensor(ssum[:, :], y_sq[:, 0, :], y_sq[:, 1, :], ALU.add).then_inc(ry_sum, 1)
                elif kind == "rfin":
                    r = step[1]
                    dve.wait_ge(root_ready, 3 + r)
                    link(inverse_root(ssum[:, :], aux[:, 2, :], 1.0 / R_V, GN_EPS, y_sq[:, 0, :], y_sq[:, 1, :]))
                    for half in range(2):
                        dve.tensor_tensor(y_sq[:, half, :], aux[:, half, :], ssum[:, :], ALU.mult).then_inc(ry_freed, 1)
                    for half in range(2):
                        dve.wait_ge(ry_freed, 2 * r + half + 1)
                        dve.wait_ge(gate_act, gates_before(("rg", r, half)) + 1)
                        dve.scalar_tensor_tensor(y_sq[:, half, :], y_sq[:, half, :], col("ret_gn", 2 * r + half), srg[:, r % 2, half, :],
                                                 ALU.mult, ALU.mult).then_inc(split_in, 1)
                elif kind == "rlo":
                    r = step[1]
                    for half in range(2):
                        lo_part(step, half, yr_lo[:, 2 * r + half, :], y_sq[:, half, :], yr_hi[:, 2 * r + half, :])
                elif kind == "logits":
                    b, i = step[1], nth(logit_steps, step)
                    nk = (b + 1) * P
                    if b == 0:
                        link(dve.memset(bias[:, 0:P], 0.0))
                        link(dve.memset(bias[0:CHUNK, CHUNK:P], NEG_BIG))
                    if i == 0:
                        dve.wait_ge(rope_ready, len(rope_steps))
                    at = 8 * (i % 2)
                    for hd in range(A_HEADS):
                        j = A_HEADS * i + hd
                        dve.wait_ge(lg_done, j + 1)
                        dve.tensor_tensor_reduce(out=probs_of(b, hd), in0=aux[:, 2 + j % 2, 0:nk], in1=bias[:, bias_at[b]:bias_at[b] + nk],
                                                 scale=A_DIM ** -0.5, scalar=TAKEN, op0=ALU.add, op1=ALU.max,
                                                 accum_out=row_max[:, at + hd:at + hd + 1]).then_inc(lg_read, 1)
                    dve.wait_ge(lg_read, A_HEADS * (i + 1))
                    dve.tensor_scalar(neg_max[:, at:at + 8], row_max[:, at:at + 8], -1.0, None, ALU.mult).then_inc(neg_ready, 1)
                elif kind == "attend":
                    b = step[1]
                    i = nth(logit_steps, ("logits", b))
                    at = 8 * (i % 2)
                    dve.wait_ge(exp_done, A_HEADS * (i + 1))
                    link(dve.reciprocal(row_inv[:, at:at + 8], row_sum[:, at:at + 8]))
                    for hd in range(A_HEADS):
                        dve.tensor_scalar(probs_of(b, hd), probs_of(b, hd), row_inv[:, at + hd:at + hd + 1], None, ALU.mult).then_inc(p_ready, 1)
                    dve.wait_ge(tile_done, t + 1)
                    dve.tensor_copy(tmp[:, 0, :], bank).then_inc(tile_freed, 1)
                    dve.wait_ge(tile_freed, t + 1)
                    lo_part(step, 0, ya_lo[:, :, blk(b)], tmp[:, 0, :].rearrange("p (c q) -> p c q", c=4), ya_hi[:, :, blk(b)])
                elif kind == "wa":
                    if step[1]:
                        dve.wait_ge(split_ready, nth(split_steps, (("mg", step[1] - 1), 0)) + 1)
                    for i in range(2):
                        dve.wait_ge(tile_done, t + i + 1)
                        dve.tensor_copy(gate_t[:, i, :], acc[:, (t + i) % BANKS, :]).then_inc(tile_freed, 1)
                elif kind == "wb":
                    dve.wait_ge(gate_act, gates_before(("gb", step[1])) + 1)
                    dve.tensor_tensor(branch_b[:, :], bank, up_t[:, 1, :], ALU.mult).then_inc(tile_freed, 1)
                elif kind == "mg":
                    m = step[1]
                    x = gate_t[:, m % 2, :]
                    dve.wait_ge(tile_freed, max(plan.first[("wb", m)][1] + 1, plan.first[("wa", m - m % 2)][1] + m % 2 + 1))
                    link(dve.tensor_tensor(x, x, up_t[:, 0, :], ALU.mult))
                    dve.tensor_tensor(x, x, branch_b[:, :], ALU.add).then_inc(split_in, 1)
                    lo_part(step, 0, mg_lo[:, m, :], x, mg_hi[:, m, :])
                elif kind == "wout":
                    m = step[1]
                    dve.tensor_tensor(h[:, m, :], bank, h[:, m, :], ALU.add).then_inc(tile_freed, 1)
                    norm_chunk(2, m, col("ffn2_norm", m))
            rstd_of_norm(7, 3)
            ffn_up(1, "up2")
            ffn_down("down2", 3, lambda m: col("ple_norm", m), 0.5)
            link(dve.tensor_tensor(small[:, 48:48 + KD], cols[:, COL["final_norm"]:COL["final_norm"] + KD],
                                   cols[:, COL["l0_norm1"]:COL["l0_norm1"] + KD], ALU.mult))
            rstd_of_norm(8, 4)
            for c in range(2):
                dve.wait_ge(p_split, c + 1)
                dve.tensor_tensor(p_lo[:, c, :], p_raw[:, c, :], p_hi[:, c, :].bitcast(F32), ALU.subtract).then_inc(hid_ready, 1)

            def ple_add(m):
                dve.wait_ge(gate_act, gates_before(("pgate", m)) + 1)
                link(dve.tensor_tensor(gate_t[:, m % 2, :], gate_t[:, m % 2, :], proj[:, m, :], ALU.mult))
                dve.tensor_tensor(h[:, m, :], h[:, m, :], gate_t[:, m % 2, :], ALU.add).then_inc(h_updated, 1)

            def ple_squares(m):
                for e, total in ((0, ssum), (1, ssum2)):
                    dve.wait_ge(sq_ready, SQ[4] + 2 * m + e + 1)
                    add_squares(total, SQ[4] + 2 * m + e, m == 0)

            for step in PLE_STEPS:
                n, t = plan.first[step]
                dve.wait_ge(tile_done, t + 1)
                if step[0] == "pgate":
                    m = step[1]
                    dve.tensor_tensor(gate_t[:, m % 2, :], acc[:, t % BANKS, :], rstd[:, :], ALU.mult).then_inc(tile_freed, 1)
                    if m >= 2:
                        ple_add(m)
                    if 2 <= m < KD - 1:
                        ple_squares(m)
                else:
                    for i in range(4):
                        dve.wait_ge(tile_done, t + i + 1)
                        dve.tensor_copy(proj[:, 4 * step[1] + i, :], acc[:, (t + i) % BANKS, :]).then_inc(tile_freed, 1)
                    if step[1] == 1:
                        dve.wait_ge(tile_freed, t + 4)
                        ple_add(0)
                        ple_add(1)
                        ple_squares(0)
                        ple_squares(1)
            for m in range(KD):
                dve.wait_ge(u_hi_ready, KD * 4 + m + 1)
                dve.scalar_tensor_tensor(u_lo[:, m, :], h[:, m, :], small[:, 48 + m:49 + m], u_hi[:, m, :].bitcast(F32),
                                         ALU.mult, ALU.subtract).then_inc(u_ready, 1)

            ple_squares(KD - 1)

            dve.wait_ge(stat_done, 9)
            a_tok, x_tok = small[:, 160:160 + NT], small[:, 12:12 + NT]
            dve.tensor_scalar(a_tok, aux[:, 2, 0:NT], 1.0 / D, NORM_EPS, ALU.mult, ALU.add)
            link(dve.tensor_scalar(gres, aux[:, 0, :], 1.0 / D, NORM_EPS, ALU.mult, ALU.add))
            dve.tensor_scalar(a_tok, a_tok, NORM_EPS, None, ALU.mult)
            link(dve.tensor_scalar(sq[:, 0, :], gres, NORM_EPS, None, ALU.mult))
            link(dve.scalar_tensor_tensor(x_tok, aux[:, 2, NT:2 * NT], 1.0 / D, a_tok, ALU.mult, ALU.add))
            dve.scalar_tensor_tensor(sq[:, 0, :], aux[:, 1, :], 1.0 / D, sq[:, 0, :], ALU.mult, ALU.add).then_inc(ms2_ready, 1)
            dve.wait_ge(root_ready, 9)
            newton(rstd[:, :], sq[:, 0, :], sq[:, 1, :]).then_inc(rstd_ready, 1)
            link(newton(rstd_tok[:, :], x_tok, small[:, 4:4 + NT]))
            keep = ssum
            link(dve.memset(keep[:, :], 1.0))
            link(dve.memset(keep[:, 0:S:CHUNK], 0.0))
            dve.wait_ge(rstd_ready, 5)

            for step in GLA:
                kind = step[0]
                n, t = plan.first[step]
                bank = acc[:, t % BANKS, :]
                if kind in PROJECTS:
                    dve.wait_ge(tile_done, t + 1)
                if kind == "alow":
                    dve.tensor_tensor(alow_t[0:G_RANK, :], bank[0:G_RANK, :], rstd[0:G_RANK, :], ALU.mult).then_inc(tile_freed, 1)
                elif kind == "alpha":
                    for c in range(G_HEADS):
                        dve.wait_ge(tile_done, t + c + 1)
                        dve.tensor_scalar(gcum[:, c, :], acc[:, (t + c) % BANKS, :], col("b_alpha", c), None, ALU.add).then_inc(tile_freed, 1)
                    dve.memset(gsc[:, :, :], 0.0)
                elif kind == "cum":
                    for c in range(G_HEADS):
                        dve.wait_ge(al_ln, 2 * G_HEADS + c + 1)
                        link(dve.scalar_tensor_tensor(tmp[:, c, :], gcum[:, c, :], 0.0, tmp[:, c, :], ALU.min, ALU.subtract))
                        dve.tensor_tensor_scan(gcum[:, c, :], keep[:, :], tmp[:, c, :], 0.0, ALU.mult, ALU.add).then_inc(al_ready, 1)
                elif kind == "res":
                    if step[1] == 0:
                        dve.wait_ge(root_ready, 10)
                        link(newton(gres, gres, ssum2))
                    for c in (2 * step[1], 2 * step[1] + 1):
                        dve.scalar_tensor_tensor(h[:, c, :], h[:, c, :], col("final_norm", c), gres, ALU.mult, ALU.mult)
                elif kind in ("gk", "gq"):
                    dve.tensor_tensor(gkq[:, 1 if kind == "gq" else 0, :], bank, rstd[:, :], ALU.mult).then_inc(tile_freed, 1)
                elif kind == "gv":
                    for i in range(2):
                        dve.wait_ge(tile_done, t + i + 1)
                        dve.tensor_tensor(gvt[:, step[1] % 2, 2 * i:2 * i + 2, :], acc[:, (t + i) % BANKS, :].rearrange("p (a b) -> p a b", a=2),
                                          rstd_tok[:, 2 * i:2 * i + 2].unsqueeze(2).to_broadcast([P, 2, G_DV]), ALU.mult).then_inc(tile_freed, 1)
                elif kind == "gpre":
                    r = step[1]
                    cum = gcum[:, r, :].rearrange("p (n c) -> p n c", c=CHUNK)
                    dve.wait_ge(al_ready, G_HEADS)
                    dve.tensor_tensor(up_t[:, 0, :].rearrange("p (n c) -> p n c", c=CHUNK), cum[:, :, CHUNK - 1:CHUNK].to_broadcast([P, S // CHUNK, CHUNK]),
                                      cum, ALU.subtract).then_inc(gd_ready, 1)
                    dve.wait_ge(tile_freed, plan.first[("gq", r)][1] + 1)
                    dve.wait_ge(ge_ready, 3 * r + 2)
                    dve.scalar_tensor_tensor(gqd[:, :], gkq[:, 1, :], G_DK ** -0.5, gate_t[:, 0, :], ALU.mult, ALU.mult)
                    dve.tensor_tensor(gki[:, :], gkq[:, 0, :], gate_t[:, 1, :], ALU.mult)
                    dve.wait_ge(ge_ready, 3 * r + 3)
                    dve.tensor_tensor(up_t[:, 1, :], gkq[:, 0, :], up_t[:, 0, :], ALU.mult).then_inc(gqk_ready, 1)
                elif kind == "gsc":
                    r = step[1]
                    dve.wait_ge(gs_done, r + 1)
                    for e in range(2):
                        rows = slice(e * CHUNK, (e + 1) * CHUNK)
                        ins = dve.tensor_tensor(gsc[rows, :, rows], aux[rows, 2, 0:NT * CHUNK].rearrange("p (a b) -> p a b", a=NT),
                                                consts[rows, C_MASK:C_MASK + CHUNK].unsqueeze(1).to_broadcast([CHUNK, NT, CHUNK]), ALU.mult)
                    ins.then_inc(gsc_ready, 1)
                elif kind == "gkv":
                    r = step[1]
                    for n in range(7):
                        kv = state_bank(n)
                        dve.wait_ge(gkv_done, 7 * r + (4 if n < 4 else 7))
                        if n == 0:
                            dve.tensor_copy(gst[:, 0, :], kv).then_inc(gst_ready, 1)
                        else:
                            end = n * CHUNK + CHUNK - 1
                            dve.wait_ge(gst_ready, 7 * r + n)
                            dve.scalar_tensor_tensor(gst[:, n, :], gst[:, n - 1, :], gate_t[:, 0, end:end + 1], kv, ALU.mult, ALU.add).then_inc(gst_ready, 1)
                elif kind == "gout":
                    r = step[1]
                    for i in range(2):
                        dve.wait_ge(tile_done, t + i + 1)
                        dve.tensor_copy(go[:, r, 2 * i:2 * i + 2, :], acc[:, (t + i) % BANKS, :].rearrange("p (a b) -> p a b", a=2)).then_inc(tile_freed, 1)
                elif kind == "gn":
                    r = step[1]
                    four = slice(NT * r, NT * (r + 1))
                    dve.wait_ge(root_ready, 11 + r)
                    link(inverse_root(head_rstd[:, four], head_sq[:, four], 1.0 / G_DV, NORM_EPS, head_x[:, four], head_root[:, four]))
                    for tt in range(NT):
                        ins = dve.tensor_scalar(go[:, r, tt, :], go[:, r, tt, :], head_rstd[:, NT * r + tt:NT * r + tt + 1], None, ALU.mult)
                    ins.then_inc(gon_ready, 1)
                elif kind == "gr":
                    if step[1] == 0:
                        dve.wait_ge(gqk_ready, G_HEADS)
                    dve.tensor_tensor(gkq[:, step[1] % 2, :], bank, rstd[:, :], ALU.mult).then_inc(tile_freed, 1)
                elif kind == "gt":
                    c = step[1]
                    dve.wait_ge(gt_done, c + 1)
                    dve.wait_ge(gate_act, gates_before(("gr", c)) + 1)
                    dve.scalar_tensor_tensor(up_t[:, c % 2, :], aux[:, 2 + c % 2, :], col("gla_out_norm", c), gkq[:, c % 2, :],
                                             ALU.mult, ALU.mult).then_inc(split_in, 1)
                    lo_part(step, 0, gy_lo[:, c, :], up_t[:, c % 2, :], gy_hi[:, c, :])
                elif kind == "gwout":
                    m = step[1]
                    dve.tensor_tensor(h[:, m, :], bank, h[:, m, :], ALU.add).then_inc(tile_freed, 1)
                    norm_chunk(5, m, col("l0_norm2", m))
            rstd_of_norm(15, 6)
            conv_up(2, "up3")
            ffn_down("down3", 6, lambda m: None, 1.0)
            rstd_of_norm(16, 7)
            for c in range(KD):
                dve.scalar_tensor_tensor(h[:, c, :], h[:, c, :], col("final_norm_2", c), rstd[:, :], ALU.mult, ALU.mult).then_inc(out_ready, 1)

        @block.tensor
        def _(pe):
            free_when = {}

            def claim(bank):
                if bank in free_when:
                    pe.wait_ge(*free_when[bank])

            def slabs_ready(n):
                pe.wait_ge(lo_ready, n + 1)

            def free_bank(t):
                if t >= BANKS:
                    pe.wait_ge(tile_freed, t - BANKS + 1)
                return acc[:, t % BANKS, :]

            def mm3(o, w, x_hi, x_lo, first, last):
                slot, columns = w
                pe.matmul(o, w_lo[:, slot, columns], x_hi, start=first, stop=False)
                pe.matmul(o, w_hi[:, slot, columns], x_lo, start=False, stop=False)
                return pe.matmul(o, w_hi[:, slot, columns], x_hi, start=False, stop=last)

            def sums(k, second=False):
                pe.wait_ge(sq_added, SQ[k + 1])
                claim(0)
                last = pe.matmul(aux[:, 0, :], ones[:, :], ssum[:, :], start=True, stop=True)
                if k == 4:
                    claim(1)
                    pe.matmul(aux[:, 1, :], ones[:, :], ssum2, start=True, stop=True)
                if k in (1, 4):
                    claim(1 if k == 1 else 2)
                    for i, total in enumerate((ssum, ssum2) if k == 4 else (ssum,)):
                        for tt in range(NT):
                            last = pe.matmul(aux[:, 1 if k == 1 else 2, i * NT + tt:i * NT + tt + 1], total[:, blk(tt)], ones[:, 0:1], start=True, stop=True)
                last.then_inc(stat_done, 1)
                for bank in range(3):
                    free_when[bank] = (rstd_ready, k + 1)

            def fm_tile(t, blocks, x_hi, x_lo, ready=None):
                o = free_bank(t)
                seen = None
                for k, (n, b) in enumerate(blocks):
                    if n != seen:
                        slabs_ready(n)
                        seen = n
                    if ready is not None:
                        pe.wait_ge(*ready(k))
                    last = mm3(o, (n % RING, blk(b)), x_hi[:, k, :], x_lo[:, k, :], k == 0, k == len(blocks) - 1)
                last.then_inc(tile_done, 1)

            def token_tiles(t, n, width, per_tile, per_slab):
                for i in range(NT // per_tile):
                    free_bank(t + i)
                    for tt in range(i * per_tile, (i + 1) * per_tile):
                        o = acc[:, (t + i) % BANKS, (tt % per_tile) * width:(tt % per_tile + 1) * width]
                        for k in range(KD):
                            slot = (n + k // per_slab) % RING
                            columns = slice((k % per_slab) * width, (k % per_slab + 1) * width)
                            slabs_ready(n + k // per_slab)
                            pe.matmul(o, u_lo[:, k, blk(tt)], w_hi[:, slot, columns], start=k == 0, stop=False)
                            pe.matmul(o, u_hi[:, k, blk(tt)], w_lo[:, slot, columns], start=False, stop=False)
                            last = pe.matmul(o, u_hi[:, k, blk(tt)], w_hi[:, slot, columns], start=False, stop=k == KD - 1)
                    last.then_inc(tile_done, 1)

            def ffn_up(k, name):
                n0, t0 = plan.first[name]
                for j in range(RING):
                    fm_tile(t0 + j, [(n0 + j, b) for b in range(KD)], u_hi, u_lo, (lambda c: (u_ready, KD * k + c + 1)) if j == 0 else None)
                    if j == 0:
                        sums({0: 0, 2: 2, 5: 5}[k])
                with pe.Fori(1, 2 * KF // RING) as i:
                    for j in range(RING):
                        pe.wait_ge(lo_ready, i * RING + (n0 + j + 1))
                        pe.wait_ge(tile_freed, i * RING + (t0 + j - BANKS + 1))
                        for b in range(KD):
                            last = mm3(acc[:, (t0 + j) % BANKS, :], ((n0 + j) % RING, blk(b)), u_hi[:, b, :], u_lo[:, b, :], b == 0, b == KD - 1)
                        last.then_inc(tile_done, 1)

            def ffn_down(f, name):
                n0, t0 = plan.first[name]
                with pe.Fori(0, 2) as i:
                    for m in range(4):
                        o = acc[:, (t0 + m) % BANKS, :]
                        pe.wait_ge(tile_freed, i * 4 + (t0 + m - BANKS + 1))
                        for k in range(KF):
                            j = DOWN_SLABS * m + k // 8
                            if k % 8 == 0:
                                pe.wait_ge(lo_ready, i * (4 * DOWN_SLABS) + (n0 + j + 1))
                            if k == KF - 1:
                                pe.wait_ge(hid_ready, HIDDEN[f])
                            last = mm3(o, ((n0 + j) % RING, blk(k % 8)), hid_hi[:, k, :], hid_lo[:, k, :], k == 0, k == KF - 1)
                            if k % 8 == 7:
                                last.then_inc(slab_used, 1)
                        last.then_inc(tile_done, 1)

            HIDDEN = [KF, 2 * KF, 3 * KF + 2]
            pe.wait_ge(consts_set, 3)
            ffn_up(0, "up1")
            ffn_down(0, "down1")

            for step in MIX:
                kind = step[0]
                n, t = plan.first[step]
                if step == MIX[0]:
                    fm_tile(t, [(n, b) for b in range(KD)], u_hi, u_lo, lambda c: (u_ready, KD + c + 1))
                    sums(1)
                elif kind == "avw":
                    token_tiles(t, n, 72, NT, KD)
                elif kind == "rv":
                    token_tiles(t, n, R_V, 2, 4)
                elif kind in ("rg", "kk", "iq", "rq", "rk", "aq", "ga", "gb"):
                    fm_tile(t, [(n, b) for b in range(KD)], u_hi, u_lo)
                elif kind == "index":
                    b = step[1]
                    nk = (b + 1) * P
                    pe.wait_ge(rope_ready, nth(rope_steps, ("iq", 3)) + 1)
                    pe.wait_ge(keys_copied, 64)
                    for hd in range(2 * step[2], 2 * step[2] + 2):
                        j = index_units[b] + hd
                        rows = slice(64 * (hd % 2), 64 * (hd % 2) + 64)
                        claim(2 + j % 2)
                        pe.matmul(aux[:, 2 + j % 2, 0:nk], q8[rows, hd // 2, blk(b)], ikd[rows, 0:nk], start=True, stop=True).then_inc(idx_scored, 1)
                        free_when[2 + j % 2] = (idx_relu, j + 1)
                elif kind == "rscore":
                    r = step[1]
                    pe.wait_ge(rope_ready, nth(rope_steps, ("rk", r)) + 1)
                    for jt in range(NT):
                        nq = S - jt * P
                        claim(2 + jt % 2)
                        pe.matmul(aux[:, 2 + jt % 2, 0:nq], rqk[:, 1, blk(jt)], rqk[:, 0, jt * P:S], start=True, stop=True).then_inc(rs_done, 1)
                        free_when[2 + jt % 2] = (rw_ready, NT * r + jt + 1)
                elif kind == "ry":
                    r = step[1]
                    pe.wait_ge(rv_ready, 2 * r + 2)
                    claim(0)
                    claim(1)
                    for jt in range(NT):
                        pe.wait_ge(rw_ready, NT * r + jt + 1)
                        nq = S - jt * P
                        for half in range(2):
                            last = pe.matmul(aux[:, half, jt * P:S], rv[:, r % 2, jt, blk(half)], wts[:, wts_at[jt]:wts_at[jt] + nq],
                                             start=jt == 0, stop=jt == NT - 1)
                    last.then_inc(ry_done, 1)
                    free_when[0] = (ry_freed, 2 * r + 1)
                    free_when[1] = (ry_freed, 2 * r + 2)
                elif kind == "rsum":
                    r = step[1]
                    pe.wait_ge(ry_sum, r + 1)
                    claim(2)
                    pe.matmul(aux[:, 2, :], ones[:, :], ssum[:, :], start=True, stop=True).then_inc(stat_done, 1)
                    free_when[2] = (ry_freed, 2 * r + 1)
                elif kind == "logits":
                    b, i = step[1], nth(logit_steps, step)
                    nk = (b + 1) * P
                    pe.wait_ge(rope_ready, len(rope_steps))
                    for hd in range(A_HEADS):
                        j = A_HEADS * i + hd
                        rows = slice(64 * (hd % 2), 64 * (hd % 2) + 64)
                        claim(2 + j % 2)
                        pe.matmul(aux[:, 2 + j % 2, 0:nk], q8[rows, hd // 2, blk(b)], akd[rows, 0:nk], start=True, stop=True).then_inc(lg_done, 1)
                        free_when[2 + j % 2] = (lg_read, j + 1)
                elif kind == "attend":
                    b = step[1]
                    base = pt_base[step]
                    groups = [(parity, kt) for parity in range(2) for kt in range(b + 1)]

                    def turn(g):
                        parity, kt = groups[g]
                        claim((base + g) % 2)
                        if parity == 0 and kt == 0:
                            pe.wait_ge(p_ready, A_HEADS * (nth(attend_steps, step) + 1))
                        for i in range(4):
                            last = pe.transpose(aux[:, (base + g) % 2, blk(i)], probs_of(b, 2 * i + parity)[:, blk(kt)], ident)
                        last.then_inc(pt_done, 1)
                        free_when[(base + g) % 2] = (pt_ready, base + g + 1)

                    o = free_bank(t)
                    turn(0)
                    for g, (parity, kt) in enumerate(groups):
                        if g + 1 < len(groups):
                            turn(g + 1)
                        pe.wait_ge(pt_ready, base + g + 1)
                        last = pe.matmul(o[64 * parity:64 * parity + 64, :], avt[:, kt, 0:A_DIM], pt[:, (base + g) % 2, :],
                                         start=kt == 0, stop=kt == b)
                    last.then_inc(tile_done, 1)
                elif kind == "wa":
                    pe.wait_ge(split_ready, nth(split_steps, (("attend", 1), 0)) + 1)
                    for i in range(2):
                        fm_tile(t + i, [(n, 4 * i + b) for b in range(4)], ya_hi, ya_lo)
                elif kind == "wb":
                    fm_tile(t, [(n, b) for b in range(KD)], yr_hi, yr_lo)
                elif kind == "wout":
                    fm_tile(t, [(n, b) for b in range(KD)], mg_hi, mg_lo,
                            (lambda c: (split_ready, nth(split_steps, (("mg", c), 0)) + 1)) if step[1] == 0 else None)
            ffn_up(2, "up2")
            ffn_down(1, "down2")

            for step in PLE_STEPS:
                n, t = plan.first[step]
                if step[0] == "pgate":
                    fm_tile(t, [(n, b) for b in range(KD)], u_hi, u_lo, (lambda c: (u_ready, KD * 3 + c + 1)) if step[1] == 0 else None)
                    if step[1] == 0:
                        sums(3)
                else:
                    pe.wait_ge(hid_ready, 2 * KF + 2)
                    for i in range(4):
                        fm_tile(t + i, [(n, 2 * i), (n, 2 * i + 1)], p_hi, p_lo)

            for step in GLA:
                kind = step[0]
                n, t = plan.first[step]
                if kind == "alow":
                    o = free_bank(t)
                    slabs_ready(n)
                    for k in range(KD):
                        pe.wait_ge(u_ready, KD * 4 + k + 1)
                        last = mm3(o[0:G_RANK, :], (n % RING, slice(k * G_RANK, (k + 1) * G_RANK)), u_hi[:, k, :], u_lo[:, k, :], k == 0, k == KD - 1)
                    last.then_inc(tile_done, 1)
                    sums(4)
                elif kind == "alpha":
                    pe.wait_ge(tile_freed, plan.first[("alow",)][1] + 1)
                    pe.wait_ge(pt_loaded, 32)
                    for c in range(G_HEADS):
                        free_bank(t + c)
                        pe.matmul(acc[:, (t + c) % BANKS, :], walpha[0:G_RANK, blk(c)], alow_t[0:G_RANK, :], start=True, stop=True).then_inc(tile_done, 1)
                elif kind == "gv":
                    token_tiles(t, n, G_DV, 2, 4)
                elif kind in ("gk", "gq", "gr"):
                    fm_tile(t, [(n, b) for b in range(KD)], u_hi, u_lo)
                elif kind == "gsc":
                    r = step[1]
                    pe.wait_ge(gqk_ready, r + 1)
                    claim(3)
                    for tt in range(NT):
                        last = pe.transpose(aux[:, 3, blk(tt)], up_t[:, 1, blk(tt)], ident)
                    last.then_inc(gke_done, 1)
                    free_when[3] = (gke_ready, r + 1)
                    claim(2)
                    for tt in range(NT):
                        for e in range(2):
                            tok = slice(tt * P + e * CHUNK, tt * P + (e + 1) * CHUNK)
                            last = pe.matmul(aux[e * CHUNK:(e + 1) * CHUNK, 2, tt * CHUNK:(tt + 1) * CHUNK], gki[:, tok], gqd[:, tok], start=True, stop=True)
                    last.then_inc(gs_done, 1)
                    free_when[2] = (gsc_ready, r + 1)
                elif kind == "gkv":
                    r = step[1]
                    pe.wait_ge(gke_ready, r + 1)
                    pe.wait_ge(tile_freed, plan.first[("gv", r)][1] + 2)
                    for c in range(7):
                        tt, rows = c // 2, slice((c % 2) * CHUNK, (c % 2 + 1) * CHUNK)
                        if c in (0, 1, 4, 5):
                            claim(c % 2)
                        pe.matmul(state_bank(c), gket[rows, tt, :], gvt[rows, r % 2, tt, :], start=True, stop=True).then_inc(gkv_done, 1)
                        free_when[c % 2] = (gst_ready, 7 * r + c + 1)
                elif kind == "gout":
                    r = step[1]
                    pe.wait_ge(gsc_ready, r + 1)
                    for tt in range(NT):
                        if tt % 2 == 0:
                            free_bank(t + tt // 2)
                        o = acc[:, (t + tt // 2) % BANKS, (tt % 2) * G_DV:(tt % 2 + 1) * G_DV]
                        last = pe.matmul(o, gsc[:, tt, :], gvt[:, r % 2, tt, :], start=True, stop=True)
                        for e in range(2):
                            c = 2 * tt + e
                            if c:
                                pe.wait_ge(gst_ready, 7 * r + c)
                                last = pe.matmul(o[e * CHUNK:(e + 1) * CHUNK, :], gqd[:, c * CHUNK:(c + 1) * CHUNK], gst[:, c - 1, :],
                                                 start=False, stop=True, skip_group_check=True)
                        if tt % 2:
                            last.then_inc(tile_done, 1)
                elif kind == "gt":
                    c = step[1]
                    pe.wait_ge(gon_ready, c // 2 + 1)
                    claim(2 + c % 2)
                    for tt in range(NT):
                        last = pe.transpose(aux[:, 2 + c % 2, blk(tt)], go[:, c // 2, tt, blk(c % 2)], ident)
                    last.then_inc(gt_done, 1)
                    free_when[2 + c % 2] = (split_in, nth(made_steps, (step, 0)) + 1)
                elif kind == "gwout":
                    fm_tile(t, [(n, b) for b in range(KD)], gy_hi, gy_lo,
                            (lambda c: (split_ready, nth(split_steps, (("gt", c), 0)) + 1)) if step[1] == 0 else None)
            ffn_up(5, "up3")
            ffn_down(2, "down3")
            sums(6)


def _blocks(w):
    k, m = w.shape
    return w.reshape(k // P, P, m // P, P).transpose(2, 1, 0, 3).reshape(m // P, P, k)


def _moving(w):
    k, m = w.shape
    return w.reshape(k // P, P, m).transpose(1, 0, 2).reshape(P, k // P * m)


def _pairs(a, b):
    return np.stack([_blocks(a), _blocks(b)], 1).reshape(-1, P, a.shape[0])


def _halves(w):
    return _moving(w).reshape(P, 2, SLAB).transpose(1, 0, 2)


def _shape_constants():
    consts = np.zeros((P, NCONST), np.float32)
    p = np.arange(P)
    consts[:, C_ID:C_ID + P] = np.eye(P)
    consts[:, C_MASK:C_MASK + CHUNK] = (p % CHUNK)[:, None] <= np.arange(CHUNK)[None, :]
    inv_a, inv_r = (10000.0 ** (-np.arange(n) / n) for n in (32, 64))
    consts[:, C_INV_A] = inv_a[p % 32]
    consts[:, C_INV_R] = inv_r[p % 64]
    consts[:, C_SGN_A] = np.where(p % 64 < 32, -1.0, 1.0)
    consts[:, C_SGN_R] = np.where(p < 64, -1.0, 1.0)
    log_gamma = np.log1p(-np.exp2(-5.0 - np.arange(R_HEADS)))
    i, j = np.arange(S)[None, :], p[:, None]
    seen = (i >= P) | (j < (i // CHUNK + 1) * CHUNK)
    decay = np.exp(log_gamma[:, None, None] * np.abs(i - j)) * seen * R_QK ** -0.5
    return consts, decay.astype(np.float32)


def kernel(**inputs):
    import concourse.bacc as bacc
    from concourse.bass_utils import run_bass_kernel_spmd as run

    a = {k: np.asarray(v) for k, v in inputs.items()}
    consts, decay = _shape_constants()
    w_in = a["w_in"][0]
    at, z = 0, {}
    for name, n in (("aq", 512), ("ak", 64), ("av", 64), ("iq", 512), ("ik", 64), ("iw", 8), ("rq", 512), ("rk", 512),
                    ("rv", 1024), ("rg", 1024), ("ga", 1024), ("gb", 1024)):
        z[name] = w_in[:, at:at + n]
        at += n
    z["kk"] = np.concatenate([z["ik"], z["ak"]], 1)
    tiles = {k: _blocks(z[k]) for k in ("aq", "iq", "rq", "rk", "rg", "ga", "gb", "kk")}
    tiles["wb"] = _blocks(a["w_branch_b"][0])
    tiles["wout"] = _blocks(a["w_out"][0])
    wa = _blocks(a["w_branch_a"][0])
    mix = []
    for step in MIX:
        kind = step[0]
        if kind == "rv":
            mix += list(_halves(z["rv"][:, step[1] * R_V:(step[1] + 1) * R_V]))
        elif kind == "rg":
            mix.append(tiles["rg"][2 * step[1] + step[2]])
        elif kind == "wa":
            mix.append(np.concatenate([wa[step[1]], wa[step[1] + 1]], 1))
        elif kind in tiles:
            mix.append(tiles[kind][step[1] if len(step) > 1 else 0])
    g_in = a["l0_gla_w_in_2"]
    gq, gk, gv, gr, glow = (g_in[:, i:j] for i, j in ((0, 512), (512, 1024), (1024, 2048), (2048, 3072), (3072, 3088)))
    gt = {"gq": _blocks(gq), "gk": _blocks(gk), "gr": _blocks(gr), "gwout": _blocks(a["l0_gla_w_out_2"])}
    gla = []
    for step in GLA[1:]:
        if step[0] == "gv":
            gla += list(_halves(gv[:, step[1] * G_DV:(step[1] + 1) * G_DV]))
        elif step[0] in gt:
            gla.append(gt[step[0]][step[1]])
    pgate = _blocks(a["w_ple_gate"][0])
    pproj = _blocks(a["w_ple_proj"][0]).transpose(1, 0, 2).reshape(P, 2, SLAB)
    ple = [pproj[:, s[1]] if s[0] == "pproj" else pgate[s[1]] for s in PLE_STEPS]
    up3 = a["l0_ffn_w_up_2"]

    def columns(v):
        return v.reshape(-1, P).T

    conv = a["l0_ffn_conv_w_2"]
    vectors = {"ffn1_norm": a["ffn1_norm"], "mix_norm": a["mix_norm"], "ret_gn": a["ret_gn"], "ffn2_norm": a["ffn2_norm"],
               "ple_norm": a["ple_norm"], "final_norm": a["final_norm"], "l0_norm1": a["l0_norm1_2"],
               "gla_out_norm": a["l0_gla_out_norm_2"], "l0_norm2": a["l0_norm2_2"], "final_norm_2": a["final_norm_2"],
               "b_alpha": a["l0_gla_b_alpha_2"], "conv_w0": conv[0], "conv_w1": conv[1], "conv_w2": conv[2],
               "conv_b": a["l0_ffn_conv_b_2"]}
    arrays = {
        "xT": a["x"][0].T.reshape(KD, P, S),
        "pT": a["p"][0, 0].T.reshape(2, P, S).transpose(1, 0, 2),
        "positions": np.broadcast_to(a["positions"], (P, S)),
        "vectors": np.concatenate([columns(vectors[name]) for name, _ in VECTORS], 1),
        "consts": consts,
        "decay": decay,
        "w_up1": _pairs(a["ffn1_w_gate"][0], a["ffn1_w_up"][0]),
        "w_down1": _blocks(a["ffn1_w_down"][0]),
        "w_avw": _moving(np.concatenate([z["av"], z["iw"]], 1)),
        "w_mix": np.stack(mix),
        "w_up2": _pairs(a["ffn2_w_gate"][0], a["ffn2_w_up"][0]),
        "w_down2": _blocks(a["ffn2_w_down"][0]),
        "w_ple": np.stack(ple),
        "w_alow": _moving(glow),
        "w_alpha": a["l0_gla_w_alpha_up_2"],
        "w_gla": np.stack(gla),
        "w_up3": _pairs(up3[:, :FF], up3[:, FF:]),
        "w_down3": _blocks(a["l0_ffn_w_down_2"]),
    }
    nc = bacc.Bacc("TRN2", target_bir_lowering=False, num_devices=1)
    feeds, A = {}, {}
    for name, v in arrays.items():
        v = np.ascontiguousarray(v)
        feeds[f"in_{name}"] = v
        A[name] = nc.dram_tensor(f"in_{name}", v.shape, mybir.dt.from_np(v.dtype), kind="ExternalInput").ap()
    out = nc.dram_tensor("out_xT", (KD, P, S), F32, kind="ExternalOutput").ap()
    layer_program(nc, A, out)
    r = run(nc, [feeds], core_ids=[0])
    return r.results[0]["out_xT"].reshape(D, S).T.reshape(1, S, D)
```

```python
from contextlib import ExitStack

import numpy as np
import concourse.bass as bass
from concourse import mybir

F32 = mybir.dt.float32
F32R = mybir.dt.float32r
I32 = mybir.dt.int32
ALU = mybir.AluOpType
ACT = mybir.ActivationFunctionType
AX_X = mybir.AxisListType.X

P = 128
S = 512
NT = S // P
D = 1024
KD = D // P
FF = 2816
KF = FF // P
CHUNK = 64
TOPK = min(256, S // 4)
TOPK_STEPS = 8
A_HEADS, A_DIM = 8, 64
AVW = A_DIM + A_HEADS
R_HEADS, R_QK, R_V = 4, 128, 256
G_HEADS, G_DK, G_DV, G_RANK, G_TAU = 4, 128, 256, 16, 16.0
PLE = 256
NORM_EPS, GN_EPS = 1e-6, 1e-5
NEG_BIG = -1e30
SCORE_MAX = 3.0e38
TAKEN = -3.0e38

RING = 4
BANKS = 4
SLAB = 8 * P
DOWN_SLABS = 3
DOWN_LAST = (KF - 2 * 8) * P

TWO_PI = 2.0 * np.pi
PI_A = 6.28125
PI_B = float(np.float32(np.floor((TWO_PI - PI_A) * 2 ** 21) / 2 ** 21))
PI_C = float(np.float32(TWO_PI - PI_A - PI_B))
PI_MAX = 3.1415925

VECTORS = [("ffn1_norm", KD), ("mix_norm", KD), ("ret_gn", KD), ("ffn2_norm", KD), ("ple_norm", KD),
           ("final_norm", KD), ("l0_norm1", KD), ("gla_out_norm", KD), ("l0_norm2", KD), ("final_norm_2", KD),
           ("b_alpha", 4), ("conv_w0", 2 * KF), ("conv_w1", 2 * KF), ("conv_w2", 2 * KF), ("conv_b", 2 * KF)]
COL = {name: sum(n for _, n in VECTORS[:i]) for i, (name, _) in enumerate(VECTORS)}
NCOLS = sum(n for _, n in VECTORS)
C_ID, C_MASK, C_INV_A, C_INV_R, C_SGN_A, C_SGN_R, NCONST = 0, P, P + CHUNK, P + CHUNK + 1, P + CHUNK + 2, P + CHUNK + 3, P + CHUNK + 4

MIX = [("rg", 0, 0),
       ("avw",),
       ("kk",), ("avt",),
       ("iq", 0), ("rot", "kk"),
       ("iq", 1), ("rot", "iq", 0),
       ("iq", 2), ("rot", "iq", 1),
       ("iq", 3), ("rot", "iq", 2), ("rot", "iq", 3),
       ("rq", 0),
       ("rk", 0), ("rot", "rq", 0),
       ("rg", 0, 1), ("index", 3, 0), ("rot", "rk", 0),
       ("rv", 0), ("index", 3, 1), ("index", 3, 2), ("index", 3, 3), ("topk", 3, 0),
       ("rq", 1), ("rscore", 0), ("topk", 3, 1), ("index", 2, 0), ("ry", 0),
       ("rk", 1), ("rsq", 0), ("topk", 3, 2),
       ("rg", 1, 0), ("rsum", 0), ("rot", "rq", 1), ("rfin", 0), ("rot", "rk", 1),
       ("rg", 1, 1), ("topk", 3, 3), ("index", 2, 1), ("topk", 3, 4), ("rlo", 0),
       ("rv", 1),
       ("rq", 2), ("rscore", 1), ("topk", 3, 5),
       ("rk", 2), ("index", 2, 2), ("ry", 1), ("rsq", 1), ("topk", 3, 6),
       ("rg", 2, 0), ("rsum", 1), ("rot", "rq", 2), ("topk", 3, 7),
       ("rg", 2, 1), ("rfin", 1), ("rot", "rk", 2),
       ("rv", 2), ("index", 2, 3), ("topk", 2, 0), ("rlo", 1),
       ("rq", 3), ("rscore", 2), ("index", 1, 0), ("topk", 2, 1),
       ("rk", 3), ("ry", 2), ("rsq", 2), ("index", 1, 1), ("topk", 2, 2), ("topk", 2, 3),
       ("rg", 3, 0), ("index", 1, 2),
       ("rg", 3, 1), ("rsum", 2), ("rot", "rq", 3), ("topk", 2, 4), ("index", 1, 3), ("rfin", 2),
       ("rot", "rk", 3), ("topk", 2, 5),
       ("aq", 0),
       ("rv", 3), ("rot", "aq", 0), ("topk", 2, 6), ("rlo", 2),
       ("aq", 1), ("rscore", 3), ("topk", 2, 7),
       ("aq", 2), ("ry", 3), ("rsq", 3), ("rot", "aq", 1), ("topk", 1, 0),
       ("aq", 3), ("rsum", 3), ("rot", "aq", 2), ("rfin", 3),
       ("gb", 0), ("gate", "gb", 0), ("rot", "aq", 3), ("rlo", 3), ("gate", "ga", 0), ("topk", 1, 1),
       ("ga", 0), ("logits", 3), ("topk", 1, 2), ("topk", 1, 3), ("topk", 1, 4),
       ("wb", 0), ("logits", 0), ("topk", 1, 5), ("probs", 3),
       ("gb", 1), ("attend", 3), ("gate", "gb", 1),
       ("wb", 1), ("logits", 2), ("topk", 1, 6), ("topk", 1, 7), ("probs", 0),
       ("gb", 2), ("attend", 0), ("gate", "gb", 2), ("probs", 2),
       ("wb", 2), ("attend", 2), ("logits", 1), ("probs", 1),
       ("gb", 3), ("attend", 1), ("gate", "gb", 3),
       ("wb", 3),
       ("wa", 0), ("mg", 0), ("ga", 1), ("gate", "ga", 1), ("mg", 1), ("ga", 2), ("gate", "ga", 2), ("wa", 2), ("mg", 2),
       ("ga", 3), ("gate", "ga", 3), ("mg", 3)]
for _m in range(4, KD):
    MIX += [("gb", _m), ("gate", "gb", _m), ("wb", _m), ("ga", _m), ("gate", "ga", _m)] + ([("wa", _m)] if _m % 2 == 0 else []) + [("mg", _m)]
MIX += [("wout", m) for m in range(KD)]

PLE_STEPS = [("pgate", 0), ("pgate", 1), ("pproj", 0), ("pproj", 1)] + [("pgate", m) for m in range(2, KD)]

GLA = [("alow",), ("gv", 0), ("alpha",), ("gk", 0), ("cum",), ("gq", 0), ("gpre", 0), ("gv", 1), ("gsc", 0),
       ("res", 0), ("gk", 1), ("gkv", 0), ("gq", 1), ("gout", 0), ("gpre", 1), ("gv", 2), ("gsc", 1), ("res", 1),
       ("gk", 2), ("gkv", 1), ("gq", 2), ("gout", 1), ("gn", 0), ("gpre", 2), ("gv", 3), ("gsc", 2), ("res", 2),
       ("gk", 3), ("gkv", 2), ("gq", 3), ("gout", 2), ("gn", 1), ("gpre", 3), ("gr", 0), ("gr", 1), ("gt", 0),
       ("gsc", 3), ("gt", 1), ("gr", 2), ("gkv", 3), ("gr", 3), ("gout", 3), ("gn", 2), ("gt", 2), ("gt", 3),
       ("gr", 4), ("res", 3), ("gr", 5), ("gn", 3), ("gt", 4), ("gt", 5), ("gr", 6), ("gt", 6), ("gr", 7),
       ("gt", 7)]
GLA += [("gwout", m) for m in range(KD)]

PROJECTS = {"avw": (1, 1), "rv": (2, 2), "rg": (1, 1), "kk": (1, 1), "iq": (1, 1), "rq": (1, 1), "rk": (1, 1),
            "aq": (1, 1), "attend": (0, 1), "wa": (1, 2), "ga": (1, 1), "gb": (1, 1), "wb": (1, 1), "wout": (1, 1),
            "pgate": (1, 1), "pproj": (1, 4), "alow": (1, 1), "alpha": (0, 4), "gk": (1, 1), "gq": (1, 1),
            "gv": (2, 2), "gr": (1, 1), "gout": (0, 2), "gwout": (1, 1)}
GATES = ("rg", "ga", "gb", "pgate", "gr")
ROPE = ("kk", "iq", "aq", "rq", "rk")


class Plan:

    def __init__(self):
        self.slabs = self.tiles = self.mids = 0
        self.release = []
        self.width = []
        self.first = {}

    def up(self, name):
        self.first[name] = (self.slabs, self.tiles)
        for _ in range(2 * KF):
            self.tiles += 1
            self.release.append(("tile", self.tiles))
            self.width.append(SLAB)
        self.slabs += 2 * KF

    def down(self, name):
        self.first[name] = (self.slabs, self.tiles)
        for _ in range(KD):
            self.tiles += 1
            for s in range(DOWN_SLABS - 1):
                self.mids += 1
                self.release.append(("mid", self.mids))
                self.width.append(SLAB)
            self.release.append(("tile", self.tiles))
            self.width.append(DOWN_LAST)
        self.slabs += KD * DOWN_SLABS

    def steps(self, name, steps):
        self.first[name] = (self.slabs, self.tiles)
        for step in steps:
            slabs, tiles = PROJECTS.get(step[0], (0, 0))
            self.first[step] = (self.slabs, self.tiles)
            self.tiles += tiles
            for _ in range(slabs):
                self.release.append(("tile", self.tiles))
                self.width.append({"avw": KD * AVW, "alow": KD * G_RANK}.get(step[0], SLAB))
            self.slabs += slabs


def layer_program(nc, A, out):
    plan = Plan()
    plan.up("up1")
    plan.down("down1")
    plan.steps("mix", MIX)
    plan.up("up2")
    plan.down("down2")
    plan.steps("ple", PLE_STEPS)
    plan.steps("gla", GLA)
    plan.up("up3")
    plan.down("down3")
    N = plan.slabs

    with ExitStack() as ctx:
        def sb(name, shape, dt=F32, on=ctx):
            return on.enter_context(nc.sbuf_tensor(name, shape, dt))

        def sem(name):
            return ctx.enter_context(nc.semaphore(name))

        w_raw = sb("w_raw", [P, RING, SLAB])
        w_hi = sb("w_hi", [P, RING, SLAB], F32R)
        w_lo = sb("w_lo", [P, RING, SLAB], F32R)
        h = sb("h", [P, KD, S])
        u_hi = sb("u_hi", [P, KD, S], F32R)
        u_lo = sb("u_lo", [P, KD, S], F32R)
        tmp = sb("tmp", [P, 6, S])
        side = sb("side", [P, 2, S])
        ssum = sb("ssum", [P, S])
        rstd = sb("rstd", [P, S])
        ones = sb("ones", [P, P])
        cols = sb("cols", [P, NCOLS])
        consts = sb("consts", [P, NCONST])
        eps = sb("eps", [P, 2])
        rstd_tok = sb("rstd_tok", [P, NT])
        small = sb("small", [P, 176])
        gate_t, up_t, sq = tmp[:, 0:2, :], tmp[:, 2:4, :], tmp[:, 4:6, :]
        gres, ssum2 = side[:, 0, :], side[:, 1, :]
        pt = sq
        cos_a, sin_a = side[:, 0, :], side[:, 1, :]
        neg_max, row_sum, row_max, row_inv = (small[:, c:c + 16] for c in (16, 32, 64, 80))
        v_mean = small[:, 56:64]
        top8 = small[:, 168:176]
        head_sq, head_root, head_x, head_rstd = (small[:, c:c + 16] for c in (96, 112, 128, 144))
        ident = consts[:, C_ID:C_ID + P]

        with ExitStack() as region:
            hid_hi = sb("hid_hi", [P, KF, S], F32R, region)
            hid_lo = sb("hid_lo", [P, KF, S], F32R, region)
        with ExitStack() as region:
            yr_hi = sb("yr_hi", [P, KD, S], F32R, region)
            yr_lo = sb("yr_lo", [P, KD, S], F32R, region)
            with ExitStack() as inner:
                q8 = sb("q8", [P, 4, S], F32, inner)
                ikd = sb("ikd", [P, S], F32, inner)
                akd = sb("akd", [P, S], F32, inner)
                bias = sb("bias", [P, NT * (NT + 1) // 2 * P], F32, inner)
                avt = sb("avt", [P, NT, AVW], F32, inner)
                with ExitStack() as sub:
                    cos_r = sb("cos_r", [P, S], F32, sub)
                    sin_r = sb("sin_r", [P, S], F32, sub)
                    rv = sb("rv", [P, 2, NT, R_V], F32, sub)
                    rqk = sb("rqk", [P, 2, S], F32, sub)
                    wts = sb("wts", [P, NT * (NT + 1) // 2 * P], F32, sub)
                    dec = sb("dec", [P, S], F32, sub)
                    srg = sb("srg", [P, 2, 2, S], F32, sub)
                    y_sq = sb("y_sq", [P, 2, S], F32, sub)
                with ExitStack() as sub:
                    probs = sb("probs", [P, 5 * 2 * S], F32, sub)
                    ya_hi = sb("ya_hi", [P, 4, S], F32R, sub)
                    ya_lo = sb("ya_lo", [P, 4, S], F32R, sub)
                    gated_b = sb("gated_b", [P, S], F32, sub)
            with ExitStack() as inner:
                mg_hi = sb("mg_hi", [P, KD, S], F32R, inner)
                mg_lo = sb("mg_lo", [P, KD, S], F32R, inner)
        with ExitStack() as region:
            gy_hi = sb("gy_hi", [P, KD, S], F32R, region)
            gy_lo = sb("gy_lo", [P, KD, S], F32R, region)
            gcum = sb("gcum", [P, G_HEADS, S], F32, region)
            with ExitStack() as inner:
                proj = sb("proj", [P, KD, S], F32, inner)
                p_raw = sb("p_raw", [P, 2, S], F32, inner)
                p_hi = sb("p_hi", [P, 2, S], F32R, inner)
                p_lo = sb("p_lo", [P, 2, S], F32R, inner)
            with ExitStack() as inner:
                gvt = sb("gvt", [P, 2, NT, G_DV], F32, inner)
                gkq = sb("gkq", [P, 2, S], F32, inner)
                gki = sb("gki", [P, S], F32, inner)
                gqd = sb("gqd", [P, S], F32, inner)
                gket = sb("gket", [P, NT, P], F32, inner)
                gsc = sb("gsc", [P, NT, P], F32, inner)
                gst = sb("gst", [P, 7, G_DV], F32, inner)
                go = sb("go", [P, G_HEADS, NT, G_DV], F32, inner)
                walpha = sb("walpha", [P, 4 * P], F32, inner)
                alow_t = sb("alow_t", [P, S], F32, inner)

        acc = ctx.enter_context(nc.psum_tensor("acc", [P, BANKS, S], F32))
        aux = ctx.enter_context(nc.psum_tensor("aux", [P, 4, S], F32))

        raw_loaded = [sem(f"raw_loaded{i}") for i in range(RING)]
        x_loaded = [sem(f"x_loaded{i}") for i in range(KD)]
        vec_loaded = sem("vec_loaded")
        consts_loaded = sem("consts_loaded")
        pos_loaded = sem("pos_loaded")
        dec_loaded = sem("dec_loaded")
        ple_loaded = sem("ple_loaded")
        out_stored = sem("out_stored")
        consts_set = sem("consts_set")
        hi_ready = sem("hi_ready")
        lo_ready = sem("lo_ready")
        slab_used = sem("slab_used")
        tile_done = sem("tile_done")
        tile_freed = sem("tile_freed")
        u_hi_ready = sem("u_hi_ready")
        u_ready = sem("u_ready")
        sq_ready = sem("sq_ready")
        sq_added = sem("sq_added")
        stat_done = sem("stat_done")
        ms2_ready = sem("ms2_ready")
        root_ready = sem("root_ready")
        rstd_ready = sem("rstd_ready")
        dve_step = sem("dve_step")
        gate_act = sem("gate_act")
        prod_ready = sem("prod_ready")
        prod_hi = sem("prod_hi")
        hid_ready = sem("hid_ready")
        conv_step = sem("conv_step")
        conv_done = sem("conv_done")
        angle_ready = sem("angle_ready")
        table_ready = sem("table_ready")
        swapped = [sem("swapped0"), sem("swapped1")]
        rotated = sem("rotated")
        rope_ready = sem("rope_ready")
        keys_copied = sem("keys_copied")
        avt_done = sem("avt_done")
        avt_ready = sem("avt_ready")
        idx_scored = sem("idx_scored")
        idx_relu = sem("idx_relu")
        idx_added = sem("idx_added")
        lg_done = sem("lg_done")
        lg_read = sem("lg_read")
        neg_ready = sem("neg_ready")
        exp_done = sem("exp_done")
        p_ready = sem("p_ready")
        pt_done = sem("pt_done")
        pt_ready = sem("pt_ready")
        mean_ready = sem("mean_ready")
        rv_ready = sem("rv_ready")
        rs_done = sem("rs_done")
        rw_ready = sem("rw_ready")
        ry_done = sem("ry_done")
        ry_sq = sem("ry_sq")
        ry_sum = sem("ry_sum")
        var_ready = sem("var_ready")
        ry_freed = sem("ry_freed")
        yr_ready = sem("yr_ready")
        split_in = sem("split_in")
        split_hi = sem("split_hi")
        split_ready = sem("split_ready")
        p_split = sem("p_split")
        h_updated = sem("h_updated")
        out_ready = sem("out_ready")
        al_ln = sem("al_ln")
        al_ready = sem("al_ready")
        gd_ready = sem("gd_ready")
        ge_ready = sem("ge_ready")
        gqk_ready = sem("gqk_ready")
        gke_done = sem("gke_done")
        gke_ready = sem("gke_ready")
        gs_done = sem("gs_done")
        gsc_ready = sem("gsc_ready")
        gkv_done = sem("gkv_done")
        gst_ready = sem("gst_ready")
        go_sq = sem("go_sq")
        gon_ready = sem("gon_ready")
        gt_done = sem("gt_done")

        branch_b = [gated_b[:, :], side[:, 0, :], side[:, 1, :], ssum[:, :]]

        SQ = [0, 8, 16, 24, 32, 48, 56, 64]
        rope_steps = [s for s in MIX if s[0] in ROPE]
        gate_steps = [s[1:] if s[0] == "gate" else s for s in MIX + PLE_STEPS + GLA if s[0] in ("rg", "gate", "pgate", "gr")]
        split_steps = []
        for s in MIX:
            if s[0] == "rlo":
                split_steps += [(s, 0), (s, 1)]
            elif s[0] in ("attend", "mg"):
                split_steps += [(s, 0)]
        split_steps += [(("gt", c), 0) for c in range(KD)]
        made_steps = [s for s in split_steps if s[0][0] != "attend"]
        lo_steps = [s for s in split_steps if s[0][0] != "rlo"]
        index_units = {b: A_HEADS * i for i, b in enumerate((3, 2, 1))}
        logit_steps = [s for s in MIX if s[0] == "logits"]
        attend_steps = [s for s in MIX if s[0] == "attend"]
        pt_base = {}
        for s in attend_steps:
            pt_base[s] = sum(2 * (t[1] + 1) for t in attend_steps[:attend_steps.index(s)])
        FFNS = 3

        def nth(steps, step):
            return steps.index(step)

        def gates_before(step):
            before = {"rg": 1, "ga": 1, "gb": 1, "pgate": 2, "gr": 2}[step[0]]
            return before * KF + nth(gate_steps, step)

        z_gate = tmp.rearrange("p a b -> p (a b)")[:, 2 * S:3 * S + 2]
        z_up = tmp.rearrange("p a b -> p (a b)")[:, 3 * S + 2:4 * S + 4]
        TABLES = [(C_INV_A, 0.25, cos_a, None), (C_INV_A, 0.0, sin_a, C_SGN_A),
                  (C_INV_R, 0.25, up_t[:, 0, :], None), (C_INV_R, 0.0, up_t[:, 1, :], C_SGN_R)]
        GATES_FFN = [0, KF + nth(gate_steps, ("pgate", 0)), 2 * KF + len(gate_steps)]
        bias_at = {0: 0, 1: P, 2: 3 * P, 3: 6 * P}
        wts_at = {0: 0, 1: 4 * P, 2: 7 * P, 3: 9 * P}
        probs_at = {3: 0, 0: 8 * S, 2: 0, 1: 6 * S}

        def probs_of(b, hd):
            n = (b + 1) * P
            return probs[:, probs_at[b] + hd * n:probs_at[b] + (hd + 1) * n]

        def state_bank(c):
            at = (c // 2) % 2 * G_DV
            return aux[:, c // 4 * 2 + c % 2, at:at + G_DV]

        def blk(b):
            return slice(b * P, (b + 1) * P)

        def load_count(n):
            return 16 * (n // RING + 1)

        block = ctx.enter_context(nc.Block())

        @block.sync
        def _(sp):
            def load(n, src):
                if n >= RING:
                    sp.wait_ge(lo_ready, n - RING + 1)
                sp.dma_start(w_raw[:, n % RING, 0:plan.width[n]], src).then_inc(raw_loaded[n % RING], 16)

            def load_up(name, w, first=0):
                n0 = plan.first[name][0]
                with sp.Fori(first // RING, 2 * KF // RING) as i:
                    for j in range(RING):
                        sp.wait_ge(lo_ready, i * RING + (n0 + j - RING + 1))
                        sp.dma_start(w_raw[:, (n0 + j) % RING, :], w[i * RING + j]).then_inc(raw_loaded[(n0 + j) % RING], 16)

            def load_down(name, w):
                n0 = plan.first[name][0]
                with sp.Fori(0, 2) as i:
                    for j in range(4 * DOWN_SLABS):
                        width, at = plan.width[n0 + j], (j % DOWN_SLABS) * SLAB
                        sp.wait_ge(lo_ready, i * (4 * DOWN_SLABS) + (n0 + j - RING + 1))
                        sp.dma_start(w_raw[:, (n0 + j) % RING, 0:width],
                                     w[i * 4 + j // DOWN_SLABS][:, at:at + width]).then_inc(raw_loaded[(n0 + j) % RING], 16)

            load(0, A["w_up1"][0])
            sp.dma_start(cols[:, :], A["vectors"]).then_inc(vec_loaded, 16)
            for c in range(KD):
                sp.dma_start(h[:, c, :], A["xT"][c]).then_inc(x_loaded[c], 16)
                if c == 3:
                    load(1, A["w_up1"][1])
            for n in range(2, RING):
                load(n, A["w_up1"][n])
            sp.dma_start(consts[:, :], A["consts"]).then_inc(consts_loaded, 16)
            load_up("up1", A["w_up1"], RING)
            load_down("down1", A["w_down1"])

            mix0, avw = plan.first["mix"][0], plan.first[("avw",)][0]
            mix_end = plan.first["up2"][0]
            loaded = [mix0]

            def load_mix(upto):
                while loaded[0] < min(upto, mix_end):
                    n = loaded[0]
                    load(n, A["w_avw"] if n == avw else A["w_mix"][n - mix0 - (n > avw)])
                    loaded[0] += 1
            load_mix(mix0 + 3)
            sp.wait_ge(tile_done, plan.first["mix"][1])
            sp.dma_start(dec[:, :], A["decay"][0]).then_inc(dec_loaded, 16)
            for step in MIX:
                n, t = plan.first[step]
                load_mix(n + 6)
                if step[0] in ROPE:
                    z = nth(rope_steps, step)
                    half = 64 if step[0] in ("rq", "rk") else 32
                    sp.wait_ge(tile_freed, t + 1)
                    for g in range(P // half):
                        to, of = g * half, (g ^ 1) * half
                        sp.dma_start(up_t[to:to + half, z % 2, :], gate_t[of:of + half, z % 2, :]).then_inc(swapped[z % 2], 16)
                if step == ("rot", "kk"):
                    sp.wait_ge(rope_ready, 1)
                    for rows in (slice(0, 64), slice(64, 128)):
                        sp.dma_start(ikd[rows, :], wts[0:64, 0:S]).then_inc(keys_copied, 16)
                        sp.dma_start(akd[rows, :], wts[64:128, 0:S]).then_inc(keys_copied, 16)
                if step[0] == "ry" and step[1] + 1 < R_HEADS:
                    sp.wait_ge(rw_ready, NT * (step[1] + 1))
                    sp.dma_start(dec[:, :], A["decay"][step[1] + 1]).then_inc(dec_loaded, 16)
            load_up("up2", A["w_up2"])
            load_down("down2", A["w_down2"])
            ple0 = plan.first["ple"][0]
            for n in range(ple0, ple0 + 4):
                load(n, A["w_ple"][n - ple0])
            sp.wait_ge(tile_done, plan.first["ple"][1])
            sp.dma_start(p_raw[:, :, :], A["pT"]).then_inc(ple_loaded, 16)
            for n in range(ple0 + 4, plan.first["gla"][0]):
                load(n, A["w_ple"][n - ple0])
            gla0 = plan.first["gla"][0]
            load(gla0, A["w_alow"])
            for n in range(gla0 + 1, gla0 + RING):
                load(n, A["w_gla"][n - gla0 - 1])
            sp.wait_ge(h_updated, KD)
            sp.dma_start(walpha[0:G_RANK, :], A["w_alpha"]).then_inc(ple_loaded, 16)
            for n in range(gla0 + RING, plan.first["up3"][0]):
                load(n, A["w_gla"][n - gla0 - 1])
            load_up("up3", A["w_up3"])
            load_down("down3", A["w_down3"])
            for c in range(KD):
                sp.wait_ge(out_ready, c + 1)
                sp.dma_start(out[c], h[:, c, :]).then_inc(out_stored, 16)
            sp.wait_ge(out_stored, 16 * KD)

        @block.gpsimd
        def _(pool):
            pool.memset(ones[:, :], 1.0).then_inc(consts_set, 1)
            pool.memset(eps[:, 0:1], NORM_EPS).then_inc(consts_set, 1)
            pool.memset(eps[:, 1:2], GN_EPS).then_inc(consts_set, 1)

            def lo_part(slot, width, count):
                pool.wait_ge(hi_ready, count)
                pool.tensor_tensor(w_lo[:, slot, 0:width], w_raw[:, slot, 0:width], w_hi[:, slot, 0:width].bitcast(F32),
                                   ALU.subtract).then_inc(lo_ready, 1)

            def lo_run(n0, n1):
                rounds = (n1 - n0) // RING
                if rounds:
                    with pool.Fori(0, rounds) as i:
                        for j in range(RING):
                            lo_part((n0 + j) % RING, SLAB, i * RING + (n0 + j + 1))
                for n in range(n0 + rounds * RING, n1):
                    lo_part(n % RING, SLAB, n + 1)

            def lo_down(n0):
                with pool.Fori(0, 2) as i:
                    for j in range(4 * DOWN_SLABS):
                        lo_part((n0 + j) % RING, plan.width[n0 + j], i * (4 * DOWN_SLABS) + (n0 + j + 1))

            def rotate(of):
                kind, z = of[0], nth(rope_steps, of)
                cos, sin = (cos_r[:, :], sin_r[:, :]) if kind in ("rq", "rk") else (cos_a, sin_a)
                dst = {"kk": lambda: wts[:, 0:S], "iq": lambda: q8[:, of[1], :], "aq": lambda: q8[:, of[1], :],
                       "rq": lambda: rqk[:, 0, :], "rk": lambda: rqk[:, 1, :]}[kind]()
                x, y = gate_t[:, z % 2, :], up_t[:, z % 2, :]
                pool.wait_ge(tile_freed, plan.first[of][1] + 1)
                if kind in ("rq", "rk") and of[1]:
                    pool.wait_ge(rs_done, NT * of[1])
                if kind == "aq":
                    pool.wait_ge(idx_scored, A_HEADS * len(index_units))
                pool.tensor_tensor(dst, x, cos, ALU.mult)
                pool.wait_ge(swapped[z % 2], 16 * sum(2 if s[0] in ("rq", "rk") else 4 for s in rope_steps[z % 2:z + 1:2]))
                pool.tensor_tensor(y, y, sin, ALU.mult).then_inc(rotated, 1)
                pool.wait_ge(rotated, z + 1)
                pool.tensor_tensor(dst, dst, y, ALU.add).then_inc(rope_ready, 1)

            def at(name):
                return plan.first[name][0]
            lo_run(0, at("down1"))
            lo_down(at("down1"))
            n = at("mix")
            for step in MIX:
                slabs = PROJECTS.get(step[0], (0, 0))[0]
                while n < plan.first[step][0] + slabs + RING and n < at("up2"):
                    lo_part(n % RING, plan.width[n], n + 1)
                    n += 1
                if step[0] == "rv":
                    for i in range(2):
                        pool.wait_ge(mean_ready, 2 * step[1] + i + 1)
                        part, mean = rv[:, step[1] % 2, 2 * i:2 * i + 2, :], v_mean[:, 4 * (step[1] % 2) + 2 * i:4 * (step[1] % 2) + 2 * i + 2]
                        pool.tensor_tensor(part, part, mean.unsqueeze(2).to_broadcast([P, 2, R_V]), ALU.add).then_inc(rv_ready, 1)
                if step[0] == "rlo":
                    for half in range(2):
                        pool.wait_ge(split_hi, nth(split_steps, (step, half)) + 1)
                        c = 2 * step[1] + half
                        pool.tensor_tensor(yr_lo[:, c, :], y_sq[:, half, :], yr_hi[:, c, :].bitcast(F32), ALU.subtract).then_inc(yr_ready, 1)
                if step[0] == "rot":
                    rotate(step[1:])
            lo_run(at("up2"), at("down2"))
            lo_down(at("down2"))
            lo_run(at("ple"), at("gla"))
            lo_part(at("gla") % RING, plan.width[at("gla")], at("gla") + 1)
            lo_run(at("gla") + 1, at("down3"))
            lo_down(at("down3"))

        @block.scalar
        def _(act):
            done = [0]

            def hi_part(slot, width, count, used):
                act.wait_ge(raw_loaded[slot], count)
                if used is not None:
                    act.wait_ge(used[0], used[1])
                act.activation(w_hi[:, slot, 0:width], w_raw[:, slot, 0:width], ACT.Copy).then_inc(hi_ready, 1)

            def split_slabs(upto):
                while done[0] < min(upto, N):
                    n = done[0]
                    used = None
                    if n >= RING:
                        kind, count = plan.release[n - RING]
                        used = (tile_done if kind == "tile" else slab_used, count)
                    hi_part(n % RING, plan.width[n], load_count(n), used)
                    done[0] += 1

            def norm_chunk(k, c, gain, tile=None):
                if tile is not None:
                    act.wait_ge(tile_freed, tile + 1)
                if gain is not None:
                    act.activation(u_hi[:, c, :], h[:, c, :], ACT.Copy, scale=gain).then_inc(u_hi_ready, 1)
                e = SQ[k] + c
                if e >= 2:
                    act.wait_ge(sq_added, e - 1)
                act.activation(sq[:, e % 2, :], h[:, c, :], ACT.Square).then_inc(sq_ready, 1)

            def root(k):
                act.wait_ge(stat_done, k + 1)
                act.activation(sq[:, 1, :], aux[:, 0, :], ACT.Sqrt, bias=eps[:, 0:1], scale=1.0 / D).then_inc(root_ready, 1)

            def ffn_up(f, name, conv=False):
                n0, t0 = plan.first[name]

                def pair(b, i2, i4, split_a, split_b):
                    if conv:
                        split_a()
                        act.wait_ge(conv_done, i4 + (2 * b + 1))
                        act.activation(tmp[:, 0, :], tmp[:, 0, :], ACT.Silu).then_inc(gate_act, 1)
                    else:
                        split_a()
                        act.wait_ge(tile_freed, i4 + (t0 + 2 * b + 1))
                        act.activation(gate_t[:, b, :], gate_t[:, b, :], ACT.Silu).then_inc(gate_act, 1)
                    act.wait_ge(prod_ready, i2 + (f * KF + b + 1))
                    src = tmp[:, 1, :] if conv else up_t[:, b, :]
                    act.activation(hid_hi[:, i2 + b, :], src, ACT.Copy).then_inc(prod_hi, 1)
                    split_b()

                rounds = KF // 2
                with act.Fori(0, rounds - 1) as i:
                    for b in range(2):
                        def ahead(j):
                            n = n0 + RING + j
                            hi_part(n % RING, SLAB, i * 16 + load_count(n), (tile_done, i * 4 + (t0 + j + 1)))
                        pair(b, i * 2, i * 4, lambda: ahead(2 * b), lambda: ahead(2 * b + 1))
                done[0] = n0 + 4 * rounds
                for b in range(2):
                    p = 2 * (rounds - 1) + b
                    pair(b, 2 * (rounds - 1), 4 * (rounds - 1), lambda: split_slabs(n0 + 2 * p + 5), lambda: split_slabs(n0 + 2 * p + 6))

            def ffn_down(name, k, gain):
                n0, t0 = plan.first[name]
                for m in range(KD):
                    if m < KD - 1:
                        split_slabs(n0 + DOWN_SLABS * (m + 1) + RING)
                    norm_chunk(k, m, gain(m), t0 + m)
                    if m == KD - 1:
                        split_slabs(n0 + DOWN_SLABS * (m + 1) + RING)
                    if name == "down1" and 1 <= m <= len(TABLES):
                        table(m - 1)

            def table(i):
                dst, scale = TABLES[i][2:]
                act.wait_ge(angle_ready, i + 1)
                act.activation(dst, gate_t[:, 1, :], ACT.Sin, scale=1.0 if scale is None else consts[:, scale:scale + 1]).then_inc(table_ready, 1)

            def split_to_hi(step, half, dst, src):
                act.wait_ge(split_in, nth(made_steps, (step, half)) + 1)
                act.activation(dst, src, ACT.Copy).then_inc(split_hi, 1)

            def col(name, c):
                return cols[:, COL[name] + c:COL[name] + c + 1]

            split_slabs(1)
            act.wait_ge(vec_loaded, 16)
            for c in range(KD):
                act.wait_ge(x_loaded[c], 16)
                act.activation(u_hi[:, c, :], h[:, c, :], ACT.Copy, scale=col("ffn1_norm", c)).then_inc(u_hi_ready, 1)
            split_slabs(2)
            for c in range(KD):
                norm_chunk(0, c, None)
                if c in (3, 7):
                    split_slabs(3 + c // 4)
            act.wait_ge(consts_set, 3)
            root(0)
            ffn_up(0, "up1")
            act.wait_ge(hid_ready, KF)
            act.dma_start(gate_t[:, 0, :].bitcast(I32), A["positions"]).then_inc(pos_loaded, 16)
            ffn_down("down1", 1, lambda m: col("mix_norm", m))
            act.wait_ge(stat_done, 2)
            act.activation(small[:, 0:NT], aux[:, 1, 0:NT], ACT.Sqrt, bias=eps[:, 0:1], scale=1.0 / D)
            act.activation(sq[:, 1, :], aux[:, 0, :], ACT.Sqrt, bias=eps[:, 0:1], scale=1.0 / D).then_inc(root_ready, 1)

            for step in MIX:
                kind = step[0]
                n, t = plan.first[step]
                if kind in GATES:
                    split_slabs(n + PROJECTS[kind][0] + RING)
                if kind == "rg":
                    buf = srg[:, step[1] % 2, step[2], :]
                    act.wait_ge(tile_freed, t + 1)
                    act.activation(buf, buf, ACT.Silu).then_inc(gate_act, 1)
                elif kind == "gate":
                    buf = up_t[:, 0 if step[1] == "ga" else 1, :]
                    act.wait_ge(tile_freed, plan.first[step[1:]][1] + 1)
                    act.activation(buf, buf, ACT.Sigmoid).then_inc(gate_act, 1)
                elif kind == "index":
                    nk = (step[1] + 1) * P
                    for hd in range(2 * step[2], 2 * step[2] + 2):
                        j = index_units[step[1]] + hd
                        act.wait_ge(idx_scored, j + 1)
                        if j >= 2:
                            act.wait_ge(idx_added, j - 1)
                        act.activation(sq[:, j % 2, 0:nk], aux[:, 2 + j % 2, 0:nk], ACT.Relu, scale=A_DIM ** -0.5).then_inc(idx_relu, 1)
                elif kind == "rsq":
                    act.wait_ge(ry_done, step[1] + 1)
                    for half in range(2):
                        if step[1]:
                            act.wait_ge(yr_ready, 2 * step[1])
                        act.activation(y_sq[:, half, :], aux[:, half, :], ACT.Square).then_inc(ry_sq, 1)
                elif kind == "rsum":
                    act.wait_ge(var_ready, step[1] + 1)
                    act.activation(y_sq[:, 1, :], y_sq[:, 0, :], ACT.Sqrt).then_inc(root_ready, 1)
                elif kind == "rlo":
                    for half in range(2):
                        split_to_hi(step, half, yr_hi[:, 2 * step[1] + half, :], y_sq[:, half, :])
                elif kind == "logits":
                    b, i = step[1], nth(logit_steps, step)
                    act.wait_ge(neg_ready, i + 1)
                    for hd in range(A_HEADS):
                        act.activation(probs_of(b, hd), probs_of(b, hd), ACT.Exp, bias=neg_max[:, 8 * (i % 2) + hd:8 * (i % 2) + hd + 1],
                                       accum_out=row_sum[:, 8 * (i % 2) + hd:8 * (i % 2) + hd + 1]).then_inc(exp_done, 1)
                elif kind == "attend":
                    b = step[1]
                    for g in range(2 * (b + 1)):
                        gg = pt_base[step] + g
                        act.wait_ge(pt_done, gg + 1)
                        act.activation(pt[:, gg % 2, :], aux[:, gg % 2, :], ACT.Copy).then_inc(pt_ready, 1)
                    act.wait_ge(tile_freed, t + 1)
                    act.activation(ya_hi[:, :, blk(b)], tmp[:, 0, :].rearrange("p (c q) -> p c q", c=4), ACT.Copy).then_inc(split_hi, 1)
                elif kind == "mg":
                    split_to_hi(step, 0, mg_hi[:, step[1], :], gate_t[:, step[1] % 2, :])
                elif kind == "wout":
                    norm_chunk(2, step[1], col("ffn2_norm", step[1]), t)
                split_slabs(n + PROJECTS.get(kind, (0, 0))[0] + RING)
            root(6)
            ffn_up(1, "up2")
            ffn_down("down2", 3, lambda m: col("ple_norm", m))
            act.wait_ge(ple_loaded, 16)
            for c in range(2):
                act.activation(p_hi[:, c, :], p_raw[:, c, :], ACT.Copy).then_inc(p_split, 1)
            root(7)

            def gla_squares(m):
                act.wait_ge(h_updated, m + 1)
                for e, scale in ((0, 1.0), (1, col("final_norm", m))):
                    act.wait_ge(sq_added, SQ[4] + 2 * m + e - 1)
                    act.activation(sq[:, e, :], h[:, m, :], ACT.Square, scale=scale).then_inc(sq_ready, 1)

            def gla_hi(c):
                act.wait_ge(h_updated, c + 1)
                act.activation(u_hi[:, c, :], h[:, c, :], ACT.Copy, scale=small[:, 48 + c:49 + c]).then_inc(u_hi_ready, 1)

            for step in PLE_STEPS:
                n, t = plan.first[step]
                if step[0] == "pgate":
                    m = step[1]
                    if m == KD - 1:
                        act.wait_ge(tile_done, t + 1)
                        for c in range(3):
                            gla_hi(c)
                    split_slabs(n + PROJECTS["pgate"][0] + RING)
                    act.wait_ge(tile_freed, t + 1)
                    act.activation(gate_t[:, m % 2, :], gate_t[:, m % 2, :], ACT.Sigmoid).then_inc(gate_act, 1)
                    if 2 <= m < KD - 1:
                        gla_squares(m)
                elif step[1] == 1:
                    gla_squares(0)
                    gla_squares(1)
                split_slabs(n + PROJECTS[step[0]][0] + RING)
            for c in range(3, KD):
                gla_hi(c)
            gla_squares(KD - 1)
            act.wait_ge(ms2_ready, 1)
            act.activation(sq[:, 1, :], sq[:, 0, :], ACT.Sqrt)
            act.activation(small[:, 4:4 + NT], small[:, 12:12 + NT], ACT.Sqrt).then_inc(root_ready, 1)
            act.activation(ssum2, gres, ACT.Sqrt).then_inc(root_ready, 1)

            for step in GLA:
                kind = step[0]
                n, t = plan.first[step]
                if kind in GATES:
                    split_slabs(n + PROJECTS[kind][0] + RING)
                if kind == "alpha":
                    for c in range(G_HEADS):
                        act.wait_ge(tile_freed, t + c + 1)
                        act.activation(tmp[:, c, :], gcum[:, c, :], ACT.Abs).then_inc(al_ln, 1)
                    for c in range(G_HEADS):
                        act.wait_ge(al_ln, c + 1)
                        act.activation(tmp[:, c, :], tmp[:, c, :], ACT.Exp, scale=-1.0).then_inc(al_ln, 1)
                    for c in range(G_HEADS):
                        act.wait_ge(al_ln, G_HEADS + c + 1)
                        act.activation(tmp[:, c, :], tmp[:, c, :], ACT.Ln, bias=ones[:, 0:1]).then_inc(al_ln, 1)
                elif kind == "gpre":
                    r = step[1]
                    act.wait_ge(al_ready, G_HEADS)
                    if r:
                        act.wait_ge(gst_ready, 7 * r)
                    act.activation(gate_t[:, 0, :], gcum[:, r, :], ACT.Exp, scale=1.0 / G_TAU).then_inc(ge_ready, 1)
                    act.activation(gate_t[:, 1, :], gcum[:, r, :], ACT.Exp, scale=-1.0 / G_TAU).then_inc(ge_ready, 1)
                    act.wait_ge(gd_ready, r + 1)
                    act.activation(up_t[:, 0, :], up_t[:, 0, :], ACT.Exp, scale=1.0 / G_TAU).then_inc(ge_ready, 1)
                elif kind == "gsc":
                    r = step[1]
                    act.wait_ge(gke_done, r + 1)
                    if r:
                        act.wait_ge(gkv_done, 7 * r)
                    act.activation(gket[:, :, :], aux[:, 3, :].rearrange("p (a b) -> p a b", a=NT), ACT.Copy).then_inc(gke_ready, 1)
                elif kind == "gout":
                    r = step[1]
                    for tt in range(NT):
                        act.wait_ge(tile_freed, t + tt // 2 + 1)
                        if NT * r + tt >= 2:
                            act.wait_ge(go_sq, NT * r + tt - 1)
                        act.activation(sq[:, tt % 2, 0:G_DV], go[:, r, tt, :], ACT.Square,
                                       accum_out=head_sq[:, NT * r + tt:NT * r + tt + 1]).then_inc(go_sq, 1)
                    act.wait_ge(go_sq, NT * (r + 1))
                    act.activation(head_root[:, NT * r:NT * (r + 1)], head_sq[:, NT * r:NT * (r + 1)], ACT.Sqrt,
                                   bias=eps[:, 0:1], scale=1.0 / G_DV).then_inc(root_ready, 1)
                elif kind == "gr":
                    act.wait_ge(tile_freed, t + 1)
                    act.activation(gkq[:, step[1] % 2, :], gkq[:, step[1] % 2, :], ACT.Silu).then_inc(gate_act, 1)
                elif kind == "gt":
                    split_to_hi(step, 0, gy_hi[:, step[1], :], up_t[:, step[1] % 2, :])
                elif kind == "gwout":
                    norm_chunk(5, step[1], col("l0_norm2", step[1]), t)
                split_slabs(n + PROJECTS.get(kind, (0, 0))[0] + RING)
            root(9)
            ffn_up(2, "up3", conv=True)
            ffn_down("down3", 6, lambda m: None)
            root(10)

        @block.vector
        def _(dve):
            step_no = [0]

            def link(ins):
                step_no[0] += 1
                ins.then_inc(dve_step, 1)
                dve.wait_ge(dve_step, step_no[0])

            def col(name, c):
                return cols[:, COL[name] + c:COL[name] + c + 1]

            def norm_chunk(k, c, gain):
                if gain is not None:
                    u_lo_chunk(k, c, gain)
                e = SQ[k] + c
                dve.wait_ge(sq_ready, e + 1)
                add_squares(ssum, e, c == 0)

            def u_lo_chunk(k, c, gain):
                dve.wait_ge(u_hi_ready, KD * k + c + 1)
                dve.scalar_tensor_tensor(u_lo[:, c, :], h[:, c, :], gain, u_hi[:, c, :].bitcast(F32),
                                         ALU.mult, ALU.subtract).then_inc(u_ready, 1)

            def add_squares(total, e, first):
                if first:
                    dve.tensor_copy(total[:, :], sq[:, e % 2, :]).then_inc(sq_added, 1)
                else:
                    dve.wait_ge(sq_added, e)
                    dve.tensor_tensor(total[:, :], total[:, :], sq[:, e % 2, :], ALU.add).then_inc(sq_added, 1)

            def inverse_root(dst, ms, scale, epsilon, x, root):
                link(dve.tensor_scalar(x, ms, scale, epsilon, ALU.mult, ALU.add))
                return newton(dst, x, root)

            def newton(dst, x, root):
                link(dve.reciprocal(root, root))
                link(dve.tensor_tensor(x, x, root, ALU.mult))
                link(dve.tensor_tensor(x, x, root, ALU.mult))
                link(dve.tensor_scalar(x, x, -0.5, 1.5, ALU.mult, ALU.add))
                return dve.tensor_tensor(dst, x, root, ALU.mult)

            def rstd_of_norm(roots, count):
                dve.wait_ge(root_ready, roots)
                inverse_root(rstd[:, :], aux[:, 0, :], 1.0 / D, NORM_EPS, sq[:, 0, :], sq[:, 1, :]).then_inc(rstd_ready, 1)
                dve.wait_ge(rstd_ready, count)

            def ffn_up(f, name):
                t0 = plan.first[name][1]
                with dve.Fori(0, KF // 2) as i:
                    for b in range(2):
                        dve.wait_ge(tile_done, i * 4 + (t0 + 2 * b + 1))
                        dve.tensor_tensor(gate_t[:, b, :], acc[:, (t0 + 2 * b) % BANKS, :], rstd[:, :], ALU.mult).then_inc(tile_freed, 1)
                        dve.wait_ge(tile_done, i * 4 + (t0 + 2 * b + 2))
                        dve.tensor_tensor(up_t[:, b, :], acc[:, (t0 + 2 * b + 1) % BANKS, :], rstd[:, :], ALU.mult).then_inc(tile_freed, 1)
                        dve.wait_ge(gate_act, i * 2 + (GATES_FFN[f] + b + 1))
                        dve.wait_ge(tile_freed, i * 4 + (t0 + 2 * b + 2))
                        dve.tensor_tensor(up_t[:, b, :], gate_t[:, b, :], up_t[:, b, :], ALU.mult).then_inc(prod_ready, 1)
                        dve.wait_ge(prod_hi, i * 2 + (f * KF + b + 1))
                        dve.tensor_tensor(hid_lo[:, i * 2 + b, :], up_t[:, b, :], hid_hi[:, i * 2 + b, :].bitcast(F32),
                                          ALU.subtract).then_inc(hid_ready, 1)

            def conv_up(f, name):
                t0 = plan.first[name][1]
                dve.memset(z_gate[:, 0:2], 0.0)
                dve.memset(z_up[:, 0:2], 0.0)

                def conv_col(name, i2, b, off):
                    return cols[:, bass.ds(i2 + (COL[name] + off + b), 1)]

                with dve.Fori(0, KF // 2) as i:
                    for b in range(2):
                        for part, z in enumerate((z_gate, z_up)):
                            c = 2 * b + part
                            dve.wait_ge(tile_done, i * 4 + (t0 + c + 1))
                            dve.tensor_tensor(z[:, 2:2 + S], acc[:, (t0 + c) % BANKS, :], rstd[:, :], ALU.mult).then_inc(tile_freed, 1)
                            dve.wait_ge(tile_freed, i * 4 + (t0 + c + 1))
                            dve.tensor_scalar(tmp[:, part, :], z[:, 2:2 + S], conv_col("conv_w2", i * 2, b, part * KF),
                                              conv_col("conv_b", i * 2, b, part * KF), ALU.mult, ALU.add).then_inc(conv_step, 1)
                            dve.wait_ge(conv_step, i * 8 + (2 * c + 1))
                            dve.scalar_tensor_tensor(tmp[:, part, :], z[:, 1:1 + S], conv_col("conv_w1", i * 2, b, part * KF),
                                                     tmp[:, part, :], ALU.mult, ALU.add).then_inc(conv_step, 1)
                            dve.wait_ge(conv_step, i * 8 + (2 * c + 2))
                            dve.scalar_tensor_tensor(tmp[:, part, :], z[:, 0:S], conv_col("conv_w0", i * 2, b, part * KF),
                                                     tmp[:, part, :], ALU.mult, ALU.add).then_inc(conv_done, 1)
                        dve.wait_ge(gate_act, i * 2 + (GATES_FFN[f] + b + 1))
                        dve.wait_ge(conv_done, i * 4 + (2 * b + 2))
                        dve.tensor_tensor(tmp[:, 1, :], tmp[:, 0, :], tmp[:, 1, :], ALU.mult).then_inc(prod_ready, 1)
                        dve.wait_ge(prod_hi, i * 2 + (f * KF + b + 1))
                        dve.tensor_tensor(hid_lo[:, i * 2 + b, :], tmp[:, 1, :], hid_hi[:, i * 2 + b, :].bitcast(F32),
                                          ALU.subtract).then_inc(hid_ready, 1)

            def table(i):
                inv, quarter = TABLES[i][:2]
                angle, turns = gate_t[:, 1, :], rstd[:, :]
                if i == 0:
                    dve.wait_ge(pos_loaded, 16)
                    dve.wait_ge(consts_loaded, 16)
                else:
                    dve.wait_ge(table_ready, i)
                link(dve.tensor_scalar(angle, gate_t[:, 0, :].bitcast(I32), consts[:, inv:inv + 1], None, ALU.mult))
                link(dve.tensor_scalar(turns.bitcast(I32), angle, 1.0 / TWO_PI, quarter, ALU.mult, ALU.add))
                link(dve.tensor_copy(turns, turns.bitcast(I32)))
                for part in (PI_A, PI_B, PI_C):
                    link(dve.scalar_tensor_tensor(angle, turns, -part, angle, ALU.mult, ALU.add))
                link(dve.tensor_scalar(angle, angle, quarter * TWO_PI, PI_MAX, ALU.add, ALU.min))
                dve.tensor_scalar(angle, angle, -PI_MAX, None, ALU.max).then_inc(angle_ready, 1)

            def ffn_down(name, k, gain, half):
                t0 = plan.first[name][1]
                for m in range(KD):
                    dve.wait_ge(tile_done, t0 + m + 1)
                    dve.scalar_tensor_tensor(h[:, m, :], acc[:, (t0 + m) % BANKS, :], half, h[:, m, :],
                                             ALU.mult, ALU.add).then_inc(tile_freed, 1)
                    norm_chunk(k, m, gain(m))
                    if name == "down1" and m < len(TABLES):
                        table(m)

            def lo_part(step, half, dst, src, hi):
                dve.wait_ge(split_hi, nth(split_steps, (step, half)) + 1)
                dve.tensor_tensor(dst, src, hi.bitcast(F32), ALU.subtract).then_inc(split_ready, 1)

            dve.wait_ge(vec_loaded, 16)
            for c in range(KD):
                u_lo_chunk(0, c, col("ffn1_norm", c))
            for c in range(KD):
                norm_chunk(0, c, None)
            rstd_of_norm(1, 1)
            ffn_up(0, "up1")
            ffn_down("down1", 1, lambda m: col("mix_norm", m), 0.5)
            rstd_of_norm(2, 2)
            link(inverse_root(rstd_tok[:, :], aux[:, 1, 0:NT], 1.0 / D, NORM_EPS, small[:, 8:8 + NT], small[:, 0:NT]))

            dve.wait_ge(table_ready, 4)
            dve.tensor_copy(cos_r[:, :], up_t[:, 0, :])
            link(dve.tensor_copy(sin_r[:, :], up_t[:, 1, :]))

            for step in MIX:
                kind = step[0]
                n, t = plan.first[step]
                bank = acc[:, t % BANKS, :]
                if kind in PROJECTS:
                    dve.wait_ge(tile_done, t + 1)
                if kind == "avw":
                    dve.tensor_tensor(y_sq[0:AVW, 0, :], bank[0:AVW, :], rstd[0:AVW, :], ALU.mult).then_inc(tile_freed, 1)
                elif kind == "avt":
                    dve.wait_ge(avt_done, 1)
                    link(dve.tensor_copy(avt[:, :, :], aux[:, 3, 0:NT * AVW].rearrange("p (a b) -> p a b", a=NT)))
                    dve.tensor_scalar(avt[:, :, A_DIM:AVW], avt[:, :, A_DIM:AVW], A_HEADS ** -0.5, None, ALU.mult).then_inc(avt_ready, 1)
                    dve.wait_ge(avt_ready, 1)
                elif kind == "rv":
                    v = rv[:, step[1] % 2, :, :]
                    for i in range(2):
                        dve.wait_ge(tile_done, t + i + 1)
                        part = v[:, 2 * i:2 * i + 2, :]
                        dve.tensor_tensor(part, acc[:, (t + i) % BANKS, :].rearrange("p (a b) -> p a b", a=2),
                                          rstd_tok[:, 2 * i:2 * i + 2].unsqueeze(2).to_broadcast([P, 2, R_V]), ALU.mult).then_inc(tile_freed, 1)
                        dve.wait_ge(tile_freed, t + i + 1)
                        mean = v_mean[:, 4 * (step[1] % 2) + 2 * i:4 * (step[1] % 2) + 2 * i + 2]
                        link(dve.reduce_sum(mean, part, AX_X))
                        dve.tensor_scalar(mean, mean, -1.0 / R_V, None, ALU.mult).then_inc(mean_ready, 1)
                elif kind in ("rg", "ga", "gb"):
                    buf = {"rg": lambda: srg[:, step[1] % 2, step[2], :], "ga": lambda: up_t[:, 0, :], "gb": lambda: up_t[:, 1, :]}[kind]()
                    if step in (("gb", 0), ("ga", 0)):
                        dve.wait_ge(rope_ready, len(rope_steps) - (kind == "gb"))
                    dve.tensor_tensor(buf, bank, rstd[:, :], ALU.mult).then_inc(tile_freed, 1)
                elif kind in ROPE:
                    z = nth(rope_steps, step)
                    if z >= 2:
                        dve.wait_ge(rope_ready, z - 1)
                    dve.tensor_tensor(gate_t[:, z % 2, :], bank, rstd[:, :], ALU.mult).then_inc(tile_freed, 1)
                elif kind == "index":
                    b = step[1]
                    nk = (b + 1) * P
                    score = bias[:, bias_at[b]:bias_at[b] + nk]
                    for hd in range(2 * step[2], 2 * step[2] + 2):
                        j = index_units[b] + hd
                        w = avt[:, b, A_DIM + hd:A_DIM + hd + 1]
                        dve.wait_ge(idx_relu, j + 1)
                        if hd == 0:
                            dve.tensor_scalar(score, sq[:, j % 2, 0:nk], w, None, ALU.mult).then_inc(idx_added, 1)
                        else:
                            dve.wait_ge(idx_added, j)
                            dve.scalar_tensor_tensor(score, sq[:, j % 2, 0:nk], w, score, ALU.mult, ALU.add).then_inc(idx_added, 1)
                elif kind == "topk":
                    b = step[1]
                    nk = (b + 1) * P
                    score = bias[:, bias_at[b]:bias_at[b] + nk]
                    if step[2] == 0:
                        dve.wait_ge(idx_added, index_units[b] + A_HEADS)
                        link(dve.memset(score[0:CHUNK, nk - CHUNK:nk], NEG_BIG))
                    for _ in range(TOPK // 8 // TOPK_STEPS):
                        link(dve.max(top8, score))
                        link(dve.match_replace(score, top8, score, TAKEN))
                    if step[2] == TOPK_STEPS - 1:
                        link(dve.tensor_scalar(score, score, TAKEN, NEG_BIG, ALU.not_equal, ALU.mult))
                elif kind == "rscore":
                    r = step[1]
                    dve.wait_ge(dec_loaded, 16 * (r + 1))
                    for jt in range(NT):
                        nq = S - jt * P
                        dve.wait_ge(rs_done, NT * r + jt + 1)
                        dve.tensor_tensor(wts[:, wts_at[jt]:wts_at[jt] + nq], aux[:, 2 + jt % 2, 0:nq], dec[:, 0:nq], ALU.mult).then_inc(rw_ready, 1)
                elif kind == "rsq":
                    dve.wait_ge(ry_sq, 2 * step[1] + 2)
                    dve.tensor_tensor(ssum[:, :], y_sq[:, 0, :], y_sq[:, 1, :], ALU.add).then_inc(ry_sum, 1)
                elif kind == "rsum":
                    dve.wait_ge(stat_done, 3 + step[1])
                    dve.tensor_scalar(y_sq[:, 0, :], aux[:, 2, :], 1.0 / R_V, GN_EPS, ALU.mult, ALU.add).then_inc(var_ready, 1)
                elif kind == "rfin":
                    r = step[1]
                    dve.wait_ge(root_ready, 3 + r)
                    link(newton(ssum[:, :], y_sq[:, 0, :], y_sq[:, 1, :]))
                    for half in range(2):
                        dve.tensor_tensor(y_sq[:, half, :], aux[:, half, :], ssum[:, :], ALU.mult).then_inc(ry_freed, 1)
                    for half in range(2):
                        dve.wait_ge(ry_freed, 2 * r + half + 1)
                        dve.wait_ge(gate_act, gates_before(("rg", r, half)) + 1)
                        dve.scalar_tensor_tensor(y_sq[:, half, :], y_sq[:, half, :], col("ret_gn", 2 * r + half), srg[:, r % 2, half, :],
                                                 ALU.mult, ALU.mult).then_inc(split_in, 1)
                elif kind == "logits":
                    b, i = step[1], nth(logit_steps, step)
                    nk = (b + 1) * P
                    if b == 0:
                        link(dve.memset(bias[:, 0:P], 0.0))
                        link(dve.memset(bias[0:CHUNK, CHUNK:P], NEG_BIG))
                    if i == 0:
                        dve.wait_ge(rope_ready, len(rope_steps))
                    at = 8 * (i % 2)
                    for hd in range(A_HEADS):
                        j = A_HEADS * i + hd
                        dve.wait_ge(lg_done, j + 1)
                        dve.tensor_tensor_reduce(out=probs_of(b, hd), in0=aux[:, 2 + j % 2, 0:nk], in1=bias[:, bias_at[b]:bias_at[b] + nk],
                                                 scale=A_DIM ** -0.5, scalar=TAKEN, op0=ALU.add, op1=ALU.max,
                                                 accum_out=row_max[:, at + hd:at + hd + 1]).then_inc(lg_read, 1)
                    dve.wait_ge(lg_read, A_HEADS * (i + 1))
                    dve.tensor_scalar(neg_max[:, at:at + 8], row_max[:, at:at + 8], -1.0, None, ALU.mult).then_inc(neg_ready, 1)
                elif kind == "probs":
                    b = step[1]
                    i = nth(logit_steps, ("logits", b))
                    at = 8 * (i % 2)
                    dve.wait_ge(exp_done, A_HEADS * (i + 1))
                    link(dve.reciprocal(row_inv[:, at:at + 8], row_sum[:, at:at + 8]))
                    for hd in range(A_HEADS):
                        dve.tensor_scalar(probs_of(b, hd), probs_of(b, hd), row_inv[:, at + hd:at + hd + 1], None, ALU.mult).then_inc(p_ready, 1)
                elif kind == "attend":
                    b = step[1]
                    dve.tensor_copy(tmp[:, 0, :], bank).then_inc(tile_freed, 1)
                    dve.wait_ge(tile_freed, t + 1)
                    lo_part(step, 0, ya_lo[:, :, blk(b)], tmp[:, 0, :].rearrange("p (c q) -> p c q", c=4), ya_hi[:, :, blk(b)])
                elif kind == "wa":
                    if step[1]:
                        dve.wait_ge(split_ready, nth(lo_steps, (("mg", step[1] - 1), 0)) + 1)
                    for i in range(2):
                        dve.wait_ge(tile_done, t + i + 1)
                        dve.tensor_copy(gate_t[:, i, :], acc[:, (t + i) % BANKS, :]).then_inc(tile_freed, 1)
                elif kind == "wb":
                    dve.wait_ge(gate_act, gates_before(("gb", step[1])) + 1)
                    dve.tensor_tensor(branch_b[step[1] % 4], bank, up_t[:, 1, :], ALU.mult).then_inc(tile_freed, 1)
                elif kind == "mg":
                    m = step[1]
                    x = gate_t[:, m % 2, :]
                    dve.wait_ge(gate_act, gates_before(("ga", m)) + 1)
                    dve.wait_ge(tile_freed, max(plan.first[("wb", m)][1] + 1, plan.first[("wa", m - m % 2)][1] + m % 2 + 1))
                    link(dve.tensor_tensor(x, x, up_t[:, 0, :], ALU.mult))
                    dve.tensor_tensor(x, x, branch_b[m % 4], ALU.add).then_inc(split_in, 1)
                    lo_part(step, 0, mg_lo[:, m, :], x, mg_hi[:, m, :])
                elif kind == "wout":
                    m = step[1]
                    dve.tensor_tensor(h[:, m, :], bank, h[:, m, :], ALU.add).then_inc(tile_freed, 1)
                    norm_chunk(2, m, col("ffn2_norm", m))
            rstd_of_norm(7, 3)
            ffn_up(1, "up2")
            ffn_down("down2", 3, lambda m: col("ple_norm", m), 0.5)
            link(dve.tensor_tensor(small[:, 48:48 + KD], cols[:, COL["final_norm"]:COL["final_norm"] + KD],
                                   cols[:, COL["l0_norm1"]:COL["l0_norm1"] + KD], ALU.mult))
            for c in range(2):
                dve.wait_ge(p_split, c + 1)
                dve.tensor_tensor(p_lo[:, c, :], p_raw[:, c, :], p_hi[:, c, :].bitcast(F32), ALU.subtract).then_inc(hid_ready, 1)
            rstd_of_norm(8, 4)

            def ple_add(m):
                dve.wait_ge(gate_act, gates_before(("pgate", m)) + 1)
                link(dve.tensor_tensor(gate_t[:, m % 2, :], gate_t[:, m % 2, :], proj[:, m, :], ALU.mult))
                dve.tensor_tensor(h[:, m, :], h[:, m, :], gate_t[:, m % 2, :], ALU.add).then_inc(h_updated, 1)

            def gla_lo(c):
                dve.wait_ge(u_hi_ready, KD * 4 + c + 1)
                dve.scalar_tensor_tensor(u_lo[:, c, :], h[:, c, :], small[:, 48 + c:49 + c], u_hi[:, c, :].bitcast(F32),
                                         ALU.mult, ALU.subtract).then_inc(u_ready, 1)

            def ple_squares(m):
                for e, total in ((0, ssum), (1, ssum2)):
                    dve.wait_ge(sq_ready, SQ[4] + 2 * m + e + 1)
                    add_squares(total, SQ[4] + 2 * m + e, m == 0)

            for step in PLE_STEPS:
                n, t = plan.first[step]
                dve.wait_ge(tile_done, t + 1)
                if step[0] == "pgate":
                    m = step[1]
                    dve.tensor_tensor(gate_t[:, m % 2, :], acc[:, t % BANKS, :], rstd[:, :], ALU.mult).then_inc(tile_freed, 1)
                    if m == KD - 1:
                        for c in range(3):
                            gla_lo(c)
                    if m >= 2:
                        ple_add(m)
                    if 2 <= m < KD - 1:
                        ple_squares(m)
                else:
                    for i in range(4):
                        dve.wait_ge(tile_done, t + i + 1)
                        dve.tensor_copy(proj[:, 4 * step[1] + i, :], acc[:, (t + i) % BANKS, :]).then_inc(tile_freed, 1)
                    if step[1] == 1:
                        dve.wait_ge(tile_freed, t + 4)
                        ple_add(0)
                        ple_add(1)
                        ple_squares(0)
                        ple_squares(1)
            for c in range(3, KD):
                gla_lo(c)

            ple_squares(KD - 1)

            dve.wait_ge(stat_done, 9)
            a_tok, x_tok = small[:, 160:160 + NT], small[:, 12:12 + NT]
            dve.tensor_scalar(a_tok, aux[:, 2, 0:NT], 1.0 / D, NORM_EPS, ALU.mult, ALU.add)
            link(dve.tensor_scalar(gres, aux[:, 0, :], 1.0 / D, NORM_EPS, ALU.mult, ALU.add))
            dve.tensor_scalar(a_tok, a_tok, NORM_EPS, None, ALU.mult)
            link(dve.tensor_scalar(sq[:, 0, :], gres, NORM_EPS, None, ALU.mult))
            link(dve.scalar_tensor_tensor(x_tok, aux[:, 2, NT:2 * NT], 1.0 / D, a_tok, ALU.mult, ALU.add))
            dve.scalar_tensor_tensor(sq[:, 0, :], aux[:, 1, :], 1.0 / D, sq[:, 0, :], ALU.mult, ALU.add).then_inc(ms2_ready, 1)
            dve.wait_ge(root_ready, 9)
            newton(rstd[:, :], sq[:, 0, :], sq[:, 1, :]).then_inc(rstd_ready, 1)
            link(newton(rstd_tok[:, :], x_tok, small[:, 4:4 + NT]))
            keep = ssum
            link(dve.memset(keep[:, :], 1.0))
            link(dve.memset(keep[:, 0:S:CHUNK], 0.0))
            dve.wait_ge(rstd_ready, 5)

            for step in GLA:
                kind = step[0]
                n, t = plan.first[step]
                bank = acc[:, t % BANKS, :]
                if kind in PROJECTS:
                    dve.wait_ge(tile_done, t + 1)
                if kind == "alow":
                    dve.tensor_tensor(alow_t[0:G_RANK, :], bank[0:G_RANK, :], rstd[0:G_RANK, :], ALU.mult).then_inc(tile_freed, 1)
                elif kind == "alpha":
                    for c in range(G_HEADS):
                        dve.wait_ge(tile_done, t + c + 1)
                        dve.tensor_scalar(gcum[:, c, :], acc[:, (t + c) % BANKS, :], col("b_alpha", c), None, ALU.add).then_inc(tile_freed, 1)
                    dve.memset(gsc[:, :, :], 0.0)
                elif kind == "cum":
                    for c in range(G_HEADS):
                        dve.wait_ge(al_ln, 2 * G_HEADS + c + 1)
                        link(dve.scalar_tensor_tensor(tmp[:, c, :], gcum[:, c, :], 0.0, tmp[:, c, :], ALU.min, ALU.subtract))
                        dve.tensor_tensor_scan(gcum[:, c, :], keep[:, :], tmp[:, c, :], 0.0, ALU.mult, ALU.add).then_inc(al_ready, 1)
                elif kind == "res":
                    if step[1] == 0:
                        dve.wait_ge(root_ready, 10)
                        link(newton(gres, gres, ssum2))
                    for c in (2 * step[1], 2 * step[1] + 1):
                        dve.scalar_tensor_tensor(h[:, c, :], h[:, c, :], col("final_norm", c), gres, ALU.mult, ALU.mult)
                elif kind in ("gk", "gq"):
                    dve.tensor_tensor(gkq[:, 1 if kind == "gq" else 0, :], bank, rstd[:, :], ALU.mult).then_inc(tile_freed, 1)
                elif kind == "gv":
                    for i in range(2):
                        dve.wait_ge(tile_done, t + i + 1)
                        dve.tensor_tensor(gvt[:, step[1] % 2, 2 * i:2 * i + 2, :], acc[:, (t + i) % BANKS, :].rearrange("p (a b) -> p a b", a=2),
                                          rstd_tok[:, 2 * i:2 * i + 2].unsqueeze(2).to_broadcast([P, 2, G_DV]), ALU.mult).then_inc(tile_freed, 1)
                elif kind == "gpre":
                    r = step[1]
                    cum = gcum[:, r, :].rearrange("p (n c) -> p n c", c=CHUNK)
                    dve.wait_ge(al_ready, G_HEADS)
                    dve.tensor_tensor(up_t[:, 0, :].rearrange("p (n c) -> p n c", c=CHUNK), cum[:, :, CHUNK - 1:CHUNK].to_broadcast([P, S // CHUNK, CHUNK]),
                                      cum, ALU.subtract).then_inc(gd_ready, 1)
                    dve.wait_ge(tile_freed, plan.first[("gq", r)][1] + 1)
                    dve.wait_ge(ge_ready, 3 * r + 2)
                    dve.scalar_tensor_tensor(gqd[:, :], gkq[:, 1, :], G_DK ** -0.5, gate_t[:, 0, :], ALU.mult, ALU.mult)
                    dve.tensor_tensor(gki[:, :], gkq[:, 0, :], gate_t[:, 1, :], ALU.mult)
                    dve.wait_ge(ge_ready, 3 * r + 3)
                    dve.tensor_tensor(up_t[:, 1, :], gkq[:, 0, :], up_t[:, 0, :], ALU.mult).then_inc(gqk_ready, 1)
                elif kind == "gsc":
                    r = step[1]
                    dve.wait_ge(gs_done, r + 1)
                    for e in range(2):
                        rows = slice(e * CHUNK, (e + 1) * CHUNK)
                        link(dve.tensor_scalar(gsc[rows, :, rows], aux[rows, 2, 0:NT * CHUNK].rearrange("p (a b) -> p a b", a=NT),
                                               -SCORE_MAX, SCORE_MAX, ALU.max, ALU.min))
                        ins = dve.tensor_tensor(gsc[rows, :, rows], gsc[rows, :, rows], consts[rows, C_MASK:C_MASK + CHUNK].unsqueeze(1).to_broadcast([CHUNK, NT, CHUNK]), ALU.mult)
                    ins.then_inc(gsc_ready, 1)
                elif kind == "gkv":
                    r = step[1]
                    for n in range(7):
                        kv = state_bank(n)
                        dve.wait_ge(gkv_done, 7 * r + (4 if n < 4 else 7))
                        if n == 0:
                            dve.tensor_copy(gst[:, 0, :], kv).then_inc(gst_ready, 1)
                        else:
                            end = n * CHUNK + CHUNK - 1
                            dve.wait_ge(gst_ready, 7 * r + n)
                            dve.scalar_tensor_tensor(gst[:, n, :], gst[:, n - 1, :], gate_t[:, 0, end:end + 1], kv, ALU.mult, ALU.add).then_inc(gst_ready, 1)
                elif kind == "gout":
                    r = step[1]
                    for i in range(2):
                        dve.wait_ge(tile_done, t + i + 1)
                        dve.tensor_copy(go[:, r, 2 * i:2 * i + 2, :], acc[:, (t + i) % BANKS, :].rearrange("p (a b) -> p a b", a=2)).then_inc(tile_freed, 1)
                elif kind == "gn":
                    r = step[1]
                    four = slice(NT * r, NT * (r + 1))
                    dve.wait_ge(root_ready, 11 + r)
                    link(inverse_root(head_rstd[:, four], head_sq[:, four], 1.0 / G_DV, NORM_EPS, head_x[:, four], head_root[:, four]))
                    for tt in range(NT):
                        ins = dve.tensor_scalar(go[:, r, tt, :], go[:, r, tt, :], head_rstd[:, NT * r + tt:NT * r + tt + 1], None, ALU.mult)
                    ins.then_inc(gon_ready, 1)
                elif kind == "gr":
                    if step[1] == 0:
                        dve.wait_ge(gqk_ready, G_HEADS)
                    dve.tensor_tensor(gkq[:, step[1] % 2, :], bank, rstd[:, :], ALU.mult).then_inc(tile_freed, 1)
                elif kind == "gt":
                    c = step[1]
                    dve.wait_ge(gt_done, c + 1)
                    dve.wait_ge(gate_act, gates_before(("gr", c)) + 1)
                    dve.scalar_tensor_tensor(up_t[:, c % 2, :], aux[:, 2 + c % 2, :], col("gla_out_norm", c), gkq[:, c % 2, :],
                                             ALU.mult, ALU.mult).then_inc(split_in, 1)
                    lo_part(step, 0, gy_lo[:, c, :], up_t[:, c % 2, :], gy_hi[:, c, :])
                elif kind == "gwout":
                    m = step[1]
                    dve.tensor_tensor(h[:, m, :], bank, h[:, m, :], ALU.add).then_inc(tile_freed, 1)
                    norm_chunk(5, m, col("l0_norm2", m))
            rstd_of_norm(15, 6)
            conv_up(2, "up3")
            ffn_down("down3", 6, lambda m: None, 1.0)
            rstd_of_norm(16, 7)
            for c in range(KD):
                dve.scalar_tensor_tensor(h[:, c, :], h[:, c, :], col("final_norm_2", c), rstd[:, :], ALU.mult, ALU.mult).then_inc(out_ready, 1)

        @block.tensor
        def _(pe):
            free_when = {}

            def claim(bank):
                if bank in free_when:
                    pe.wait_ge(*free_when[bank])

            def slabs_ready(n):
                pe.wait_ge(lo_ready, n + 1)

            def free_bank(t):
                if t >= BANKS:
                    pe.wait_ge(tile_freed, t - BANKS + 1)
                return acc[:, t % BANKS, :]

            def mm3(o, w, x_hi, x_lo, first, last):
                slot, columns = w
                pe.matmul(o, w_lo[:, slot, columns], x_hi, start=first, stop=False)
                pe.matmul(o, w_hi[:, slot, columns], x_lo, start=False, stop=False)
                return pe.matmul(o, w_hi[:, slot, columns], x_hi, start=False, stop=last)

            def sums(k):
                pe.wait_ge(sq_added, SQ[k + 1])
                claim(0)
                last = pe.matmul(aux[:, 0, :], ones[:, :], ssum[:, :], start=True, stop=True)
                if k == 4:
                    claim(1)
                    pe.matmul(aux[:, 1, :], ones[:, :], ssum2, start=True, stop=True)
                if k in (1, 4):
                    claim(1 if k == 1 else 2)
                    for i, total in enumerate((ssum, ssum2) if k == 4 else (ssum,)):
                        for tt in range(NT):
                            last = pe.matmul(aux[:, 1 if k == 1 else 2, i * NT + tt:i * NT + tt + 1], total[:, blk(tt)], ones[:, 0:1], start=True, stop=True)
                last.then_inc(stat_done, 1)
                for bank in range(3):
                    free_when[bank] = (rstd_ready, k + 1)

            def fm_tile(t, blocks, x_hi, x_lo, ready=None):
                o = free_bank(t)
                seen = None
                for k, (n, b) in enumerate(blocks):
                    if n != seen:
                        slabs_ready(n)
                        seen = n
                    if ready is not None:
                        pe.wait_ge(*ready(k))
                    last = mm3(o, (n % RING, blk(b)), x_hi[:, k, :], x_lo[:, k, :], k == 0, k == len(blocks) - 1)
                last.then_inc(tile_done, 1)

            def token_tiles(t, n, width, per_tile, per_slab):
                for i in range(NT // per_tile):
                    free_bank(t + i)
                    for tt in range(i * per_tile, (i + 1) * per_tile):
                        o = acc[:, (t + i) % BANKS, (tt % per_tile) * width:(tt % per_tile + 1) * width]
                        for k in range(KD):
                            slot = (n + k // per_slab) % RING
                            columns = slice((k % per_slab) * width, (k % per_slab + 1) * width)
                            slabs_ready(n + k // per_slab)
                            pe.matmul(o, u_lo[:, k, blk(tt)], w_hi[:, slot, columns], start=k == 0, stop=False)
                            pe.matmul(o, u_hi[:, k, blk(tt)], w_lo[:, slot, columns], start=False, stop=False)
                            last = pe.matmul(o, u_hi[:, k, blk(tt)], w_hi[:, slot, columns], start=False, stop=k == KD - 1)
                    last.then_inc(tile_done, 1)

            def ffn_up(k, name):
                n0, t0 = plan.first[name]
                for j in range(RING):
                    fm_tile(t0 + j, [(n0 + j, b) for b in range(KD)], u_hi, u_lo, (lambda c: (u_ready, KD * k + c + 1)) if j == 0 else None)
                    if j == (1 if k == 0 else 0):
                        sums(k)
                with pe.Fori(1, 2 * KF // RING) as i:
                    for j in range(RING):
                        pe.wait_ge(lo_ready, i * RING + (n0 + j + 1))
                        pe.wait_ge(tile_freed, i * RING + (t0 + j - BANKS + 1))
                        for b in range(KD):
                            last = mm3(acc[:, (t0 + j) % BANKS, :], ((n0 + j) % RING, blk(b)), u_hi[:, b, :], u_lo[:, b, :], b == 0, b == KD - 1)
                        last.then_inc(tile_done, 1)

            def ffn_down(f, name):
                n0, t0 = plan.first[name]
                with pe.Fori(0, 2) as i:
                    for m in range(4):
                        o = acc[:, (t0 + m) % BANKS, :]
                        pe.wait_ge(tile_freed, i * 4 + (t0 + m - BANKS + 1))
                        for k in range(KF):
                            j = DOWN_SLABS * m + k // 8
                            if k % 8 == 0:
                                pe.wait_ge(lo_ready, i * (4 * DOWN_SLABS) + (n0 + j + 1))
                            if k == 0 or k >= KF - 4:
                                pe.wait_ge(hid_ready, HIDDEN[f] - KF + max(k + 1, KF - 4))
                            last = mm3(o, ((n0 + j) % RING, blk(k % 8)), hid_hi[:, k, :], hid_lo[:, k, :], k == 0, k == KF - 1)
                            if k % 8 == 7:
                                last.then_inc(slab_used, 1)
                        last.then_inc(tile_done, 1)

            HIDDEN = [KF, 2 * KF, 3 * KF + 2]
            pe.wait_ge(consts_set, 3)
            ffn_up(0, "up1")
            ffn_down(0, "down1")

            for step in MIX:
                kind = step[0]
                n, t = plan.first[step]
                if step == MIX[0]:
                    fm_tile(t, [(n, b) for b in range(KD)], u_hi, u_lo, lambda c: (u_ready, KD + c + 1))
                    sums(1)
                elif kind == "avw":
                    o = free_bank(t)
                    slabs_ready(n)
                    for k in range(KD):
                        last = mm3(o[0:AVW, :], (n % RING, slice(k * AVW, (k + 1) * AVW)), u_hi[:, k, :], u_lo[:, k, :], k == 0, k == KD - 1)
                    last.then_inc(tile_done, 1)
                elif kind == "avt":
                    pe.wait_ge(tile_freed, plan.first[("avw",)][1] + 1)
                    pe.wait_ge(consts_loaded, 16)
                    claim(3)
                    for tt in range(NT):
                        last = pe.transpose(aux[:, 3, tt * AVW:(tt + 1) * AVW], y_sq[0:AVW, 0, blk(tt)], ident[0:AVW, 0:AVW])
                    last.then_inc(avt_done, 1)
                    free_when[3] = (avt_ready, 1)
                elif kind == "rv":
                    token_tiles(t, n, R_V, 2, 4)
                elif kind in ("rg", "kk", "iq", "rq", "rk", "aq", "ga", "gb"):
                    fm_tile(t, [(n, b) for b in range(KD)], u_hi, u_lo)
                elif kind == "index":
                    b = step[1]
                    nk = (b + 1) * P
                    pe.wait_ge(rope_ready, nth(rope_steps, ("iq", 3)) + 1)
                    pe.wait_ge(keys_copied, 64)
                    for hd in range(2 * step[2], 2 * step[2] + 2):
                        j = index_units[b] + hd
                        rows = slice(64 * (hd % 2), 64 * (hd % 2) + 64)
                        claim(2 + j % 2)
                        pe.matmul(aux[:, 2 + j % 2, 0:nk], q8[rows, hd // 2, blk(b)], ikd[rows, 0:nk], start=True, stop=True).then_inc(idx_scored, 1)
                        free_when[2 + j % 2] = (idx_relu, j + 1)
                elif kind == "rscore":
                    r = step[1]
                    pe.wait_ge(rope_ready, nth(rope_steps, ("rk", r)) + 1)
                    for jt in range(NT):
                        nq = S - jt * P
                        claim(2 + jt % 2)
                        pe.matmul(aux[:, 2 + jt % 2, 0:nq], rqk[:, 1, blk(jt)], rqk[:, 0, jt * P:S], start=True, stop=True).then_inc(rs_done, 1)
                        free_when[2 + jt % 2] = (rw_ready, NT * r + jt + 1)
                elif kind == "ry":
                    r = step[1]
                    pe.wait_ge(rv_ready, 2 * r + 2)
                    claim(0)
                    claim(1)
                    for jt in range(NT):
                        pe.wait_ge(rw_ready, NT * r + jt + 1)
                        nq = S - jt * P
                        for half in range(2):
                            last = pe.matmul(aux[:, half, jt * P:S], rv[:, r % 2, jt, blk(half)], wts[:, wts_at[jt]:wts_at[jt] + nq],
                                             start=jt == 0, stop=jt == NT - 1)
                    last.then_inc(ry_done, 1)
                    free_when[0] = (ry_freed, 2 * r + 1)
                    free_when[1] = (ry_freed, 2 * r + 2)
                elif kind == "rsum":
                    r = step[1]
                    pe.wait_ge(ry_sum, r + 1)
                    claim(2)
                    pe.matmul(aux[:, 2, :], ones[:, :], ssum[:, :], start=True, stop=True).then_inc(stat_done, 1)
                    free_when[2] = (var_ready, r + 1)
                elif kind == "logits":
                    b, i = step[1], nth(logit_steps, step)
                    nk = (b + 1) * P
                    pe.wait_ge(rope_ready, len(rope_steps))
                    for hd in range(A_HEADS):
                        j = A_HEADS * i + hd
                        rows = slice(64 * (hd % 2), 64 * (hd % 2) + 64)
                        claim(2 + j % 2)
                        pe.matmul(aux[:, 2 + j % 2, 0:nk], q8[rows, hd // 2, blk(b)], akd[rows, 0:nk], start=True, stop=True).then_inc(lg_done, 1)
                        free_when[2 + j % 2] = (lg_read, j + 1)
                elif kind == "attend":
                    b = step[1]
                    base = pt_base[step]
                    groups = [(parity, kt) for parity in range(2) for kt in range(b + 1)]

                    def turn(g):
                        parity, kt = groups[g]
                        claim((base + g) % 2)
                        if parity == 0 and kt == 0:
                            pe.wait_ge(p_ready, A_HEADS * (nth(attend_steps, step) + 1))
                        for i in range(4):
                            last = pe.transpose(aux[:, (base + g) % 2, blk(i)], probs_of(b, 2 * i + parity)[:, blk(kt)], ident)
                        last.then_inc(pt_done, 1)
                        free_when[(base + g) % 2] = (pt_ready, base + g + 1)

                    o = free_bank(t)
                    turn(0)
                    for g, (parity, kt) in enumerate(groups):
                        if g + 1 < len(groups):
                            turn(g + 1)
                        pe.wait_ge(pt_ready, base + g + 1)
                        last = pe.matmul(o[64 * parity:64 * parity + 64, :], avt[:, kt, 0:A_DIM], pt[:, (base + g) % 2, :],
                                         start=kt == 0, stop=kt == b)
                    last.then_inc(tile_done, 1)
                elif kind == "wa":
                    pe.wait_ge(split_ready, nth(lo_steps, (("attend", 1), 0)) + 1)
                    for i in range(2):
                        fm_tile(t + i, [(n, 4 * i + b) for b in range(4)], ya_hi, ya_lo)
                elif kind == "wb":
                    pe.wait_ge(yr_ready, KD)
                    fm_tile(t, [(n, b) for b in range(KD)], yr_hi, yr_lo)
                elif kind == "wout":
                    fm_tile(t, [(n, b) for b in range(KD)], mg_hi, mg_lo,
                            (lambda c: (split_ready, nth(lo_steps, (("mg", c), 0)) + 1)) if step[1] == 0 else None)
            ffn_up(2, "up2")
            ffn_down(1, "down2")

            for step in PLE_STEPS:
                n, t = plan.first[step]
                if step[0] == "pgate":
                    fm_tile(t, [(n, b) for b in range(KD)], u_hi, u_lo, (lambda c: (u_ready, KD * 3 + c + 1)) if step[1] == 0 else None)
                    if step[1] == 0:
                        sums(3)
                else:
                    pe.wait_ge(hid_ready, 2 * KF + 2)
                    for i in range(4):
                        fm_tile(t + i, [(n, 2 * i), (n, 2 * i + 1)], p_hi, p_lo)

            for step in GLA:
                kind = step[0]
                n, t = plan.first[step]
                if kind == "alow":
                    o = free_bank(t)
                    slabs_ready(n)
                    for k in range(KD):
                        pe.wait_ge(u_ready, KD * 4 + k + 1)
                        last = mm3(o[0:G_RANK, :], (n % RING, slice(k * G_RANK, (k + 1) * G_RANK)), u_hi[:, k, :], u_lo[:, k, :], k == 0, k == KD - 1)
                    last.then_inc(tile_done, 1)
                    sums(4)
                elif kind == "alpha":
                    pe.wait_ge(tile_freed, plan.first[("alow",)][1] + 1)
                    pe.wait_ge(ple_loaded, 32)
                    for c in range(G_HEADS):
                        free_bank(t + c)
                        pe.matmul(acc[:, (t + c) % BANKS, :], walpha[0:G_RANK, blk(c)], alow_t[0:G_RANK, :], start=True, stop=True).then_inc(tile_done, 1)
                elif kind == "gv":
                    token_tiles(t, n, G_DV, 2, 4)
                elif kind in ("gk", "gq", "gr"):
                    fm_tile(t, [(n, b) for b in range(KD)], u_hi, u_lo)
                elif kind == "gsc":
                    r = step[1]
                    pe.wait_ge(gqk_ready, r + 1)
                    claim(3)
                    for tt in range(NT):
                        last = pe.transpose(aux[:, 3, blk(tt)], up_t[:, 1, blk(tt)], ident)
                    last.then_inc(gke_done, 1)
                    free_when[3] = (gke_ready, r + 1)
                    claim(2)
                    for tt in range(NT):
                        for e in range(2):
                            tok = slice(tt * P + e * CHUNK, tt * P + (e + 1) * CHUNK)
                            last = pe.matmul(aux[e * CHUNK:(e + 1) * CHUNK, 2, tt * CHUNK:(tt + 1) * CHUNK], gki[:, tok], gqd[:, tok], start=True, stop=True)
                    last.then_inc(gs_done, 1)
                    free_when[2] = (gsc_ready, r + 1)
                elif kind == "gkv":
                    r = step[1]
                    pe.wait_ge(gke_ready, r + 1)
                    pe.wait_ge(tile_freed, plan.first[("gv", r)][1] + 2)
                    for c in range(7):
                        tt, rows = c // 2, slice((c % 2) * CHUNK, (c % 2 + 1) * CHUNK)
                        bank = c // 4 * 2 + c % 2
                        if c in (0, 1, 4, 5):
                            claim(bank)
                        pe.matmul(state_bank(c), gket[rows, tt, :], gvt[rows, r % 2, tt, :], start=True, stop=True).then_inc(gkv_done, 1)
                        free_when[bank] = (gst_ready, 7 * r + c + 1)
                elif kind == "gout":
                    r = step[1]
                    pe.wait_ge(gsc_ready, r + 1)
                    for tt in range(NT):
                        if tt % 2 == 0:
                            free_bank(t + tt // 2)
                        o = acc[:, (t + tt // 2) % BANKS, (tt % 2) * G_DV:(tt % 2 + 1) * G_DV]
                        last = pe.matmul(o, gsc[:, tt, :], gvt[:, r % 2, tt, :], start=True, stop=True)
                        for e in range(2):
                            c = 2 * tt + e
                            if c:
                                pe.wait_ge(gst_ready, 7 * r + c)
                                last = pe.matmul(o[e * CHUNK:(e + 1) * CHUNK, :], gqd[:, c * CHUNK:(c + 1) * CHUNK], gst[:, c - 1, :],
                                                 start=False, stop=True, skip_group_check=True)
                        if tt % 2:
                            last.then_inc(tile_done, 1)
                elif kind == "gt":
                    c = step[1]
                    pe.wait_ge(gon_ready, c // 2 + 1)
                    claim(2 + c % 2)
                    for tt in range(NT):
                        last = pe.transpose(aux[:, 2 + c % 2, blk(tt)], go[:, c // 2, tt, blk(c % 2)], ident)
                    last.then_inc(gt_done, 1)
                    free_when[2 + c % 2] = (split_in, nth(made_steps, (step, 0)) + 1)
                elif kind == "gwout":
                    fm_tile(t, [(n, b) for b in range(KD)], gy_hi, gy_lo,
                            (lambda c: (split_ready, nth(lo_steps, (("gt", c), 0)) + 1)) if step[1] == 0 else None)
            ffn_up(5, "up3")
            ffn_down(2, "down3")
            sums(6)


def _blocks(w):
    k, m = w.shape
    return w.reshape(k // P, P, m // P, P).transpose(2, 1, 0, 3).reshape(m // P, P, k)


def _moving(w):
    k, m = w.shape
    return w.reshape(k // P, P, m).transpose(1, 0, 2).reshape(P, k // P * m)


def _pairs(a, b):
    return np.stack([_blocks(a), _blocks(b)], 1).reshape(-1, P, a.shape[0])


def _halves(w):
    return _moving(w).reshape(P, 2, SLAB).transpose(1, 0, 2)


def _shape_constants():
    consts = np.zeros((P, NCONST), np.float32)
    p = np.arange(P)
    consts[:, C_ID:C_ID + P] = np.eye(P)
    consts[:, C_MASK:C_MASK + CHUNK] = (p % CHUNK)[:, None] <= np.arange(CHUNK)[None, :]
    inv_a, inv_r = (10000.0 ** (-np.arange(n) / n) for n in (32, 64))
    consts[:, C_INV_A] = inv_a[p % 32]
    consts[:, C_INV_R] = inv_r[p % 64]
    consts[:, C_SGN_A] = np.where(p % 64 < 32, -1.0, 1.0)
    consts[:, C_SGN_R] = np.where(p < 64, -1.0, 1.0)
    log_gamma = np.log1p(-np.exp2(-5.0 - np.arange(R_HEADS)))
    i, j = np.arange(S)[None, :], p[:, None]
    seen = (i >= P) | (j < (i // CHUNK + 1) * CHUNK)
    decay = np.exp(log_gamma[:, None, None] * np.abs(i - j)) * seen * R_QK ** -0.5
    return consts, decay.astype(np.float32)


def kernel(**inputs):
    import concourse.bacc as bacc
    from concourse.bass_utils import run_bass_kernel_spmd as run

    a = {k: np.asarray(v) for k, v in inputs.items()}
    consts, decay = _shape_constants()
    w_in = a["w_in"][0]
    at, z = 0, {}
    for name, n in (("aq", 512), ("ak", 64), ("av", 64), ("iq", 512), ("ik", 64), ("iw", 8), ("rq", 512), ("rk", 512),
                    ("rv", 1024), ("rg", 1024), ("ga", 1024), ("gb", 1024)):
        z[name] = w_in[:, at:at + n]
        at += n
    z["kk"] = np.concatenate([z["ik"], z["ak"]], 1)
    tiles = {k: _blocks(z[k]) for k in ("aq", "iq", "rq", "rk", "rg", "ga", "gb", "kk")}
    tiles["wb"] = _blocks(a["w_branch_b"][0])
    tiles["wout"] = _blocks(a["w_out"][0])
    wa = _blocks(a["w_branch_a"][0])
    mix = []
    for step in MIX:
        kind = step[0]
        if kind == "rv":
            mix += list(_halves(z["rv"][:, step[1] * R_V:(step[1] + 1) * R_V]))
        elif kind == "rg":
            mix.append(tiles["rg"][2 * step[1] + step[2]])
        elif kind == "wa":
            mix.append(np.concatenate([wa[step[1]], wa[step[1] + 1]], 1))
        elif kind in tiles:
            mix.append(tiles[kind][step[1] if len(step) > 1 else 0])
    g_in = a["l0_gla_w_in_2"]
    gq, gk, gv, gr, glow = (g_in[:, i:j] for i, j in ((0, 512), (512, 1024), (1024, 2048), (2048, 3072), (3072, 3088)))
    gt = {"gq": _blocks(gq), "gk": _blocks(gk), "gr": _blocks(gr), "gwout": _blocks(a["l0_gla_w_out_2"])}
    gla = []
    for step in GLA[1:]:
        if step[0] == "gv":
            gla += list(_halves(gv[:, step[1] * G_DV:(step[1] + 1) * G_DV]))
        elif step[0] in gt:
            gla.append(gt[step[0]][step[1]])
    pgate = _blocks(a["w_ple_gate"][0])
    pproj = _blocks(a["w_ple_proj"][0]).transpose(1, 0, 2).reshape(P, 2, SLAB)
    ple = [pproj[:, s[1]] if s[0] == "pproj" else pgate[s[1]] for s in PLE_STEPS]
    up3 = a["l0_ffn_w_up_2"]

    def columns(v):
        return v.reshape(-1, P).T

    conv = a["l0_ffn_conv_w_2"]
    vectors = {"ffn1_norm": a["ffn1_norm"], "mix_norm": a["mix_norm"], "ret_gn": a["ret_gn"], "ffn2_norm": a["ffn2_norm"],
               "ple_norm": a["ple_norm"], "final_norm": a["final_norm"], "l0_norm1": a["l0_norm1_2"],
               "gla_out_norm": a["l0_gla_out_norm_2"], "l0_norm2": a["l0_norm2_2"], "final_norm_2": a["final_norm_2"],
               "b_alpha": a["l0_gla_b_alpha_2"], "conv_w0": conv[0], "conv_w1": conv[1], "conv_w2": conv[2],
               "conv_b": a["l0_ffn_conv_b_2"]}
    arrays = {
        "xT": a["x"][0].T.reshape(KD, P, S),
        "pT": a["p"][0, 0].T.reshape(2, P, S).transpose(1, 0, 2),
        "positions": np.broadcast_to(a["positions"], (P, S)),
        "vectors": np.concatenate([columns(vectors[name]) for name, _ in VECTORS], 1),
        "consts": consts,
        "decay": decay,
        "w_up1": _pairs(a["ffn1_w_gate"][0], a["ffn1_w_up"][0]),
        "w_down1": _blocks(a["ffn1_w_down"][0]),
        "w_avw": _moving(np.concatenate([z["av"], z["iw"]], 1)),
        "w_mix": np.stack(mix),
        "w_up2": _pairs(a["ffn2_w_gate"][0], a["ffn2_w_up"][0]),
        "w_down2": _blocks(a["ffn2_w_down"][0]),
        "w_ple": np.stack(ple),
        "w_alow": _moving(glow),
        "w_alpha": a["l0_gla_w_alpha_up_2"],
        "w_gla": np.stack(gla),
        "w_up3": _pairs(up3[:, :FF], up3[:, FF:]),
        "w_down3": _blocks(a["l0_ffn_w_down_2"]),
    }
    nc = bacc.Bacc("TRN2", target_bir_lowering=False, num_devices=1)
    feeds, A = {}, {}
    for name, v in arrays.items():
        v = np.ascontiguousarray(v)
        feeds[f"in_{name}"] = v
        A[name] = nc.dram_tensor(f"in_{name}", v.shape, mybir.dt.from_np(v.dtype), kind="ExternalInput").ap()
    out = nc.dram_tensor("out_xT", (KD, P, S), F32, kind="ExternalOutput").ap()
    layer_program(nc, A, out)
    r = run(nc, [feeds], core_ids=[0])
    return r.results[0]["out_xT"].reshape(D, S).T.reshape(1, S, D)
```
